# Optimizing a Trainium2 kernel written in Bass

```python
import math
import jax, jax.numpy as jnp
from jax import lax
import numpy as np

D_MODEL = 1024
BATCH = 1
SEQ = 1024
DEPTH = 2

A_HEADS = 4
A_QK_DIM = 64
A_V_DIM = 2 * A_QK_DIM
A_QK_COLS = A_HEADS * 2 * A_QK_DIM
A_WIDTH = A_HEADS * A_V_DIM
ROPE_THETA = 500000.0
ROPE_DIM = A_QK_DIM // 4
Q_BLOCK = 128
NEG_INF = -1e30
C_WIDTH = 512
CONV_WIDTH = 3
R_HEADS = 4
R_QK_DIM = 64
R_V_DIM = 2 * R_QK_DIM
R_QK_COLS = R_HEADS * R_QK_DIM
R_WIDTH = R_HEADS * R_V_DIM
R_CHUNK = 128
RET_THETA = 10000.0
N_BRANCH = 3
BRANCH_WIDTH = 512
EPS = 1e-6

SPLIT_SIZES = (A_QK_COLS, A_QK_COLS, A_WIDTH, A_WIDTH,
               C_WIDTH, C_WIDTH, C_WIDTH, C_WIDTH,
               R_QK_COLS, R_QK_COLS, R_WIDTH, R_WIDTH,
               N_BRANCH * D_MODEL)
IN_COLS = sum(SPLIT_SIZES)


def rms_norm(x, g=None):
    xf = x.astype(jnp.float32)
    y = xf * lax.rsqrt(jnp.mean(xf * xf, axis=-1, keepdims=True) + EPS)
    return y if g is None else y * g.astype(jnp.float32)

def rotate(x, cos, sin):
    x1, x2 = jnp.split(x, 2, axis=-1)
    return jnp.concatenate([x1 * cos - x2 * sin, x2 * cos + x1 * sin], axis=-1)

def diff_attention(q, k, v, lam, subln_g, lam_init):
    b, s = q.shape[0], q.shape[1]
    pos = jnp.arange(s, dtype=jnp.float32)
    inv = ROPE_THETA ** (-jnp.arange(0, ROPE_DIM, 2, dtype=jnp.float32) / ROPE_DIM)
    ang = pos[:, None] * inv[None, :]
    cos = jnp.cos(ang)[:, None, None, :]
    sin = jnp.sin(ang)[:, None, None, :]
    q = jnp.concatenate([rotate(q[..., :ROPE_DIM], cos, sin), q[..., ROPE_DIM:]], axis=-1)
    k = jnp.concatenate([rotate(k[..., :ROPE_DIM], cos, sin), k[..., ROPE_DIM:]], axis=-1)
    q = q * (A_QK_DIM ** -0.5)
    kh = k.transpose(0, 2, 3, 1, 4)
    vh = v.transpose(0, 2, 1, 3)
    nb = s // Q_BLOCK
    qb = q.transpose(0, 2, 3, 1, 4).reshape(b, A_HEADS, 2, nb, Q_BLOCK, A_QK_DIM)
    qb = qb.transpose(3, 0, 1, 2, 4, 5)
    kpos = jnp.arange(s)

    def block(args):
        qi, start = args
        sc = jnp.einsum('bhcqd,bhckd->bhcqk', qi, kh).astype(jnp.float32)
        qpos = start + jnp.arange(Q_BLOCK)
        mask = kpos[None, :] <= qpos[:, None]
        p = jax.nn.softmax(jnp.where(mask, sc, NEG_INF), axis=-1)
        w = p[:, :, 0] - lam * p[:, :, 1]
        return jnp.einsum('bhqk,bhkv->bhqv', w, vh)

    out = lax.map(block, (qb, jnp.arange(nb, dtype=jnp.int32) * Q_BLOCK))
    out = out.transpose(1, 0, 3, 2, 4).reshape(b, s, A_HEADS, A_V_DIM)
    out = rms_norm(out, subln_g) * (1.0 - lam_init)
    return out.reshape(b, s, A_WIDTH)

def short_conv(x_in, gate_b, gate_c, w):
    u = gate_c * x_in
    y = lax.conv_general_dilated(u, w[:, None, :].astype(u.dtype), window_strides=(1,),
                                 padding=[(CONV_WIDTH - 1, 0)],
                                 dimension_numbers=('NWC', 'WIO', 'NWC'),
                                 feature_group_count=C_WIDTH)
    return gate_b * y

def retention(q, k, v):
    b, s = q.shape[0], q.shape[1]
    pos = jnp.arange(s, dtype=jnp.float32)
    inv = 1.0 / (RET_THETA ** jnp.linspace(0.0, 1.0, R_QK_DIM // 2, dtype=jnp.float32))
    ang = pos[:, None] * inv[None, :]
    cos = jnp.cos(ang)[:, None, :]
    sin = jnp.sin(ang)[:, None, :]
    q = rotate(q, cos, sin)
    k = rotate(k, cos, sin) * (R_QK_DIM ** -0.5)
    log_g = jnp.log(1.0 - 2.0 ** (-5.0 - jnp.arange(R_HEADS, dtype=jnp.float32)))
    nc = s // R_CHUNK

    def chunks(t):
        return t.reshape(b, nc, R_CHUNK, R_HEADS, t.shape[-1]).transpose(0, 3, 1, 2, 4)

    qc, kc, vc = chunks(q), chunks(k), chunks(v)
    idx = jnp.arange(R_CHUNK, dtype=jnp.float32)
    diff = idx[:, None] - idx[None, :]
    dmask = jnp.where(diff >= 0,
                      jnp.exp(jnp.where(diff >= 0, diff, 0.0)[None] * log_g[:, None, None]),
                      0.0)
    inner = jnp.einsum('bhncd,bhnmd->bhncm', qc, kc) * dmask[None, :, None]
    inner = jnp.einsum('bhncm,bhnme->bhnce', inner, vc)
    zeta = jnp.exp((R_CHUNK - 1 - idx)[None, :] * log_g[:, None])
    kv = jnp.einsum('bhnmd,bhnme->bhnde', kc * zeta[None, :, None, :, None], vc)
    chunk_decay = jnp.exp(R_CHUNK * log_g)[None, :, None, None]

    def step(state, kv_n):
        return (chunk_decay * state + kv_n).astype(kv_n.dtype), state

    init = jnp.zeros((b, R_HEADS, R_QK_DIM, R_V_DIM), kv.dtype)
    _, prev = lax.scan(step, init, kv.transpose(2, 0, 1, 3, 4))
    prev = prev.transpose(1, 2, 0, 3, 4)
    xi = jnp.exp((idx + 1.0)[None, :] * log_g[:, None])
    cross = jnp.einsum('bhncd,bhnde->bhnce', qc, prev) * xi[None, :, None, :, None]
    out = (inner + cross).transpose(0, 2, 3, 1, 4).reshape(b, s, R_HEADS, R_V_DIM)
    out = rms_norm(out)
    return out.reshape(b, s, R_WIDTH)

def hybrid_layer(x, norm_g, w_in, attn_lambda, attn_subln_g, conv_w, w_branch, w_out, layer):
    b, s, _ = x.shape
    h = rms_norm(x, norm_g)
    proj = h @ w_in
    split_points = [int(p) for p in np.cumsum(SPLIT_SIZES)[:-1]]
    (aq, ak, av, az, cx, cb, cc, cz, rq, rk, rv, rz, gates) = jnp.split(proj, split_points, axis=-1)

    lam_init = 0.8 - 0.6 * math.exp(-0.3 * layer)
    lp = attn_lambda.astype(jnp.float32)
    lam = jnp.exp(jnp.sum(lp[0] * lp[1])) - jnp.exp(jnp.sum(lp[2] * lp[3])) + lam_init
    a = diff_attention(aq.reshape(b, s, A_HEADS, 2, A_QK_DIM),
                       ak.reshape(b, s, A_HEADS, 2, A_QK_DIM),
                       av.reshape(b, s, A_HEADS, A_V_DIM),
                       lam, attn_subln_g, lam_init) * jax.nn.silu(az)
    c = short_conv(cx, cb, cc, conv_w) * jax.nn.silu(cz)
    r = retention(rq.reshape(b, s, R_HEADS, R_QK_DIM),
                  rk.reshape(b, s, R_HEADS, R_QK_DIM),
                  rv.reshape(b, s, R_HEADS, R_V_DIM)) * jax.nn.silu(rz)

    g = jax.nn.sigmoid(gates.astype(jnp.float32)).reshape(b, s, N_BRANCH, D_MODEL)
    branches = (a, c, r)
    merged = g[:, :, 0] * (branches[0] @ w_branch[0])
    for i in range(1, N_BRANCH):
        merged = merged + g[:, :, i] * (branches[i] @ w_branch[i])
    return x + (merged @ w_out).astype(x.dtype)

def first_inputs(seed: int = 0) -> dict:
    key = jax.random.key(seed)
    ks = jax.random.split(key, 10)
    f32 = jnp.float32
    x = jax.random.normal(ks[0], (BATCH, SEQ, D_MODEL), f32)
    norm_g = 1.0 + 0.01 * jax.random.normal(ks[1], (DEPTH, D_MODEL), f32)
    w_in = jax.random.normal(ks[2], (DEPTH, D_MODEL, IN_COLS), f32) * D_MODEL ** -0.5
    attn_lambda = 0.1 * jax.random.normal(ks[3], (DEPTH, 4, A_QK_DIM), f32)
    attn_subln_g = 1.0 + 0.01 * jax.random.normal(ks[4], (DEPTH, A_V_DIM), f32)
    conv_w = jax.random.normal(ks[5], (DEPTH, CONV_WIDTH, C_WIDTH), f32) * CONV_WIDTH ** -0.5
    w_branch = jax.random.normal(ks[6], (DEPTH, N_BRANCH, BRANCH_WIDTH, D_MODEL), f32) * BRANCH_WIDTH ** -0.5
    w_out = jax.random.normal(ks[7], (DEPTH, D_MODEL, D_MODEL), f32) * D_MODEL ** -0.5
    final_norm_g = 1.0 + 0.01 * jax.random.normal(ks[8], (D_MODEL,), f32)
    return {"x": x, "norm_g": norm_g, "w_in": w_in, "attn_lambda": attn_lambda,
            "attn_subln_g": attn_subln_g, "conv_w": conv_w, "w_branch": w_branch,
            "w_out": w_out, "final_norm_g": final_norm_g}

def first_block(x, norm_g, w_in, attn_lambda, attn_subln_g, conv_w, w_branch, w_out, final_norm_g):
    for layer in range(DEPTH):
        x = hybrid_layer(x, norm_g[layer], w_in[layer], attn_lambda[layer], attn_subln_g[layer],
                         conv_w[layer], w_branch[layer], w_out[layer], layer)
    return rms_norm(x, final_norm_g).astype(x.dtype)


D_MIX = D_MODEL
CONV_WIDTH_2 = D_MIX // 4
CONV_GROUPS = 4
CONV_K = 31
MLA_HEADS = 8
MLA_NOPE = 64
MLA_ROPE = 32
MLA_QK = MLA_NOPE + MLA_ROPE
MLA_V = 64
MLA_WIDTH = MLA_HEADS * MLA_V
Q_LORA = 768
KV_LORA = 256
ROPE_THETA_2 = 10000.0
SG_WIDTH = D_MIX - CONV_WIDTH_2 - MLA_WIDTH
SG_HEADS = 4
SG_HEAD_DIM = SG_WIDTH // SG_HEADS
SG_CHUNK = 128
IN_SIZES = (CONV_WIDTH_2, CONV_WIDTH_2, CONV_WIDTH_2,
            Q_LORA, KV_LORA, MLA_ROPE, MLA_WIDTH,
            SG_WIDTH, SG_WIDTH, SG_WIDTH)
IN_COLS_2 = 3 * CONV_WIDTH_2 + Q_LORA + KV_LORA + MLA_ROPE + MLA_WIDTH + 3 * SG_WIDTH


def _rms_norm(x, g):
    xf = x.astype(jnp.float32)
    y = xf * lax.rsqrt(jnp.mean(xf * xf, axis=-1, keepdims=True) + EPS)
    return (y * g.astype(jnp.float32)).astype(x.dtype)

def _layer_norm(x, g, b):
    xf = x.astype(jnp.float32)
    mu = jnp.mean(xf, axis=-1, keepdims=True)
    var = jnp.mean(jnp.square(xf - mu), axis=-1, keepdims=True)
    y = (xf - mu) * lax.rsqrt(var + EPS) * g.astype(jnp.float32) + b.astype(jnp.float32)
    return y.astype(x.dtype)

def _rope_tables(seq):
    half = MLA_ROPE // 2
    inv_freq = ROPE_THETA_2 ** (-jnp.arange(half, dtype=jnp.float32) / half)
    ang = jnp.arange(seq, dtype=jnp.float32)[:, None] * inv_freq[None, :]
    return jnp.cos(ang), jnp.sin(ang)

def _apply_rope(x, cos, sin):
    half = MLA_ROPE // 2
    c = cos[None, :, None, :].astype(x.dtype)
    s = sin[None, :, None, :].astype(x.dtype)
    x1, x2 = x[..., :half], x[..., half:]
    return jnp.concatenate([x1 * c - x2 * s, x1 * s + x2 * c], axis=-1)

def _conv_branch(a, a_glu, conv_w, conv_b, ln_g, ln_b, pw_w, pw_b):
    y = a * jax.nn.sigmoid(a_glu)
    y = lax.conv_general_dilated(
        y, conv_w[:, None, :], window_strides=(1,),
        padding=[(CONV_K - 1, 0)],
        dimension_numbers=('NWC', 'WIO', 'NWC'),
        feature_group_count=CONV_WIDTH_2) + conv_b
    y = jax.nn.silu(_layer_norm(y, ln_g, ln_b))
    return y @ pw_w + pw_b

def _causal_attention(q, k, v):
    B, S, H, Dq = q.shape
    nb = S // Q_BLOCK
    scale = Dq ** -0.5
    q_blocks = jnp.moveaxis(q.reshape(B, nb, Q_BLOCK, H, Dq), 1, 0)
    k_pos = jnp.arange(S)

    def block(args):
        qb, i = args
        q_pos = i * Q_BLOCK + jnp.arange(Q_BLOCK)
        s = jnp.einsum('bqhd,bkhd->bhqk', qb, k).astype(jnp.float32) * scale
        s = jnp.where(k_pos[None, :] <= q_pos[:, None], s, -jnp.inf)
        p = jax.nn.softmax(s, axis=-1).astype(v.dtype)
        return jnp.einsum('bhqk,bkhd->bqhd', p, v)

    out = lax.map(block, (q_blocks, jnp.arange(nb)))
    return jnp.moveaxis(out, 0, 1).reshape(B, S, H * v.shape[-1])

def _mla_branch(c_q, c_kv, k_rope, q_norm_g, w_uq, kv_norm_g, w_ukv,
                qk_q_g, qk_k_g, cos, sin):
    B, S, _ = c_q.shape
    q = (_rms_norm(c_q, q_norm_g) @ w_uq).reshape(B, S, MLA_HEADS, MLA_QK)
    kv = (_rms_norm(c_kv, kv_norm_g) @ w_ukv).reshape(B, S, MLA_HEADS, MLA_NOPE + MLA_V)
    k_nope, v = kv[..., :MLA_NOPE], kv[..., MLA_NOPE:]
    k_r = jnp.broadcast_to(k_rope[:, :, None, :], (B, S, MLA_HEADS, MLA_ROPE))
    k = jnp.concatenate([k_nope, k_r], axis=-1)
    q = _rms_norm(q, qk_q_g)
    k = _rms_norm(k, qk_k_g)
    q = jnp.concatenate([q[..., :MLA_NOPE], _apply_rope(q[..., MLA_NOPE:], cos, sin)], axis=-1)
    k = jnp.concatenate([k[..., :MLA_NOPE], _apply_rope(k[..., MLA_NOPE:], cos, sin)], axis=-1)
    return _causal_attention(q, k, v)

def _sgu_branch(u, v, ln_g, ln_b, sg_w, sg_b):
    B, S, _ = u.shape
    nc = S // SG_CHUNK
    u = jax.nn.gelu(u)
    v = _layer_norm(jax.nn.gelu(v), ln_g, ln_b)
    v = v.reshape(B, nc, SG_CHUNK, SG_HEADS, SG_HEAD_DIM)
    mask = jnp.tril(jnp.ones((SG_CHUNK, SG_CHUNK), dtype=bool))
    w = jnp.where(mask[None], sg_w, jnp.zeros_like(sg_w))
    mixed = jnp.einsum('gts,bcsgd->bctgd', w, v) + sg_b.T[None, None, :, :, None]
    return u * mixed.reshape(B, S, SG_WIDTH)

def _layer(x, cos, sin, norm_g, w_in, conv_w, conv_b, conv_ln_g, conv_ln_b,
           conv_pw_w, conv_pw_b, q_norm_g, w_uq, kv_norm_g, w_ukv, qk_q_g, qk_k_g,
           sg_ln_g, sg_ln_b, sg_w, sg_b, branch_norm_g, w_out):
    h = _rms_norm(x, norm_g)
    proj = h @ w_in
    idx = np.cumsum(IN_SIZES)[:-1].tolist()
    (a, a_glu, z_conv, c_q, c_kv, k_rope, z_mla,
     u_sg, v_sg, z_sg) = jnp.split(proj, idx, axis=-1)

    y_conv = _conv_branch(a, a_glu, conv_w, conv_b, conv_ln_g, conv_ln_b,
                          conv_pw_w, conv_pw_b) * jax.nn.silu(z_conv)
    y_mla = _mla_branch(c_q, c_kv, k_rope, q_norm_g, w_uq, kv_norm_g, w_ukv,
                        qk_q_g, qk_k_g, cos, sin) * jax.nn.silu(z_mla)
    y_sg = _sgu_branch(u_sg, v_sg, sg_ln_g, sg_ln_b, sg_w, sg_b) * jax.nn.silu(z_sg)

    g_conv = branch_norm_g[:CONV_WIDTH_2]
    g_mla = branch_norm_g[CONV_WIDTH_2:CONV_WIDTH_2 + MLA_WIDTH]
    g_sg = branch_norm_g[CONV_WIDTH_2 + MLA_WIDTH:]
    y = jnp.concatenate([_rms_norm(y_conv, g_conv),
                         _rms_norm(y_mla, g_mla),
                         _rms_norm(y_sg, g_sg)], axis=-1)
    return x + y @ w_out

def second_inputs(seed: int = 0) -> dict:
    key = jax.random.key(seed)
    ks = jax.random.split(key, 24)
    f32 = jnp.float32

    def nrm(k, shape, scale):
        return jax.random.normal(k, shape, f32) * scale

    def gain(k, shape):
        return 1.0 + 0.02 * jax.random.normal(k, shape, f32)

    L = DEPTH
    return {
        'x': jax.random.normal(ks[0], (BATCH, SEQ, D_MODEL), f32),
        'norm_g': gain(ks[1], (L, D_MODEL)),
        'w_in': nrm(ks[2], (L, D_MODEL, IN_COLS_2), D_MODEL ** -0.5),
        'conv_w': nrm(ks[3], (L, CONV_K, CONV_WIDTH_2), CONV_K ** -0.5),
        'conv_b': nrm(ks[4], (L, CONV_WIDTH_2), 0.01),
        'conv_ln_g': gain(ks[5], (L, CONV_WIDTH_2)),
        'conv_ln_b': nrm(ks[6], (L, CONV_WIDTH_2), 0.01),
        'conv_pw_w': nrm(ks[7], (L, CONV_WIDTH_2, CONV_WIDTH_2), CONV_WIDTH_2 ** -0.5),
        'conv_pw_b': nrm(ks[8], (L, CONV_WIDTH_2), 0.01),
        'q_norm_g': gain(ks[9], (L, Q_LORA)),
        'w_uq': nrm(ks[10], (L, Q_LORA, MLA_HEADS * MLA_QK), Q_LORA ** -0.5),
        'kv_norm_g': gain(ks[11], (L, KV_LORA)),
        'w_ukv': nrm(ks[12], (L, KV_LORA, MLA_HEADS * (MLA_NOPE + MLA_V)), KV_LORA ** -0.5),
        'qk_q_g': gain(ks[13], (L, MLA_QK)),
        'qk_k_g': gain(ks[14], (L, MLA_QK)),
        'sg_ln_g': gain(ks[15], (L, SG_WIDTH)),
        'sg_ln_b': nrm(ks[16], (L, SG_WIDTH), 0.01),
        'sg_w': nrm(ks[17], (L, SG_HEADS, SG_CHUNK, SG_CHUNK), SG_CHUNK ** -0.5),
        'sg_b': 1.0 + nrm(ks[18], (L, SG_HEADS, SG_CHUNK), 0.1),
        'branch_norm_g': gain(ks[19], (L, D_MIX)),
        'w_out': nrm(ks[20], (L, D_MIX, D_MODEL), D_MIX ** -0.5),
    }

def second_block(x, norm_g, w_in, conv_w, conv_b, conv_ln_g, conv_ln_b, conv_pw_w,
              conv_pw_b, q_norm_g, w_uq, kv_norm_g, w_ukv, qk_q_g, qk_k_g,
              sg_ln_g, sg_ln_b, sg_w, sg_b, branch_norm_g, w_out):
    cos, sin = _rope_tables(x.shape[1])
    for l in range(DEPTH):
        x = _layer(x, cos, sin, norm_g[l], w_in[l], conv_w[l], conv_b[l],
                   conv_ln_g[l], conv_ln_b[l], conv_pw_w[l], conv_pw_b[l],
                   q_norm_g[l], w_uq[l], kv_norm_g[l], w_ukv[l], qk_q_g[l], qk_k_g[l],
                   sg_ln_g[l], sg_ln_b[l], sg_w[l], sg_b[l], branch_norm_g[l], w_out[l])
    return x


def setup_inputs(seed=0):
    out = dict(first_inputs(seed))
    for name, value in second_inputs(seed + 1).items():
        if name != "x":
            out[name + "_2"] = value
    return out


def reference(
    x, norm_g, w_in, attn_lambda, attn_subln_g, conv_w, w_branch, w_out, final_norm_g, norm_g_2,
    w_in_2, conv_w_2, conv_b_2, conv_ln_g_2, conv_ln_b_2, conv_pw_w_2, conv_pw_b_2, q_norm_g_2,
    w_uq_2, kv_norm_g_2, w_ukv_2, qk_q_g_2, qk_k_g_2, sg_ln_g_2, sg_ln_b_2, sg_w_2, sg_b_2,
    branch_norm_g_2, w_out_2,
):
    x = first_block(
        x, norm_g, w_in, attn_lambda, attn_subln_g, conv_w, w_branch, w_out, final_norm_g,
    )
    return second_block(
        x, norm_g_2, w_in_2, conv_w_2, conv_b_2, conv_ln_g_2, conv_ln_b_2, conv_pw_w_2,
        conv_pw_b_2, q_norm_g_2, w_uq_2, kv_norm_g_2, w_ukv_2, qk_q_g_2, qk_k_g_2, sg_ln_g_2,
        sg_ln_b_2, sg_w_2, sg_b_2, branch_norm_g_2, w_out_2,
    )


_drawn_inputs = setup_inputs


def setup_inputs(seed=0):
    import zlib

    import numpy as np

    out = dict(_drawn_inputs(seed))
    spreads = {}
    factors = {'attn_subln_g': 8.0,
     'final_norm_g': 3.452,
     'conv_b_2': 4.823,
     'conv_ln_g_2': 35.232,
     'conv_ln_b_2': 64.0,
     'conv_pw_b_2': 45.36,
     'q_norm_g_2': 4.593,
     'qk_q_g_2': 5.279,
     'qk_k_g_2': 4.459,
     'sg_ln_g_2': 64.0,
     'sg_ln_b_2': 200.0,
     'sg_b_2': 6.468,
     'branch_norm_g_2': 5.282}
    for name, (base, spread) in spreads.items():
        noise = np.random.default_rng([zlib.crc32(name.encode()), seed]).standard_normal(out[name].shape)
        drawn = base * np.exp(spread * noise) if base else spread * noise
        out[name] = __import__('jax').numpy.asarray(drawn.astype(out[name].dtype))
    for name, factor in factors.items():
        out[name] = (out[name] * factor).astype(out[name].dtype)
    return out
```

```python
from contextlib import ExitStack

import numpy as np
import concourse.bass as bass
from concourse import mybir

F32 = mybir.dt.float32
F32R = mybir.dt.float32r
BF16 = mybir.dt.bfloat16
ALU = mybir.AluOpType
ACT = mybir.ActivationFunctionType
AX_X = mybir.AxisListType.X



class Group:
    pass


P = 128
SEQ, D_MODEL, DEPTH = 1024, 1024, 2
KT = D_MODEL // P
NT = SEQ // P
HALF = SEQ // 2
EPS = 1e-6
NEG = -1e30

HEADS = 4
A_QK = 64
B1_TILES = 4
R_CHUNK = 128
M_HEADS, M_NOPE, M_ROPE, M_V = 8, 64, 32, 64
M_QK = M_NOPE + M_ROPE
Q_LORA_T, KV_LORA_T = 6, 2
CONV_K = 31
PAD = CONV_K - 1


def panels_of_block1():
    out = []
    for h in range(HEADS):
        out += [(("aq", h), KT, P), (("ak", h), KT, P), (("av", h), KT, P), (("az", h), KT, P)]
    out += merge_panels(0)
    for t in range(B1_TILES):
        out += [(("cx", t), KT, P), (("cc", t), KT, P), (("cb", t), KT, P), (("cz", t), KT, P)]
    out += merge_panels(1)
    for pr in range(HEADS // 2):
        out += [(("rq", pr), KT, P), (("rk", pr), KT, P)]
        for h in (2 * pr, 2 * pr + 1):
            out += [(("rv", h), KT, P), (("rz", h), KT, P)]
    out += merge_panels(2)
    out += [(("out", j), KT, P) for j in range(KT)]
    return out


def merge_panels(i):
    out = []
    for j in range(KT):
        out += [(("gate", i, j), KT, P), (("branch", i, j), B1_TILES, P)]
    return out


def panels_of_block2():
    out = []
    for t in (0, 1):
        out += [(("g", t), KT, P), (("a", t), KT, P)]
    out += [(("zc", t), KT, P) for t in (0, 1)]
    out += [(("cq", t), KT, P) for t in range(Q_LORA_T)]
    out += [(("ckv", t), KT, P) for t in range(KV_LORA_T)]
    out += [(("kr", 0), KT // 2, M_QK), (("kr", 1), KT // 2, M_QK)]
    out += [(("zm", t), KT, P) for t in range(4)]
    for n in ("v", "u", "zs"):
        out += [((n, t), KT, P) for t in (0, 1)]
    for h in range(M_HEADS):
        out += [(("q", h), Q_LORA_T, M_QK), (("kv", h), KV_LORA_T, P)]
    out += [(("out", j), KT, P) for j in range(KT)]
    return out


def runs(panels):
    out, off = [], 0
    for p in range(0, len(panels), 2):
        sizes = [panels[p + b][1] * panels[p + b][2] for b in (0, 1)]
        if out and out[-1][2] == sizes:
            out[-1][1] += 1
        else:
            out.append([p, 1, sizes, off])
        off += sum(sizes)
    return out, off


def uses_of_block1():
    a, t = [], []
    for h in range(HEADS):
        a += [("aq", h), ("ak", h), ("av", h), ("az", h)]
        t += [("swapq", h), ("swapk", h), ("vt", h)]
        for q in range(NT):
            a += [("s", h, q, 0), ("s", h, q, 1)]
            t += [("pt", h, q)]
            if q % 4 == 3:
                t += [("av", h, q // 4), ("ss", h, q // 4)]
    a += [x[0] for x in merge_panels(0)]
    for c in range(B1_TILES):
        a += [("cx", c), ("cc", c), ("cb", c), ("cz", c)]
    a += [x[0] for x in merge_panels(1)]
    for pr in range(HEADS // 2):
        a += [("rq", pr), ("rk", pr)]
        t += [("swaprq", pr), ("swaprk", pr), ("ks", pr)]
        for h in (2 * pr, 2 * pr + 1):
            a += [("rv", h), ("rz", h), ("rs", h), ("ro", h)]
            t += [("rvt", h), ("kv", h), ("rss", h)]
    a += [x[0] for x in merge_panels(2)]
    return a, t


def uses_of_block2():
    a, t = [], []
    for c in (0, 1):
        a += [("g", c), ("a", c)]
    a += [("zc", c) for c in (0, 1)] + [("cq", c) for c in range(Q_LORA_T)] + [("ckv", c) for c in range(KV_LORA_T)]
    a += [("zm", c) for c in range(4)] + [(n, c) for n in ("v", "u", "zs") for c in (0, 1)]
    a += [("pw", 0), ("pw", 1), ("sg", 0), ("sg", 1)]
    t += ["kr", "cqs", "ckvs", "cmean", "cvar", "cbn", "smean", "svar", ("vst", 0), ("vst", 1), "wgt", "sbn", "krswap"]
    for h in range(M_HEADS):
        a += [("q", h), ("kv", h)]
        t += [("qs", h), ("ks", h), ("vt", h), ("qswap", h)]
        for q in range(NT):
            a += [("s", h, q)]
            t += [("pt", h, q)]
            if q % 4 == 3:
                t += [("av", h, q // 4)]
    t += ["mbn"]
    return a, t


class Ring:

    def __init__(self, name, uses, sem):
        assert len(uses) % 2 == 0, (name, len(uses))
        self.n = len(uses)
        self.at = {u: i for i, u in enumerate(uses)}
        self.filled_sem = sem(f"{name}_filled")
        self.drained_sem = [sem(f"{name}{b}_drained") for b in (0, 1)]

    def buf(self, use):
        return self.at[use] % 2

    def filled(self, L, use, j=0):
        return self.filled_sem, L * self.n + self.at[use] + 1 + 2 * j

    def drained(self, L, use, j=0):
        u = self.at[use]
        return self.drained_sem[u % 2], L * (self.n // 2) + u // 2 + 1 + j

    def before(self, use):
        return self.at[use] >= 2

    def room(self, L, use, j=0):
        u = self.at[use]
        return self.drained_sem[u % 2], L * (self.n // 2) + u // 2 + j

    def freed(self, use):
        return self.drained_sem[self.at[use] % 2]


class Tally:

    def __init__(self, sem, per_layer, before=0):
        self.sem, self.per, self.before = sem, per_layer, before

    def upto(self, L, k):
        return self.sem, L * self.per + k + self.before


class Chain:

    def __init__(self, sem, per_layer, base=0):
        self.sem, self.per, self.k, self.L, self.base = sem, per_layer, 0, 0, base

    def step(self, eng, ins):
        ins.then_inc(self.sem, 1)
        self.k += 1
        eng.wait_ge(self.sem, self.L * self.per + self.k + self.base)

    def layer(self, L):
        self.k, self.L = 0, L


P1, P2 = panels_of_block1(), panels_of_block2()
PAN1 = {p[0]: i for i, p in enumerate(P1)}
PAN2 = {p[0]: i for i, p in enumerate(P2)}
RUNS1, COLS1 = runs(P1)
RUNS2, COLS2 = runs(P2)

class C1:
    norm = 0
    subln = KT
    conv = KT + 1
    lam_init = KT + 13
    lam_rest = KT + 14
    n = KT + 15


class C2:
    norm = 0
    conv_w = 8
    conv_b = 8 + 62
    cln_g = 72
    cln_b = 74
    pwb = 76
    qn = 78
    kvn = 84
    qg = 86
    kg = 87
    sln_g = 88
    sln_b = 90
    bn = 92
    n = 100


class K:
    ident = 0
    ones = 128
    mask = 256
    swapa = 384
    swapr = 512
    swapm = 640
    causal = 768
    dmask = 896
    xi = 896 + 512
    zeta = 896 + 768
    decay = 896 + 1024
    n = 896 + 1024 + 2




def build(nc, per1, per2, x, w1, par1, lamv, finalg, w2, par2, pww, sgw, sgb, consts, ropes, out, xs):
    counts = {}
    with ExitStack() as top:
        def sem(name):
            return top.enter_context(nc.semaphore(name))

        def sb(name, shape, dt=F32):
            return top.enter_context(nc.sbuf_tensor(name, shape, dt))

        X = sb("X", [P, KT, SEQ])
        Hhi = sb("Hhi", [P, KT, SEQ], F32R)
        Hlo = sb("Hlo", [P, KT, SEQ], F32R)
        stage = sb("stage", [P, 2, KT * P])
        Whi = sb("Whi", [P, 2, KT * P], F32R)
        Wlo = sb("Wlo", [P, 2, KT * P], F32R)
        ident = sb("ident", [P, P])
        ones = sb("ones", [P, P])
        identb = sb("identb", [P, P], BF16)
        maskb = sb("maskb", [P, P], BF16)
        rope = sb("rope", [P, 2, SEQ])
        epsc = sb("epsc", [P, 1])
        psA = top.enter_context(nc.psum_tensor("psA", [P, 2, SEQ], F32))
        psT = top.enter_context(nc.psum_tensor("psT", [P, 2, SEQ], F32))
        env = Group()
        env.nc, env.x, env.w1, env.par1, env.lamv, env.finalg = nc, x, w1, par1, lamv, finalg
        env.w2, env.par2, env.pww, env.sgw, env.sgb, env.consts = w2, par2, pww, sgw, sgb, consts
        env.ropes, env.out, env.xs, env.X, env.Hhi, env.Hlo = ropes, out, xs, X, Hhi, Hlo
        env.stage, env.Whi, env.Wlo, env.ident, env.ones, env.identb = stage, Whi, Wlo, ident, ones, identb
        env.maskb, env.rope, env.epsc, env.psA, env.psT = maskb, rope, epsc, psA, psT
        first_block(env, per1, counts)
        second_block(env, per2, counts)
    return counts


def halves(ps, m=P, lo=0):
    return [ps[lo:lo + m, h * HALF:(h + 1) * HALF] for h in (0, 1)]


def three_pass(pe, ps, whi, wlo, rhi, rlo, nk, M, begun, first=True, last=True):
    dst = halves(ps, M)
    for k in range(nk):
        cols = slice(k * M, (k + 1) * M)
        for w, r, end in ((whi, rhi, False), (whi, rlo, False), (wlo, rhi, True)):
            for h in (0, 1):
                mm = pe.matmul(dst[h], w[:, cols], r[k][:, h * HALF:(h + 1) * HALF],
                               start=first and k == 0 and r is rhi and w is whi,
                               stop=last and k == nk - 1 and end)
                if begun is not None:
                    mm.then_inc(begun, 1)
                    begun = None
    return mm


def weight_engines(block, s, w_dram, stage, Whi, Wlo, panels, the_runs, load_inputs):
    NP = len(panels)

    @block.sync
    def _(sp):
        load_inputs(sp)
        with sp.Fori(0, DEPTH) as L:
            for p0, pairs, sizes, off in the_runs:
                with sp.Fori(0, pairs) as i:
                    for b in (0, 1):
                        sp.wait_ge(s.w_split, L * NP + p0 + b + 1 + i * 2)
                        start = off + b * sizes[0] + i * sum(sizes)
                        sp.dma_start(stage[:, b, 0:sizes[b]], w_dram[L, :, bass.ds(start, sizes[b])])\
                            .then_inc(s.w_loaded[b], 16)

    @block.gpsimd
    def _(pool):
        pool.memset(s.credit[:, 0:1], 0.0).then_inc(s.w_split, 2)
        pool.memset(s.credit[:, 1:2], 0.0).then_inc(s.panel_begun, 1)
        pool.wait_ge(s.w_split, 2)
        with pool.Fori(0, DEPTH) as L:
            for p0, pairs, sizes, off in the_runs:
                with pool.Fori(0, pairs) as i:
                    for b in (0, 1):
                        n = sizes[b]
                        pool.wait_ge(s.w_loaded[b], (L * (NP // 2) + p0 // 2 + 1 + i) * 16)
                        pool.wait_ge(s.panel_begun, L * NP + p0 + b + 1 + i * 2)
                        pool.tensor_tensor(Whi[:, b, 0:n], stage[:, b, 0:n], s.credit[:, 0:1].broadcast_to([P, n]),
                                           ALU.add).then_inc(s.w_hi, 1)
                        pool.wait_ge(s.w_hi, L * NP + p0 + b + 1 + i * 2)
                        pool.tensor_tensor(Wlo[:, b, 0:n], stage[:, b, 0:n], Whi[:, b, 0:n].bitcast(F32),
                                           ALU.subtract).then_inc(s.w_split, 1)




def first_block(env, per, counts):
    nc, X, Hhi, Hlo, rope, ident, ones = env.nc, env.X, env.Hhi, env.Hlo, env.rope, env.ident, env.ones
    psA, psT, identb, maskb, epsc = env.psA, env.psT, env.identb, env.maskb, env.epsc
    SCALE = A_QK ** -0.5
    with ExitStack() as ctx:
        def sem(name):
            return ctx.enter_context(nc.semaphore("b1_" + name))

        def sb(name, shape, dt=F32):
            return ctx.enter_context(nc.sbuf_tensor("b1_" + name, shape, dt))

        Bhi = sb("Bhi", [P, B1_TILES, SEQ], F32R)
        Blo = sb("Blo", [P, B1_TILES, SEQ], F32R)
        wk = sb("wk", [P, 8, SEQ])
        upad = sb("upad", [P, SEQ + 2])
        par = sb("par", [P, DEPTH, C1.n])
        cur = sb("cur", [P, C1.n])
        fing = sb("fing", [P, KT])
        lamraw = sb("lamraw", [P, DEPTH, 4 * A_QK])
        lamt = sb("lamt", [P, 2 * A_QK])
        lam = sb("lam", [P, 6])
        gcol = sb("gcol", [P, 1])
        swapa = sb("swapa", [P, P])
        swapr = sb("swapr", [P, P])
        rtab = sb("rtab", [P, K.n - K.dmask])
        rowmax = sb("rowmax", [P, 2])
        negmax = sb("negmax", [P, 2, 2])
        rowsum = sb("rowsum", [P, 2, 2])
        inv = sb("inv", [P, 2, 2])
        credit = sb("credit", [P, 2])

        a_uses, t_uses = uses_of_block1()
        A = Ring("b1A", a_uses, lambda n: ctx.enter_context(nc.semaphore(n)))
        T = Ring("b1T", t_uses, lambda n: ctx.enter_context(nc.semaphore(n)))
        NP = len(P1)
        s = Group()
        s.credit, s.w_split, s.w_hi, s.panel_begun = credit, sem("w_split"), sem("w_hi"), sem("panel_begun")
        s.w_loaded = [sem("w_loaded0"), sem("w_loaded1")]
        consts_in, params_in, mask_in = sem("consts_in"), sem("params_in"), sem("mask_in")
        x_in = [sem("x_in0"), sem("x_in1")]
        x_turned, setup = sem("x_turned"), sem("setup")
        rope_in = Tally(sem("rope_in"), 2 * 16)
        x_ready = Tally(sem("x_ready"), KT)
        out_filled = Tally(sem("out_filled"), KT)
        x_saved = Tally(sem("x_saved"), 16)
        x_back = [Tally(sem(f"x_back{b}"), 16 * KT // 2) for b in (0, 1)]
        sq_done, sq_used = Tally(sem("sq_done"), KT), Tally(sem("sq_used"), KT)
        rstd = Tally(sem("rstd"), 1)
        h_scaled, h_hi, h_lo = (Tally(sem(n), KT) for n in ("h_scaled", "h_hi", "h_lo"))
        lam_sum, lam_exp = Tally(sem("lam_sum"), 1), Tally(sem("lam_exp"), 1)
        rotated = Tally(sem("rotated"), 2 * HEADS)
        z_ready = Tally(sem("z_ready"), HEADS)
        nmax = Tally(sem("nmax"), HEADS * NT)
        mixed = Tally(sem("mixed"), HEADS * NT)
        a_sq, a_rs, a_out = (Tally(sem(n), 2 * HEADS) for n in ("a_sq", "a_rs", "a_out"))
        b_hi, b_lo = (Tally(sem(n), 2 * HEADS + 2 * B1_TILES) for n in ("b_hi", "b_lo"))
        merged = Tally(sem("merged"), 2 * KT)
        c_out = Tally(sem("c_out"), B1_TILES)
        rk_scaled, r_rot = Tally(sem("rk_scaled"), HEADS // 2), Tally(sem("r_rot"), HEADS)
        r_sq, r_rs, r_out = (Tally(sem(n), HEADS) for n in ("r_sq", "r_rs", "r_out"))
        m_hi, m_lo = Tally(sem("m_hi"), KT), Tally(sem("m_lo"), KT)
        f_sq, f_used, f_sum, f_rs = (sem(n) for n in ("f_sq", "f_used", "f_sum", "f_rs"))
        dve_step = Chain(sem("dve_step"), per.get("d1", 1), 2)
        act_step = Chain(sem("act_step"), 1)

        Q, KK, V, Z = (wk[:, i] for i in range(4))
        PR = [[wk[:, 4], wk[:, 5]], [wk[:, 6], wk[:, 7]]]
        ROT = wk[:, 7]
        WT = X[:, 0:4].rearrange("p a b -> p (a b)").rearrange("p (k q) -> p k q", k=NT)
        RAWQ, RAWK, RAWV, TMP = X[:, 4], X[:, 5], X[:, 6], X[:, 7]
        RSQ, R_RAWQ, R_RAWK, R_RAWV = upad[:, 2:], wk[:, 4], wk[:, 5], wk[:, 6]
        KZ, SM, KS, ST, QX = wk[:, 4], wk[:, 4], wk[:, 5], wk[:, 6], wk[:, 7]
        DM = rtab[:, 0:HEADS * P].rearrange("p (h c) -> p h c", h=HEADS)
        XI = rtab[:, K.xi - K.dmask:K.zeta - K.dmask].rearrange("p (h c) -> p h c", h=2)
        ZE = rtab[:, K.zeta - K.dmask:K.decay - K.dmask].rearrange("p (h c) -> p h c", h=2)
        DEC = rtab[:, K.decay - K.dmask:]
        x_tiles = env.x.rearrange("(t p) d -> t p d", p=P)
        xs_v = env.xs.rearrange("j p n -> p j n")

        def by_chunk(ap):
            return ap.rearrange("p (n c) -> p n c", n=NT)

        def every_chunk(ap):
            return ap.unsqueeze(1).broadcast_to([ap.shape[0], NT, ap.shape[1]])

        def tile_of(ap, j):
            return ap[:, bass.ds(j, 1), :].rearrange("p a b -> p (a b)")

        def head_rows(h):
            return slice((h % 2) * A_QK, (h % 2 + 1) * A_QK)

        block = ctx.enter_context(nc.Block())

        def load_inputs(sp):
            for k, dst in ((K.ident, ident), (K.ones, ones), (K.swapa, swapa), (K.swapr, swapr)):
                sp.dma_start(dst[:], env.consts[:, k:k + P]).then_inc(consts_in, 16)
            sp.dma_start(wk[:, 0, 0:P], env.consts[:, K.mask:K.mask + P]).then_inc(mask_in, 16)
            for t in range(NT):
                if t >= 2:
                    sp.wait_ge(x_turned, t - 1)
                sp.dma_start(wk[:, 2 + t % 2], x_tiles[t]).then_inc(x_in[t % 2], 16)
            sp.dma_start(rtab[:], env.consts[:, K.dmask:K.n]).then_inc(params_in, 16)
            sp.dma_start(par[:], env.par1.rearrange("l p c -> p l c")).then_inc(params_in, 16)
            sp.dma_start(fing[:], env.finalg).then_inc(params_in, 16)
            sp.dma_start(lamraw[:], env.lamv.rearrange("l c -> (l c)").partition_broadcast(P)
                         .rearrange("p (l c) -> p l c", l=DEPTH)).then_inc(params_in, 16)

        weight_engines(block, s, env.w1, env.stage, env.Whi, env.Wlo, P1, RUNS1, load_inputs)

        @block.tensor
        def _(pe):
            def panel(L, name, rhi, rlo, nk=KT, j=0):
                p = PAN1[name]
                pe.wait_ge(s.w_split, L * NP + p + 3 + j * 2)
                if name[0] == "out":
                    pe.wait_ge(*x_ready.upto(L + 1, name[1] - 1 + j * 2))
                    dst, done = psA[:, name[1] % 2], out_filled.sem
                else:
                    if A.before(name):
                        pe.wait_ge(*A.room(L, name, j))
                    dst, done = psA[:, A.buf(name)], A.filled_sem
                three_pass(pe, dst, env.Whi[:, p % 2], env.Wlo[:, p % 2], [rhi[:, k] for k in range(nk)],
                           [rlo[:, k] for k in range(nk)], nk, P, s.panel_begun).then_inc(done, 1)

            def full(dst, lhsT, rhs, start=True, stop=True):
                for h in (0, 1):
                    c = slice(h * HALF, (h + 1) * HALF)
                    mm = pe.matmul(dst[:, c], lhsT, rhs[:, c], start=start, stop=stop)
                return mm

            def turn(dst, src, blocks):
                for i in range(blocks):
                    mm = pe.transpose(dst[:, i * P:(i + 1) * P], src[:, i * P:(i + 1) * P], ident[:])
                return mm

            def swap(L, use, raw, mat, raw_tile):
                pe.wait_ge(*A.drained(L, raw))
                pe.wait_ge(*T.room(L, use))
                full(psT[:, T.buf(use)], mat[:], raw_tile).then_inc(T.filled_sem, 1)

            def scores(L, h, q):
                for c in (0, 1):
                    use = ("s", h, q, c)
                    pe.wait_ge(*A.room(L, use))
                    if q == 0 and c == 0:
                        pe.wait_ge(*rotated.upto(L, 2 * h + 2))
                    dst, rows = psA[:, A.buf(use)], slice(c * A_QK, (c + 1) * A_QK)
                    n = (q + 1) * P
                    for k0 in range(0, n, HALF):
                        k1 = min(n, k0 + HALF)
                        pe.matmul(dst[:, k0:k1], Q[rows, q * P:n], KK[rows, k0:k1], start=True, stop=k1 < n)
                    pe.matmul(dst[:, q * P:n], identb[:], maskb[:], start=False, stop=True)\
                        .then_inc(A.filled_sem, 1)

            def attend(L, h):
                scores(L, h, 0)
                for q in range(NT):
                    if q + 1 < NT:
                        scores(L, h, q + 1)
                    use = ("pt", h, q)
                    pe.wait_ge(*T.room(L, use))
                    pe.wait_ge(*mixed.upto(L, h * NT + q + 1))
                    turn(psT[:, T.buf(use)], PR[q % 2][0], q + 1).then_inc(T.filled_sem, 1)
                    if q % 4 == 3:
                        g = q // 4
                        use = ("av", h, g)
                        pe.wait_ge(*T.drained(L, ("pt", h, q)))
                        pe.wait_ge(*T.drained(L, ("vt", h)))
                        pe.wait_ge(*T.room(L, use))
                        for k in range(q + 1):
                            c0 = max(0, k - 4 * g) * P
                            mm = pe.matmul(psT[:, T.buf(use), c0:HALF], V[:, k * P:(k + 1) * P], WT[:, k, c0:],
                                           start=k == 0, stop=k == q)
                        mm.then_inc(T.filled_sem, 1)
                        use = ("ss", h, g)
                        pe.wait_ge(*T.room(L, use))
                        pe.wait_ge(*a_sq.upto(L, 2 * h + g + 1))
                        pe.matmul(psT[:, T.buf(use), 0:HALF], ones[:], TMP[:, 0:HALF], start=True, stop=True)\
                            .then_inc(T.filled_sem, 1)

            def merge(L, i):
                with pe.Fori(0, KT) as j:
                    pe.wait_ge(*b_lo.upto(L, (8, 12, 16)[i]))
                    pe.wait_ge(*b_hi.upto(L, (8, 12, 16)[i]))
                    panel(L, ("gate", i, 0), Hhi, Hlo, j=j)
                    panel(L, ("branch", i, 0), Bhi, Blo, B1_TILES, j=j)

            def retain(L, pr, h):
                rows = head_rows(h)
                if h % 2 == 0:
                    use = ("ks", pr)
                    pe.wait_ge(*rk_scaled.upto(L, pr + 1))
                    pe.wait_ge(*T.room(L, use))
                    turn(psT[:, T.buf(use)], KZ, NT).then_inc(T.filled_sem, 1)
                use = ("rvt", h)
                pe.wait_ge(*A.drained(L, ("rv", h)))
                pe.wait_ge(*T.room(L, use))
                turn(psT[:, T.buf(use)], R_RAWV, NT).then_inc(T.filled_sem, 1)
                use = ("rs", h)
                pe.wait_ge(*r_rot.upto(L, 2 * pr + 2))
                pe.wait_ge(*A.room(L, use))
                for n in range(NT):
                    c = slice(n * P, (n + 1) * P)
                    mm = pe.matmul(psA[:, A.buf(use), c], KK[rows, c], Q[rows, c], start=True, stop=True)
                mm.then_inc(A.filled_sem, 1)
                use = ("kv", h)
                pe.wait_ge(*T.drained(L, ("rvt", h)))
                pe.wait_ge(*T.drained(L, ("ks", pr)))
                pe.wait_ge(*T.room(L, use))
                for n in range(NT - 1):
                    mm = pe.matmul(psT[rows, T.buf(use), n * P:(n + 1) * P],
                                   KS[:, n * P + (h % 2) * A_QK:n * P + (h % 2 + 1) * A_QK],
                                   V[:, n * P:(n + 1) * P], start=True, stop=True)
                mm.then_inc(T.filled_sem, 1)
                use = ("ro", h)
                pe.wait_ge(*A.room(L, use))
                pe.wait_ge(*A.drained(L, ("rs", h)))
                pe.wait_ge(*T.drained(L, ("kv", h)))
                for n in range(NT):
                    c = slice(n * P, (n + 1) * P)
                    mm = pe.matmul(psA[:, A.buf(use), c], V[:, c], SM[:, c], start=True, stop=n == 0)
                    if n:
                        mm = pe.matmul(psA[:, A.buf(use), c], ST[rows, c], QX[rows, c], start=False, stop=True)
                mm.then_inc(A.filled_sem, 1)
                use = ("rss", h)
                pe.wait_ge(*r_sq.upto(L, h + 1))
                pe.wait_ge(*T.room(L, use))
                full(psT[:, T.buf(use)], ones[:], RSQ).then_inc(T.filled_sem, 1)

            pe.wait_ge(consts_in, 64)
            for t in range(NT):
                pe.wait_ge(x_in[t % 2], 16 * (t // 2 + 1))
                if t >= 2:
                    pe.wait_ge(x_ready.sem, t - 1)
                turn(psA[:, t % 2], wk[:, 2 + t % 2], KT).then_inc(x_turned, 1)
            pe.wait_ge(setup, 1)

            with pe.Fori(0, DEPTH) as L:
                for j in range(KT):
                    pe.wait_ge(*sq_done.upto(L, j + 1))
                    full(psT[:, 0], ones[:], wk[:, j % 2], j == 0, j == KT - 1).then_inc(sq_used.sem, 1)
                pe.wait_ge(*h_hi.upto(L, KT))
                pe.wait_ge(*h_lo.upto(L, KT))
                for h in range(HEADS):
                    panel(L, ("aq", h), Hhi, Hlo)
                    panel(L, ("ak", h), Hhi, Hlo)
                    swap(L, ("swapq", h), ("aq", h), swapa, RAWQ)
                    panel(L, ("av", h), Hhi, Hlo)
                    swap(L, ("swapk", h), ("ak", h), swapa, RAWK)
                    panel(L, ("az", h), Hhi, Hlo)
                    use = ("vt", h)
                    pe.wait_ge(*A.drained(L, ("av", h)))
                    pe.wait_ge(*T.room(L, use))
                    turn(psT[:, T.buf(use)], RAWV, NT).then_inc(T.filled_sem, 1)
                    attend(L, h)
                merge(L, 0)
                for c in range(B1_TILES):
                    for n in ("cx", "cc", "cb", "cz"):
                        panel(L, (n, c), Hhi, Hlo)
                merge(L, 1)
                for pr in range(HEADS // 2):
                    panel(L, ("rq", pr), Hhi, Hlo)
                    panel(L, ("rk", pr), Hhi, Hlo)
                    swap(L, ("swaprq", pr), ("rq", pr), swapr, R_RAWQ)
                    swap(L, ("swaprk", pr), ("rk", pr), swapr, R_RAWK)
                    for h in (2 * pr, 2 * pr + 1):
                        panel(L, ("rv", h), Hhi, Hlo)
                        panel(L, ("rz", h), Hhi, Hlo)
                        retain(L, pr, h)
                merge(L, 2)
                with pe.Fori(0, KT // 2) as jj:
                    pe.wait_ge(*m_hi.upto(L, KT))
                    pe.wait_ge(*m_lo.upto(L, KT))
                    for b in (0, 1):
                        panel(L, ("out", b), Hhi, Hlo, j=jj)

            for j in range(KT):
                pe.wait_ge(f_sq, j + 1)
                full(psT[:, 0], ones[:], wk[:, j % 2], j == 0, j == KT - 1).then_inc(f_used, 1)

        @block.scalar
        def _(act):
            def root(L, use, dst, mean, done, cols=SEQ):
                act.wait_ge(*T.filled(L, use))
                act.activation(dst, psT[:, T.buf(use), 0:cols], ACT.Ln, bias=epsc[:, 0:1], scale=mean)\
                    .then_inc(T.freed(use), 1)
                act.wait_ge(*T.drained(L, use))
                act.activation(dst, dst, ACT.Exp, scale=-0.5).then_inc(done, 1)

            def take(L, use, dst, func=ACT.Copy, j=0):
                act.wait_ge(*A.filled(L, use, j))
                act.activation(dst, psA[:, A.buf(use)], func).then_inc(A.freed(use), 1)

            def exps(L, h, q):
                act.wait_ge(*nmax.upto(L, h * NT + q + 1))
                n = (q + 1) * P
                for c in (0, 1):
                    use = ("s", h, q, c)
                    act.activation(PR[q % 2][c][:, 0:n], psA[:, A.buf(use), 0:n], ACT.Exp,
                                   bias=negmax[:, q % 2, c:c + 1], scale=SCALE,
                                   accum_out=rowsum[:, q % 2, c:c + 1]).then_inc(A.freed(use), 1)

            def attend(L, h):
                exps(L, h, 0)
                for q in range(NT):
                    if q + 1 < NT:
                        exps(L, h, q + 1)
                    use = ("pt", h, q)
                    act.wait_ge(*T.filled(L, use))
                    act.activation(WT[:, 0:q + 1, (q % 4) * P:(q % 4 + 1) * P],
                                   psT[:, T.buf(use), 0:(q + 1) * P].rearrange("p (k c) -> p k c", c=P),
                                   ACT.Copy).then_inc(T.freed(use), 1)
                    if q % 4 == 3:
                        g = q // 4
                        n = 2 * h + g
                        use = ("av", h, g)
                        act.wait_ge(*T.filled(L, use))
                        if n:
                            act.wait_ge(*a_out.upto(L, n))
                        act.activation(TMP[:, 0:HALF], psT[:, T.buf(use), 0:HALF], ACT.Square)\
                            .then_inc(a_sq.sem, 1)
                        root(L, ("ss", h, g), TMP[:, 0:HALF], 1.0 / P, a_rs.sem, HALF)
                        act.wait_ge(*a_out.upto(L, n + 1))
                        act.activation(Bhi[:, h, g * HALF:(g + 1) * HALF], TMP[:, HALF:], ACT.Copy)\
                            .then_inc(b_hi.sem, 1)

            def gates(L, i):
                with act.Fori(0, KT // 2) as jj:
                    for b in (0, 1):
                        use = ("gate", i, b)
                        act.wait_ge(*A.drained(L, ("branch", i, 0), jj * 2 + b - 2))
                        act.wait_ge(*A.filled(L, use, jj * 2))
                        act.activation(wk[:, b], psA[:, A.buf(use)], ACT.Sigmoid).then_inc(A.freed(use), 1)

            with act.Fori(0, DEPTH) as L:
                act_step.layer(L)
                act.wait_ge(*x_ready.upto(L, KT))
                act.dma_start(xs_v, X[:]).then_inc(x_saved.sem, 16)
                act.dma_start(rope[:], env.ropes[0]).then_inc(rope_in.sem, 16)
                for j in range(KT):
                    if j >= 2:
                        act.wait_ge(*sq_used.upto(L, j - 1))
                    act.activation(wk[:, j % 2], X[:, j], ACT.Square).then_inc(sq_done.sem, 1)
                act.wait_ge(*sq_used.upto(L, KT))
                act_step.step(act, act.activation(wk[:, 2], psT[:, 0], ACT.Ln, bias=epsc[:, 0:1],
                                                  scale=1.0 / D_MODEL))
                act.activation(wk[:, 2], wk[:, 2], ACT.Exp, scale=-0.5).then_inc(rstd.sem, 1)
                for j in range(KT):
                    act.wait_ge(*h_scaled.upto(L, j + 1))
                    act.activation(Hhi[:, j], X[:, j], ACT.Copy).then_inc(h_hi.sem, 1)
                act.wait_ge(*h_lo.upto(L, KT))
                act.wait_ge(*lam_sum.upto(L, 1))
                act.activation(lam[:, 2:4], lam[:, 0:2], ACT.Exp).then_inc(lam_exp.sem, 1)
                for h in range(HEADS):
                    take(L, ("aq", h), RAWQ)
                    take(L, ("ak", h), RAWK)
                    take(L, ("av", h), RAWV)
                    take(L, ("az", h), Z, ACT.Silu)
                    attend(L, h)
                act.wait_ge(*rotated.upto(L, 2 * HEADS))
                act.dma_start(rope[:], env.ropes[1]).then_inc(rope_in.sem, 16)
                gates(L, 0)
                for c in range(B1_TILES):
                    if c:
                        act.wait_ge(*A.drained(L, ("cc", c - 1)))
                    take(L, ("cx", c), wk[:, 4])
                    if c:
                        act.wait_ge(*c_out.upto(L, c))
                    take(L, ("cb", c), wk[:, 5])
                    take(L, ("cz", c), wk[:, 6], ACT.Silu)
                    act.wait_ge(*c_out.upto(L, c + 1))
                    act.activation(Bhi[:, c], wk[:, 7], ACT.Copy).then_inc(b_hi.sem, 1)
                gates(L, 1)
                act.wait_ge(*merged.upto(L, KT))
                for pr in range(HEADS // 2):
                    take(L, ("rq", pr), R_RAWQ)
                    take(L, ("rk", pr), R_RAWK)
                    for h in (2 * pr, 2 * pr + 1):
                        take(L, ("rv", h), R_RAWV)
                        if h:
                            act.wait_ge(*r_out.upto(L, h))
                        take(L, ("rz", h), Z, ACT.Silu)
                        if h % 2 == 0:
                            act.wait_ge(*T.filled(L, ("ks", pr)))
                            act.activation(KS, psT[:, T.buf(("ks", pr))], ACT.Copy).then_inc(T.freed(("ks", pr)), 1)
                        use = ("ro", h)
                        act.wait_ge(*A.filled(L, use))
                        if h:
                            act.wait_ge(*b_lo.upto(L, 12 + h))
                        act.activation(RSQ, psA[:, A.buf(use)], ACT.Square).then_inc(r_sq.sem, 1)
                        root(L, ("rss", h), RSQ, 1.0 / P, r_rs.sem)
                        act.wait_ge(*r_out.upto(L, h + 1))
                        act.activation(Bhi[:, h], RSQ, ACT.Copy).then_inc(b_hi.sem, 1)
                gates(L, 2)
                for j in range(KT):
                    act.wait_ge(*merged.upto(L, KT + j + 1))
                    if j == 0:
                        act.wait_ge(*A.filled(L, ("gate", 2, 0), KT - 1))
                    act.activation(Hhi[:, j], X[:, j], ACT.Copy).then_inc(m_hi.sem, 1)
                with act.Fori(0, KT // 2) as jj:
                    for b in (0, 1):
                        act.wait_ge(*x_ready.upto(L + 1, jj * 2 + b - 1))
                        act.dma_start(wk[:, 4 + b], tile_of(xs_v, jj * 2 + b)).then_inc(x_back[b].sem, 16)

            act.wait_ge(*x_ready.upto(DEPTH, KT))
            for j in range(KT):
                if j >= 2:
                    act.wait_ge(f_used, j - 1)
                act.activation(wk[:, j % 2], X[:, j], ACT.Square).then_inc(f_sq, 1)
            act.wait_ge(f_used, KT)
            act.activation(wk[:, 2], psT[:, 0], ACT.Ln, bias=epsc[:, 0:1], scale=1.0 / D_MODEL).then_inc(f_sum, 1)
            act.wait_ge(f_sum, 1)
            act.activation(wk[:, 2], wk[:, 2], ACT.Exp, scale=-0.5).then_inc(f_rs, 1)

        @block.vector
        def _(dve):
            def step(ins):
                dve_step.step(dve, ins)

            def rotate(L, use, raw, raw_tile, dst, done):
                dve.wait_ge(*A.drained(L, raw))
                step(dve.tensor_tensor(dst, raw_tile, rope[:, 0], ALU.mult))
                dve.wait_ge(*T.filled(L, use))
                dve.tensor_tensor(ROT, psT[:, T.buf(use)], rope[:, 1], ALU.mult).then_inc(T.freed(use), 1)
                dve.wait_ge(*T.drained(L, use))
                dve.tensor_tensor(dst, dst, ROT, ALU.add).then_inc(done, 1)

            def maxima(L, h, q):
                n = (q + 1) * P
                for c in (0, 1):
                    use = ("s", h, q, c)
                    dve.wait_ge(*A.filled(L, use))
                    step(dve.reduce_max(rowmax[:, c:c + 1], psA[:, A.buf(use), 0:n], AX_X))
                dve.tensor_scalar(negmax[:, q % 2], rowmax[:], -SCALE, None, ALU.mult).then_inc(nmax.sem, 1)

            def mix(L, h, q):
                n = (q + 1) * P
                p0, p1 = PR[q % 2][0][:, 0:n], PR[q % 2][1][:, 0:n]
                dve.wait_ge(*A.drained(L, ("s", h, q, 0)))
                dve.wait_ge(*A.drained(L, ("s", h, q, 1)))
                step(dve.reciprocal(inv[:, q % 2], rowsum[:, q % 2]))
                step(dve.tensor_scalar(p1, p1, inv[:, q % 2, 1:2], lam[:, 4:5], ALU.mult, ALU.mult))
                dve.scalar_tensor_tensor(out=p0, in0=p0, scalar=inv[:, q % 2, 0:1], in1=p1, op0=ALU.mult, op1=ALU.add)\
                    .then_inc(mixed.sem, 1)

            def attend(L, h):
                maxima(L, h, 0)
                for q in range(NT):
                    if q + 1 < NT:
                        maxima(L, h, q + 1)
                    mix(L, h, q)
                    if q % 4 == 3:
                        g = q // 4
                        n = 2 * h + g
                        half = slice(g * HALF, (g + 1) * HALF)
                        use = ("av", h, g)
                        dve.wait_ge(*a_rs.upto(L, n + 1))
                        dve.scalar_tensor_tensor(out=TMP[:, HALF:], in0=psT[:, T.buf(use), 0:HALF],
                                                 scalar=gcol[:, 0:1], in1=TMP[:, 0:HALF], op0=ALU.mult,
                                                 op1=ALU.mult).then_inc(T.freed(use), 1)
                        dve.wait_ge(*T.drained(L, use))
                        dve.wait_ge(*A.drained(L, ("az", h)))
                        dve.tensor_tensor(TMP[:, HALF:], TMP[:, HALF:], Z[:, half], ALU.mult)\
                            .then_inc(a_out.sem, 1)
                        dve.wait_ge(*b_hi.upto(L, n + 1))
                        dve.tensor_tensor(Blo[:, h, half], TMP[:, HALF:], Bhi[:, h, half].bitcast(F32),
                                          ALU.subtract).then_inc(b_lo.sem, 1)

            def merge(L, i):
                with dve.Fori(0, KT // 2) as jj:
                    if i == 2:
                        dve.wait_ge(*merged.upto(L, KT))
                    for b in (0, 1):
                        use, j = ("branch", i, b), jj * 2 + b
                        dve.wait_ge(*A.filled(L, use, jj * 2))
                        dve.wait_ge(*A.drained(L, ("gate", i, b), jj * 2))
                        if i == 0:
                            dve.tensor_tensor(tile_of(X, j), wk[:, b], psA[:, A.buf(use)], ALU.mult)\
                                .then_inc(A.freed(use), 1)
                        else:
                            dve.tensor_tensor(wk[:, 2 + b], wk[:, b], psA[:, A.buf(use)], ALU.mult)\
                                .then_inc(A.freed(use), 1)
                            dve.wait_ge(*A.drained(L, use, jj * 2))
                            dve.tensor_tensor(tile_of(X, j), tile_of(X, j), wk[:, 2 + b], ALU.add)\
                                .then_inc(merged.sem, 1)

            def retain(L, pr, h):
                rows = head_rows(h)
                use = ("rvt", h)
                dve.wait_ge(*T.filled(L, use))
                dve.tensor_copy(V, psT[:, T.buf(use)]).then_inc(T.freed(use), 1)
                use = ("rs", h)
                dve.wait_ge(*A.filled(L, use))
                dve.tensor_tensor(by_chunk(SM), by_chunk(psA[:, A.buf(use)]), every_chunk(DM[:, h]), ALU.mult)\
                    .then_inc(A.freed(use), 1)
                use = ("kv", h)
                kv = psT[:, T.buf(use)]
                dve.wait_ge(*T.filled(L, use))
                step(dve.tensor_copy(ST[rows, P:2 * P], kv[rows, 0:P]))
                for n in range(1, NT - 1):
                    ins = dve.scalar_tensor_tensor(out=ST[rows, (n + 1) * P:(n + 2) * P],
                                                   in0=ST[rows, n * P:(n + 1) * P], scalar=DEC[rows, pr:pr + 1],
                                                   in1=kv[rows, n * P:(n + 1) * P], op0=ALU.mult, op1=ALU.add)
                    if n < NT - 2:
                        step(ins)
                    else:
                        ins.then_inc(T.freed(use), 1)
                use = ("ro", h)
                dve.wait_ge(*r_rs.upto(L, h + 1))
                dve.tensor_tensor(RSQ, psA[:, A.buf(use)], RSQ, ALU.mult).then_inc(A.freed(use), 1)
                dve.wait_ge(*A.drained(L, use))
                dve.wait_ge(*A.drained(L, ("rz", h)))
                dve.tensor_tensor(RSQ, RSQ, Z, ALU.mult).then_inc(r_out.sem, 1)
                dve.wait_ge(*b_hi.upto(L, 12 + h + 1))
                dve.tensor_tensor(Blo[:, h], RSQ, Bhi[:, h].bitcast(F32), ALU.subtract).then_inc(b_lo.sem, 1)

            dve.memset(upad[:, 0:2], 0.0).then_inc(dve_step.sem, 1)
            dve.memset(epsc[:], EPS).then_inc(dve_step.sem, 1)
            dve.wait_ge(consts_in, 64)
            dve.wait_ge(mask_in, 16)
            dve.wait_ge(dve_step.sem, 2)
            for t in range(NT):
                dve.wait_ge(x_turned, t + 1)
                dve.tensor_copy(X[:, :, t * P:(t + 1) * P], by_chunk(psA[:, t % 2])).then_inc(x_ready.sem, 1)
                if t == 0:
                    dve.tensor_copy(maskb[:], wk[:, 0, 0:P])
                    dve.tensor_copy(identb[:], ident[:]).then_inc(setup, 1)
            dve.wait_ge(params_in, 64)
            with dve.Fori(0, DEPTH) as L:
                dve_step.layer(L)
                step(dve.tensor_copy(cur[:], par[:, bass.ds(L, 1), :].rearrange("p a c -> p (a c)")))
                raw = lamraw[:, bass.ds(L, 1), :].rearrange("p a (m two c) -> p (a m) two c", m=2, two=2)
                step(dve.tensor_tensor(lamt[:].rearrange("p (m c) -> p m c", m=2), raw[:, :, 0], raw[:, :, 1],
                                       ALU.mult))
                dve.reduce_sum(lam[:, 0:2], lamt[:].rearrange("p (m c) -> p m c", m=2), AX_X)\
                    .then_inc(lam_sum.sem, 1)
                step(dve.tensor_tensor(gcol[:], cur[:, C1.subln:C1.subln + 1],
                                       cur[:, C1.lam_rest:C1.lam_rest + 1], ALU.mult))
                dve.wait_ge(*rstd.upto(L, 1))
                dve.wait_ge(*x_saved.upto(L, 16))
                for j in range(KT + 1):
                    if j < KT:
                        dve.scalar_tensor_tensor(out=X[:, j], in0=X[:, j], scalar=cur[:, C1.norm + j:C1.norm + j + 1],
                                                 in1=wk[:, 2], op0=ALU.mult, op1=ALU.mult).then_inc(h_scaled.sem, 1)
                    if j:
                        dve.wait_ge(*h_hi.upto(L, j))
                        dve.tensor_tensor(Hlo[:, j - 1], X[:, j - 1], Hhi[:, j - 1].bitcast(F32), ALU.subtract)\
                            .then_inc(h_lo.sem, 1)
                dve.wait_ge(*lam_exp.upto(L, 1))
                step(dve.tensor_tensor(lam[:, 5:6], lam[:, 3:4], lam[:, 2:3], ALU.subtract))
                step(dve.tensor_tensor(lam[:, 4:5], lam[:, 5:6], cur[:, C1.lam_init:C1.lam_init + 1],
                                       ALU.subtract))
                dve.wait_ge(*rope_in.upto(L, 16))
                for h in range(HEADS):
                    rotate(L, ("swapq", h), ("aq", h), RAWQ, Q, rotated.sem)
                    rotate(L, ("swapk", h), ("ak", h), RAWK, KK, rotated.sem)
                    dve.wait_ge(*T.filled(L, ("vt", h)))
                    dve.tensor_copy(V, psT[:, T.buf(("vt", h))]).then_inc(T.freed(("vt", h)), 1)
                    attend(L, h)
                merge(L, 0)
                for c in range(B1_TILES):
                    dve.wait_ge(*A.filled(L, ("cc", c)))
                    dve.wait_ge(*A.drained(L, ("cx", c)))
                    dve.tensor_tensor(upad[:, 2:], psA[:, A.buf(("cc", c))], wk[:, 4], ALU.mult)\
                        .then_inc(A.freed(("cc", c)), 1)
                    dve.wait_ge(*A.drained(L, ("cc", c)))
                    for k in range(3):
                        w = cur[:, C1.conv + 4 * k + c:C1.conv + 4 * k + c + 1]
                        if k == 0:
                            step(dve.tensor_scalar(wk[:, 7], upad[:, 0:SEQ], w, None, ALU.mult))
                        else:
                            step(dve.scalar_tensor_tensor(out=wk[:, 7], in0=upad[:, k:k + SEQ], scalar=w,
                                                          in1=wk[:, 7], op0=ALU.mult, op1=ALU.add))
                    dve.wait_ge(*A.drained(L, ("cb", c)))
                    step(dve.tensor_tensor(wk[:, 7], wk[:, 7], wk[:, 5], ALU.mult))
                    dve.wait_ge(*A.drained(L, ("cz", c)))
                    dve.tensor_tensor(wk[:, 7], wk[:, 7], wk[:, 6], ALU.mult).then_inc(c_out.sem, 1)
                    dve.wait_ge(*b_hi.upto(L, 8 + c + 1))
                    dve.tensor_tensor(Blo[:, c], wk[:, 7], Bhi[:, c].bitcast(F32), ALU.subtract)\
                        .then_inc(b_lo.sem, 1)
                merge(L, 1)
                dve.wait_ge(*rope_in.upto(L, 32))
                for pr in range(HEADS // 2):
                    rotate(L, ("swaprq", pr), ("rq", pr), R_RAWQ, Q, r_rot.sem)
                    rotate(L, ("swaprk", pr), ("rk", pr), R_RAWK, KK, r_rot.sem)
                    dve.wait_ge(*r_rot.upto(L, 2 * pr + 2))
                    step(dve.tensor_tensor(by_chunk(QX), by_chunk(Q), every_chunk(XI[:, pr]), ALU.mult))
                    dve.tensor_tensor(by_chunk(KZ), by_chunk(KK), every_chunk(ZE[:, pr]), ALU.mult)\
                        .then_inc(rk_scaled.sem, 1)
                    for h in (2 * pr, 2 * pr + 1):
                        retain(L, pr, h)
                merge(L, 2)
                for j in range(KT):
                    dve.wait_ge(*m_hi.upto(L, j + 1))
                    dve.tensor_tensor(Hlo[:, j], X[:, j], Hhi[:, j].bitcast(F32), ALU.subtract)\
                        .then_inc(m_lo.sem, 1)
                with dve.Fori(0, KT // 2) as jj:
                    for b in (0, 1):
                        dve.wait_ge(*out_filled.upto(L, jj * 2 + b + 1))
                        dve.wait_ge(*x_back[b].upto(L, jj * 16 + 16))
                        dve.tensor_tensor(tile_of(X, jj * 2 + b), psA[:, b], wk[:, 4 + b], ALU.add)\
                            .then_inc(x_ready.sem, 1)
            counts["d1"] = dve_step.k
            dve.wait_ge(f_rs, 1)
            dve.wait_ge(*x_ready.upto(DEPTH, KT))
            for j in range(KT):
                dve.scalar_tensor_tensor(out=X[:, j], in0=X[:, j], scalar=fing[:, j:j + 1], in1=wk[:, 2],
                                         op0=ALU.mult, op1=ALU.mult).then_inc(x_ready.sem, 1)
            dve.wait_ge(x_ready.sem, (DEPTH + 2) * KT)


def second_block(env, per, counts):
    nc, X, Hhi, Hlo, rope, ident, ones = env.nc, env.X, env.Hhi, env.Hlo, env.rope, env.ident, env.ones
    psA, psT, identb, maskb, epsc = env.psA, env.psT, env.identb, env.maskb, env.epsc
    SCALE = M_QK ** -0.5
    with ExitStack() as ctx:
        def sem(name):
            return ctx.enter_context(nc.semaphore("b2_" + name))

        def sb(name, shape, dt=F32):
            return ctx.enter_context(nc.sbuf_tensor("b2_" + name, shape, dt))

        wk = sb("wk", [P, 14, SEQ])
        ypad = sb("ypad", [P, 2, SEQ + PAD])
        par = sb("par", [P, DEPTH, C2.n])
        cur = sb("cur", [P, C2.n])
        pww = sb("pww", [P, 4 * P])
        sgw = sb("sgw", [P, 4, P])
        sgb = sb("sgb", [P, 2, P])
        swapm = sb("swapm", [P, M_ROPE])
        causal = sb("causal", [P, P])
        rowmax = sb("rowmax", [P, 2])
        negmax = sb("negmax", [P, 2])
        rowsum = sb("rowsum", [P, 2])
        inv = sb("inv", [P, 2])
        credit = sb("credit", [P, 2])

        a_uses, t_uses = uses_of_block2()
        A = Ring("b2A", a_uses, lambda n: ctx.enter_context(nc.semaphore(n)))
        T = Ring("b2T", t_uses, lambda n: ctx.enter_context(nc.semaphore(n)))
        NP = len(P2)
        s = Group()
        s.credit, s.w_split, s.w_hi, s.panel_begun = credit, sem("w_split"), sem("w_hi"), sem("panel_begun")
        s.w_loaded = [sem("w_loaded0"), sem("w_loaded1")]
        params_in = sem("params_in")
        layer_in = Tally(sem("layer_in"), 4 * 16)
        x_ready = Tally(sem("x_ready"), KT)
        out_filled = Tally(sem("out_filled"), KT)
        x_saved = Tally(sem("x_saved"), 16)
        x_back = [Tally(sem(f"x_back{b}"), 16 * KT // 2) for b in (0, 1)]
        sq_done, sq_used = Tally(sem("sq_done"), KT), Tally(sem("sq_used"), KT)
        rstd = Tally(sem("rstd"), 1)
        h_scaled, h_hi, h_lo = (Tally(sem(n), KT) for n in ("h_scaled", "h_hi", "h_lo"))
        conv_done = Tally(sem("conv_done"), 2)
        uz_done = Tally(sem("uz_done"), 2)
        l_sq, l_used = Tally(sem("l_sq"), KT), Tally(sem("l_used"), KT - 2)
        l_rs = Tally(sem("l_rs"), 2)
        l_scaled, l_hi, l_lo = (Tally(sem(n), KT) for n in ("l_scaled", "l_hi", "l_lo"))
        sq2 = Tally(sem("sq2"), 4)
        roots = Tally(sem("roots"), 4)
        normed = Tally(sem("normed"), 4)
        c_act, s_act = Tally(sem("c_act"), 2), Tally(sem("s_act"), 2)
        s_out = Tally(sem("s_out"), 2)
        c_fin, s_fin = Tally(sem("c_fin"), 2), Tally(sem("s_fin"), 2)
        kr_sq, kr_g, kr_rot = Tally(sem("kr_sq"), 1), Tally(sem("kr_g"), 1), Tally(sem("kr_rot"), 1)
        q_sq, k_sq, q_rs, k_rs = (Tally(sem(n), M_HEADS) for n in ("q_sq", "k_sq", "q_rs", "k_rs"))
        q_rot = Tally(sem("q_rot"), M_HEADS)
        nmax, mixed = Tally(sem("nmax"), M_HEADS * NT), Tally(sem("mixed"), M_HEADS * NT)
        m_sq, m_used, m_rs, m_fin = Tally(sem("m_sq"), 4), Tally(sem("m_used"), 3), Tally(sem("m_rs"), 1), \
            Tally(sem("m_fin"), 4)
        y_hi, y_lo = Tally(sem("y_hi"), KT), Tally(sem("y_lo"), KT)
        turned, copied, written = sem("turned"), sem("copied"), [sem("written0"), sem("written1")]
        dve_step = Chain(sem("dve_step"), per.get("d2", 1), 2)
        act_step = Chain(sem("act_step"), 1)

        ZM, ZC, UZ, YC, VG = (wk[:, a:b] for a, b in ((0, 4), (4, 6), (6, 8), (8, 10), (10, 12)))
        KR, SQK = wk[:, 12], wk[:, 13]
        ZS = [wk[:, 13], ypad[:, 1, PAD:]]
        LSQ, LROOT = [wk[:, 13], ypad[:, 0, PAD:]], ypad[:, 1, PAD:]
        S2, SROOT = [X[:, 2], X[:, 3]], X[:, 4]
        WG = wk[:, 9, 0:4 * P]
        Q, KK, PR, QROOT, ROT, RAWV, KROOT = wk[:, 4], wk[:, 5], [wk[:, 6], wk[:, 7]], wk[:, 8], wk[:, 9], \
            wk[:, 10], wk[:, 11]
        V = ypad[:, 0, PAD:PAD + HALF]
        WT = X[:, 2:6].rearrange("p a b -> p (a b)").rearrange("p (k q) -> p k q", k=NT)
        NOPE, ROPE, QK = slice(0, M_NOPE), slice(M_NOPE, M_QK), slice(0, M_QK)
        xs_v = env.xs.rearrange("j p n -> p j n")

        def by_chunk(ap):
            return ap.rearrange("p (n c) -> p n c", n=NT)

        def every_chunk(ap):
            return ap.unsqueeze(1).broadcast_to([ap.shape[0], NT, ap.shape[1]])

        def tile_of(ap, j):
            return ap[:, bass.ds(j, 1), :].rearrange("p a b -> p (a b)")

        def col(k):
            return cur[:, k:k + 1]

        def head_rows(h):
            return slice((h % 2) * M_V, (h % 2 + 1) * M_V)

        block = ctx.enter_context(nc.Block())

        def load_inputs(sp):
            sp.dma_start(par[:], env.par2.rearrange("l p c -> p l c")).then_inc(params_in, 16)
            sp.dma_start(swapm[:], env.consts[:, K.swapm:K.swapm + M_ROPE]).then_inc(params_in, 16)
            sp.dma_start(causal[:], env.consts[:, K.causal:K.causal + P]).then_inc(params_in, 16)
            sp.dma_start(rope[:], env.ropes[2]).then_inc(params_in, 16)

        weight_engines(block, s, env.w2, env.stage, env.Whi, env.Wlo, P2, RUNS2, load_inputs)

        @block.tensor
        def _(pe):
            def panel(L, name, nk=KT, M=P, j=0, tiles=None, dst=None, done=None, first=True, last=True):
                p = PAN2[name]
                pe.wait_ge(s.w_split, L * NP + p + 3 + j * 2)
                if dst is None:
                    if A.before(name):
                        pe.wait_ge(*A.room(L, name, j))
                    dst, done = psA[:, A.buf(name)], A.filled_sem
                tiles = tiles or range(nk)
                mm = three_pass(pe, dst, env.Whi[:, p % 2], env.Wlo[:, p % 2], [Hhi[:, k] for k in tiles],
                                [Hlo[:, k] for k in tiles], nk, M, s.panel_begun, first, last)
                if done is not None:
                    mm.then_inc(done, 1)

            def full(dst, lhsT, rhs, start=True, stop=True):
                for h in (0, 1):
                    c = slice(h * HALF, (h + 1) * HALF)
                    mm = pe.matmul(dst[:, c], lhsT, rhs[:, c], start=start, stop=stop)
                return mm

            def turn(dst, src, blocks):
                for i in range(blocks):
                    mm = pe.transpose(dst[:, i * P:(i + 1) * P], src[:, i * P:(i + 1) * P], ident[:])
                return mm

            def pair_sum(L, use, tiles):
                pe.wait_ge(*T.room(L, use))
                full(psT[:, T.buf(use)], ones[:], tiles[0], True, False)
                full(psT[:, T.buf(use)], ones[:], tiles[1], False, True).then_inc(T.filled_sem, 1)

            def latent(L, use, first, n):
                pe.wait_ge(*T.room(L, use))
                for j in range(first, first + n):
                    pe.wait_ge(*l_sq.upto(L, j + 1))
                    mm = full(psT[:, T.buf(use)], ones[:], LSQ[j % 2], j == first, j == first + n - 1)
                    mm.then_inc(l_used.sem if j < first + n - 1 else T.filled_sem, 1)

            def scores(L, h, q):
                use = ("s", h, q)
                pe.wait_ge(*A.room(L, use))
                if q == 0:
                    pe.wait_ge(*q_rot.upto(L, h + 1))
                dst, n = psA[:, A.buf(use)], (q + 1) * P
                for k0 in range(0, n, HALF):
                    k1 = min(n, k0 + HALF)
                    pe.matmul(dst[:, k0:k1], Q[QK, q * P:n], KK[QK, k0:k1], start=True, stop=k1 < n)
                pe.matmul(dst[:, q * P:n], identb[:], maskb[:], start=False, stop=True).then_inc(A.filled_sem, 1)

            def attend(L, h):
                rows = head_rows(h)
                scores(L, h, 0)
                for q in range(NT):
                    if q + 1 < NT:
                        scores(L, h, q + 1)
                    use = ("pt", h, q)
                    pe.wait_ge(*T.room(L, use))
                    pe.wait_ge(*mixed.upto(L, h * NT + q + 1))
                    turn(psT[:, T.buf(use)], PR[q % 2], q + 1).then_inc(T.filled_sem, 1)
                    if q % 4 == 3:
                        g = q // 4
                        use = ("av", h, g)
                        pe.wait_ge(*T.drained(L, ("pt", h, q)))
                        pe.wait_ge(*T.room(L, use))
                        for k in range(q + 1):
                            c0 = max(0, k - 4 * g) * P
                            mm = pe.matmul(psT[rows, T.buf(use), c0:HALF], V[:, k * M_V:(k + 1) * M_V],
                                           WT[:, k, c0:], start=k == 0, stop=k == q)
                        mm.then_inc(T.filled_sem, 1)

            with pe.Fori(0, DEPTH) as L:
                for j in range(KT):
                    pe.wait_ge(*sq_done.upto(L, j + 1))
                    full(psT[:, 0], ones[:], wk[:, j % 2], j == 0, j == KT - 1).then_inc(sq_used.sem, 1)
                pe.wait_ge(*h_hi.upto(L, KT))
                pe.wait_ge(*h_lo.upto(L, KT))
                for name, nk, M in P2[:PAN2[("kr", 0)]]:
                    panel(L, name)
                panel(L, ("kr", 0), KT // 2, M_QK, dst=psT[:, T.buf("kr")], last=False)
                panel(L, ("kr", 1), KT // 2, M_QK, tiles=range(KT // 2, KT), dst=psT[:, T.buf("kr")],
                      done=T.filled_sem, first=False)
                for name, nk, M in P2[PAN2[("zm", 0)]:PAN2[("q", 0)]]:
                    panel(L, name)
                latent(L, "cqs", 0, Q_LORA_T)
                latent(L, "ckvs", Q_LORA_T, KV_LORA_T)
                pe.wait_ge(*conv_done.upto(L, 2))
                pair_sum(L, "cmean", [YC[:, 0], YC[:, 1]])
                pe.wait_ge(*sq2.upto(L, 1))
                pair_sum(L, "cvar", S2)
                pe.wait_ge(*c_act.upto(L, 2))
                pe.wait_ge(*layer_in.upto(L, 64))
                for m in (0, 1):
                    pe.wait_ge(*A.room(L, ("pw", m)))
                    for k in (0, 1):
                        mm = full(psA[:, A.buf(("pw", m))], pww[:, k * 2 * P + m * P:k * 2 * P + (m + 1) * P],
                                  YC[:, k], k == 0, k == 1)
                    mm.then_inc(A.filled_sem, 1)
                pe.wait_ge(*sq2.upto(L, 2))
                pair_sum(L, "cbn", S2)
                pair_sum(L, "smean", [VG[:, 0], VG[:, 1]])
                pe.wait_ge(*sq2.upto(L, 3))
                pair_sum(L, "svar", S2)
                for t in (0, 1):
                    pe.wait_ge(*s_act.upto(L, t + 1))
                    pe.wait_ge(*T.room(L, ("vst", t)))
                    turn(psT[:, T.buf(("vst", t))], VG[:, t], NT).then_inc(T.filled_sem, 1)
                pe.wait_ge(*T.room(L, "wgt"))
                for g in range(4):
                    mm = pe.transpose(psT[:, T.buf("wgt"), g * P:(g + 1) * P], sgw[:, g], ident[:])
                mm.then_inc(T.filled_sem, 1)
                pe.wait_ge(*T.drained(L, "wgt"))
                for t in (0, 1):
                    pe.wait_ge(*T.drained(L, ("vst", t)))
                    pe.wait_ge(*A.room(L, ("sg", t)))
                    for n in range(NT):
                        for g in (0, 1):
                            mm = pe.matmul(psA[g * 64:(g + 1) * 64, A.buf(("sg", t)), n * P:(n + 1) * P],
                                           VG[:, t, n * P + g * 64:n * P + (g + 1) * 64],
                                           WG[:, (2 * t + g) * P:(2 * t + g + 1) * P], start=True, stop=True)
                    mm.then_inc(A.filled_sem, 1)
                pe.wait_ge(*sq2.upto(L, 4))
                pair_sum(L, "sbn", S2)
                pe.wait_ge(*kr_g.upto(L, 1))
                pe.wait_ge(*T.room(L, "krswap"))
                full(psT[ROPE, T.buf("krswap")], swapm[QK, :], KR[QK]).then_inc(T.filled_sem, 1)
                pe.wait_ge(*l_lo.upto(L, KT))
                pe.wait_ge(*l_hi.upto(L, KT))
                for h in range(M_HEADS):
                    panel(L, ("q", h), Q_LORA_T, M_QK)
                    panel(L, ("kv", h), KV_LORA_T, P, tiles=range(Q_LORA_T, KT))
                    use = ("qs", h)
                    pe.wait_ge(*q_sq.upto(L, h + 1))
                    pe.wait_ge(*T.room(L, use))
                    full(psT[QK, T.buf(use)], ones[QK, QK], QROOT[QK]).then_inc(T.filled_sem, 1)
                    use = ("ks", h)
                    pe.wait_ge(*k_sq.upto(L, h + 1))
                    pe.wait_ge(*T.room(L, use))
                    full(psT[QK, T.buf(use)], ones[QK, QK], SQK[QK]).then_inc(T.filled_sem, 1)
                    use = ("vt", h)
                    pe.wait_ge(*T.room(L, use))
                    for n in range(NT):
                        dst, src = psT[:, T.buf(use), n * M_V:(n + 1) * M_V], RAWV[M_NOPE:P, n * P:(n + 1) * P]
                        if n == 0:
                            pe.matmul(dst, src, ident[M_NOPE:P, M_NOPE:P], start=True, stop=True)
                        else:
                            mm = pe.transpose(dst, src, ident[M_NOPE:P, M_NOPE:P])
                    mm.then_inc(T.filled_sem, 1)
                    use = ("qswap", h)
                    pe.wait_ge(*A.drained(L, ("q", h)))
                    pe.wait_ge(*T.room(L, use))
                    full(psT[ROPE, T.buf(use)], swapm[QK, :], Q[QK]).then_inc(T.filled_sem, 1)
                    attend(L, h)
                pe.wait_ge(*T.room(L, "mbn"))
                for t in range(4):
                    pe.wait_ge(*m_sq.upto(L, t + 1))
                    full(psT[:, T.buf("mbn")], ones[:], PR[t % 2], t == 0, t == 3)\
                        .then_inc(m_used.sem if t < 3 else T.filled_sem, 1)
                with pe.Fori(0, KT // 2) as jj:
                    pe.wait_ge(*y_hi.upto(L, KT))
                    pe.wait_ge(*y_lo.upto(L, KT))
                    for b in (0, 1):
                        pe.wait_ge(*x_ready.upto(L + 1, jj * 2 + b - 1))
                        panel(L, ("out", b), j=jj, dst=psA[:, b], done=out_filled.sem)

            pe.wait_ge(*x_ready.upto(DEPTH, KT))
            for t in range(NT):
                if t >= 2:
                    pe.wait_ge(copied, t - 1)
                for j in range(KT):
                    mm = pe.transpose(psA[:, t % 2, j * P:(j + 1) * P], X[:, j, t * P:(t + 1) * P], ident[:])
                mm.then_inc(turned, 1)

        @block.scalar
        def _(act):
            def root(L, use, dst, mean, done, rows=slice(0, P)):
                act.wait_ge(*T.filled(L, use))
                act.activation(dst[rows], psT[rows, T.buf(use)], ACT.Ln, bias=epsc[rows, 0:1], scale=mean)\
                    .then_inc(T.freed(use), 1)
                act.wait_ge(*T.drained(L, use))
                act.activation(dst[rows], dst[rows], ACT.Exp, scale=-0.5).then_inc(done, 1)

            def take(L, use, dst, func=ACT.Copy):
                act.wait_ge(*A.filled(L, use))
                act.activation(dst, psA[:, A.buf(use)], func).then_inc(A.freed(use), 1)

            def squares(tiles):
                act.activation(S2[0], tiles[0], ACT.Square)
                act.activation(S2[1], tiles[1], ACT.Square).then_inc(sq2.sem, 1)

            def exps(L, h, q):
                use, n = ("s", h, q), (q + 1) * P
                act.wait_ge(*nmax.upto(L, h * NT + q + 1))
                act.activation(PR[q % 2][:, 0:n], psA[:, A.buf(use), 0:n], ACT.Exp, bias=negmax[:, q % 2:q % 2 + 1],
                               scale=SCALE, accum_out=rowsum[:, q % 2:q % 2 + 1]).then_inc(A.freed(use), 1)

            with act.Fori(0, DEPTH) as L:
                act_step.layer(L)
                act.wait_ge(*x_ready.upto(L, KT))
                act.dma_start(xs_v, X[:]).then_inc(x_saved.sem, 16)
                act.dma_start(pww[:], env.pww[L]).then_inc(layer_in.sem, 16)
                act.dma_start(sgw[:], env.sgw[L]).then_inc(layer_in.sem, 16)
                for b in (0, 1):
                    src = env.sgb[L].rearrange("(two b) t -> b two t", b=2)[b]
                    act.dma_start(sgb[b * 64:(b + 1) * 64], src.partition_broadcast(64)).then_inc(layer_in.sem, 16)
                for j in range(KT):
                    if j >= 2:
                        act.wait_ge(*sq_used.upto(L, j - 1))
                    act.activation(wk[:, j % 2], X[:, j], ACT.Square).then_inc(sq_done.sem, 1)
                act.wait_ge(*sq_used.upto(L, KT))
                act_step.step(act, act.activation(wk[:, 2], psT[:, 0], ACT.Ln, bias=epsc[:, 0:1],
                                                  scale=1.0 / D_MODEL))
                act.activation(wk[:, 2], wk[:, 2], ACT.Exp, scale=-0.5).then_inc(rstd.sem, 1)
                for j in range(KT):
                    act.wait_ge(*h_scaled.upto(L, j + 1))
                    act.activation(Hhi[:, j], X[:, j], ACT.Copy).then_inc(h_hi.sem, 1)
                act.wait_ge(*h_lo.upto(L, KT))
                for t in (0, 1):
                    take(L, ("g", t), VG[:, t], ACT.Sigmoid)
                for t in (0, 1):
                    take(L, ("zc", t), ZC[:, t], ACT.Silu)
                for t in range(Q_LORA_T):
                    take(L, ("cq", t), X[:, t])
                for t in range(KV_LORA_T):
                    take(L, ("ckv", t), X[:, Q_LORA_T + t])
                act.wait_ge(*T.filled(L, "kr"))
                act.activation(KR[ROPE], psT[ROPE, T.buf("kr")], ACT.Copy).then_inc(T.freed("kr"), 1)
                for t in range(4):
                    take(L, ("zm", t), ZM[:, t], ACT.Silu)
                for t in (0, 1):
                    act.wait_ge(*A.drained(L, ("a", t)))
                    take(L, ("v", t), VG[:, t], ACT.Gelu_apprx_tanh)
                for t in (0, 1):
                    take(L, ("u", t), UZ[:, t], ACT.Gelu_apprx_tanh)
                act.wait_ge(*conv_done.upto(L, 2))
                for t in (0, 1):
                    take(L, ("zs", t), ZS[t], ACT.Silu)
                act.wait_ge(*uz_done.upto(L, 2))
                for j in range(KT):
                    if j >= 2 and j != Q_LORA_T + 1:
                        act.wait_ge(*(T.filled(L, "cqs") if j >= Q_LORA_T else l_used.upto(L, j - 1)))
                    act.activation(LSQ[j % 2], X[:, j], ACT.Square).then_inc(l_sq.sem, 1)
                    if j == Q_LORA_T - 1:
                        root(L, "cqs", LROOT, 1.0 / (Q_LORA_T * P), l_rs.sem)
                for j in range(Q_LORA_T):
                    act.wait_ge(*l_scaled.upto(L, j + 1))
                    act.activation(Hhi[:, j], X[:, j], ACT.Copy).then_inc(l_hi.sem, 1)
                root(L, "ckvs", LROOT, 1.0 / (KV_LORA_T * P), l_rs.sem)
                for j in range(Q_LORA_T, KT):
                    act.wait_ge(*l_scaled.upto(L, j + 1))
                    act.activation(Hhi[:, j], X[:, j], ACT.Copy).then_inc(l_hi.sem, 1)
                act.wait_ge(*l_lo.upto(L, KT))
                act.wait_ge(*T.drained(L, "cmean"))
                squares([YC[:, 0], YC[:, 1]])
                root(L, "cvar", SROOT, 1.0 / 256, roots.sem)
                for t in (0, 1):
                    act.wait_ge(*normed.upto(L, t + 1))
                    act.activation(YC[:, t], YC[:, t], ACT.Silu, bias=col(C2.cln_b + t)).then_inc(c_act.sem, 1)
                act.wait_ge(*A.drained(L, ("pw", 0)))
                act.wait_ge(*A.drained(L, ("pw", 1)))
                squares([X[:, 0], X[:, 1]])
                root(L, "cbn", SROOT, 1.0 / 256, roots.sem)
                act.wait_ge(*T.drained(L, "smean"))
                act.wait_ge(*c_fin.upto(L, 2))
                squares([VG[:, 0], VG[:, 1]])
                root(L, "svar", SROOT, 1.0 / 256, roots.sem)
                for t in (0, 1):
                    act.wait_ge(*normed.upto(L, t + 3))
                    act.activation(VG[:, t], VG[:, t], ACT.Identity, bias=col(C2.sln_b + t)).then_inc(s_act.sem, 1)
                for t in (0, 1):
                    act.wait_ge(*T.filled(L, ("vst", t)))
                    act.activation(VG[:, t], psT[:, T.buf(("vst", t))], ACT.Copy).then_inc(T.freed(("vst", t)), 1)
                act.wait_ge(*s_out.upto(L, 2))
                squares([X[:, 6], X[:, 7]])
                root(L, "sbn", SROOT, 1.0 / 256, roots.sem)
                act.activation(SQK[ROPE], KR[ROPE], ACT.Square).then_inc(kr_sq.sem, 1)
                act.wait_ge(*s_fin.upto(L, 2))
                for h in range(M_HEADS):
                    act.wait_ge(*A.filled(L, ("q", h)))
                    if h:
                        act.wait_ge(*A.drained(L, ("kv", h - 1)))
                        act.wait_ge(*A.drained(L, ("q", h - 1)))
                    act.activation(QROOT[QK], psA[QK, A.buf(("q", h))], ACT.Square).then_inc(q_sq.sem, 1)
                    act.wait_ge(*A.filled(L, ("kv", h)))
                    act.activation(SQK[NOPE], psA[NOPE, A.buf(("kv", h))], ACT.Square)
                    act.activation(RAWV[M_NOPE:P], psA[M_NOPE:P, A.buf(("kv", h))], ACT.Copy).then_inc(k_sq.sem, 1)
                    root(L, ("qs", h), QROOT, 1.0 / M_QK, q_rs.sem, QK)
                    root(L, ("ks", h), KROOT, 1.0 / M_QK, k_rs.sem, QK)
                    exps(L, h, 0)
                    for q in range(NT):
                        if q + 1 < NT:
                            exps(L, h, q + 1)
                        use = ("pt", h, q)
                        act.wait_ge(*T.filled(L, use))
                        act.activation(WT[:, 0:q + 1, (q % 4) * P:(q % 4 + 1) * P],
                                       psT[:, T.buf(use), 0:(q + 1) * P].rearrange("p (k c) -> p k c", c=P),
                                       ACT.Copy).then_inc(T.freed(use), 1)
                for t in range(4):
                    if t == 0:
                        act.wait_ge(*T.drained(L, ("av", M_HEADS - 1, 1)))
                    if t >= 2:
                        act.wait_ge(*m_used.upto(L, t - 1))
                    act.activation(PR[t % 2], ZM[:, t], ACT.Square).then_inc(m_sq.sem, 1)
                root(L, "mbn", QROOT, 1.0 / 512, m_rs.sem)
                for j in (0, 1, 6, 7, 2, 3, 4, 5):
                    if 2 <= j < 6:
                        act.wait_ge(*m_fin.upto(L, j - 1))
                    act.activation(Hhi[:, j], X[:, j], ACT.Copy).then_inc(y_hi.sem, 1)
                with act.Fori(0, KT // 2) as jj:
                    for b in (0, 1):
                        act.wait_ge(*x_ready.upto(L + 1, jj * 2 + b - 1))
                        act.dma_start(wk[:, 4 + b], tile_of(xs_v, jj * 2 + b)).then_inc(x_back[b].sem, 16)

            out_tiles = env.out.rearrange("(t p) d -> t p d", p=P)
            for t in range(NT):
                act.wait_ge(copied, t + 1)
                act.dma_start(out_tiles[t], wk[:, t % 2]).then_inc(written[t % 2], 16)
            for b in (0, 1):
                act.wait_ge(written[b], 16 * NT // 2)

        @block.vector
        def _(dve):
            def step(ins):
                dve_step.step(dve, ins)

            def scale_by(dst, g, root_tile, rows=slice(0, P), src=None):
                return dve.scalar_tensor_tensor(out=dst[rows], in0=(dst if src is None else src)[rows],
                                                scalar=cur[rows, g:g + 1], in1=root_tile[rows], op0=ALU.mult,
                                                op1=ALU.mult)

            def split_low(dst, src, hi):
                return dve.tensor_tensor(dst, src, hi.bitcast(F32), ALU.subtract)

            def centre(L, use, tiles):
                dve.wait_ge(*T.filled(L, use))
                dve.scalar_tensor_tensor(out=tiles[:, 0], in0=psT[:, T.buf(use)], scalar=-1.0 / 256,
                                         in1=tiles[:, 0], op0=ALU.mult, op1=ALU.add)
                dve.scalar_tensor_tensor(out=tiles[:, 1], in0=psT[:, T.buf(use)], scalar=-1.0 / 256,
                                         in1=tiles[:, 1], op0=ALU.mult, op1=ALU.add).then_inc(T.freed(use), 1)

            def rotate(L, use, dst, done):
                dve.wait_ge(*T.filled(L, use))
                dve.tensor_tensor(ROT[ROPE], psT[ROPE, T.buf(use)], rope[ROPE, 1], ALU.mult)\
                    .then_inc(T.freed(use), 1)
                step(dve.tensor_tensor(dst[ROPE], dst[ROPE], rope[ROPE, 0], ALU.mult))
                dve.tensor_tensor(dst[ROPE], dst[ROPE], ROT[ROPE], ALU.add).then_inc(done, 1)

            def maxima(L, h, q):
                use, b = ("s", h, q), q % 2
                dve.wait_ge(*A.filled(L, use))
                step(dve.reduce_max(rowmax[:, b:b + 1], psA[:, A.buf(use), 0:(q + 1) * P], AX_X))
                dve.tensor_scalar(negmax[:, b:b + 1], rowmax[:, b:b + 1], -SCALE, None, ALU.mult)\
                    .then_inc(nmax.sem, 1)

            dve.memset(ypad[:, :, 0:PAD], 0.0).then_inc(dve_step.sem, 1)
            dve.memset(KR[NOPE], 0.0).then_inc(dve_step.sem, 1)
            dve.memset(rowmax[:], 0.0).then_inc(x_ready.sem, KT)
            dve.wait_ge(params_in, 64)
            with dve.Fori(0, DEPTH) as L:
                dve_step.layer(L)
                step(dve.tensor_copy(cur[:], par[:, bass.ds(L, 1), :].rearrange("p a c -> p (a c)")))
                dve.wait_ge(*rstd.upto(L, 1))
                dve.wait_ge(*x_saved.upto(L, 16))
                for j in range(KT + 1):
                    if j < KT:
                        scale_by(X[:, j], C2.norm + j, wk[:, 2]).then_inc(h_scaled.sem, 1)
                    if j:
                        dve.wait_ge(*h_hi.upto(L, j))
                        split_low(Hlo[:, j - 1], X[:, j - 1], Hhi[:, j - 1]).then_inc(h_lo.sem, 1)
                for t in (0, 1):
                    dve.wait_ge(*A.filled(L, ("a", t)))
                    dve.wait_ge(*A.drained(L, ("g", t)))
                    dve.tensor_tensor(ypad[:, t, PAD:], psA[:, A.buf(("a", t))], VG[:, t], ALU.mult)\
                        .then_inc(A.freed(("a", t)), 1)
                for t in (0, 1):
                    dve.wait_ge(*A.drained(L, ("a", t)))
                    step(dve.tensor_scalar(YC[:, t], ypad[:, t, 0:SEQ], col(C2.conv_w + t), col(C2.conv_b + t),
                                           ALU.mult, ALU.add))
                    for k in range(1, CONV_K):
                        ins = dve.scalar_tensor_tensor(out=YC[:, t], in0=ypad[:, t, k:k + SEQ],
                                                       scalar=col(C2.conv_w + 2 * k + t), in1=YC[:, t],
                                                       op0=ALU.mult, op1=ALU.add)
                        if k < CONV_K - 1:
                            step(ins)
                        else:
                            ins.then_inc(conv_done.sem, 1)
                for t in (0, 1):
                    dve.wait_ge(*A.drained(L, ("zs", t)))
                    dve.tensor_tensor(UZ[:, t], UZ[:, t], ZS[t], ALU.mult).then_inc(uz_done.sem, 1)
                for use, n0, n1, g in (("cqs", 0, Q_LORA_T, C2.qn), ("ckvs", Q_LORA_T, KT, C2.kvn - Q_LORA_T)):
                    dve.wait_ge(*l_rs.upto(L, 1 if n0 == 0 else 2))
                    for j in range(n0, n1 + 1):
                        if j < n1:
                            scale_by(X[:, j], g + j, LROOT).then_inc(l_scaled.sem, 1)
                        if j > n0:
                            dve.wait_ge(*l_hi.upto(L, j))
                            split_low(Hlo[:, j - 1], X[:, j - 1], Hhi[:, j - 1]).then_inc(l_lo.sem, 1)
                centre(L, "cmean", YC)
                dve.wait_ge(*roots.upto(L, 1))
                for t in (0, 1):
                    scale_by(YC[:, t], C2.cln_g + t, SROOT).then_inc(normed.sem, 1)
                for m in (0, 1):
                    dve.wait_ge(*A.filled(L, ("pw", m)))
                    dve.scalar_tensor_tensor(out=X[:, m], in0=psA[:, A.buf(("pw", m))], scalar=col(C2.pwb + m),
                                             in1=ZC[:, m], op0=ALU.add, op1=ALU.mult).then_inc(A.freed(("pw", m)), 1)
                dve.wait_ge(*roots.upto(L, 2))
                for m in (0, 1):
                    scale_by(X[:, m], C2.bn + m, SROOT).then_inc(c_fin.sem, 1)
                centre(L, "smean", VG)
                dve.wait_ge(*roots.upto(L, 3))
                for t in (0, 1):
                    scale_by(VG[:, t], C2.sln_g + t, SROOT).then_inc(normed.sem, 1)
                dve.wait_ge(*T.filled(L, "wgt"))
                dve.tensor_tensor(WG.rearrange("p (g t) -> p g t", g=4),
                                  psT[:, T.buf("wgt"), 0:4 * P].rearrange("p (g t) -> p g t", g=4),
                                  causal[:].unsqueeze(1).broadcast_to([P, 4, P]), ALU.mult)\
                    .then_inc(T.freed("wgt"), 1)
                for t in (0, 1):
                    dve.wait_ge(*A.filled(L, ("sg", t)))
                    dve.tensor_tensor(by_chunk(X[:, 6 + t]), by_chunk(psA[:, A.buf(("sg", t))]),
                                      every_chunk(sgb[:, t]), ALU.add).then_inc(A.freed(("sg", t)), 1)
                    dve.wait_ge(*A.drained(L, ("sg", t)))
                    dve.tensor_tensor(X[:, 6 + t], X[:, 6 + t], UZ[:, t], ALU.mult).then_inc(s_out.sem, 1)
                dve.wait_ge(*roots.upto(L, 4))
                for t in (0, 1):
                    scale_by(X[:, 6 + t], C2.bn + 6 + t, SROOT).then_inc(s_fin.sem, 1)
                dve.wait_ge(*kr_sq.upto(L, 1))
                dve.tensor_scalar(KR[ROPE], KR[ROPE], cur[ROPE, C2.kg:C2.kg + 1], None, ALU.mult)\
                    .then_inc(kr_g.sem, 1)
                rotate(L, "krswap", KR, kr_rot.sem)
                for h in range(M_HEADS):
                    rows = head_rows(h)
                    qb, kb = psA[:, A.buf(("q", h))], psA[:, A.buf(("kv", h))]
                    dve.wait_ge(*q_rs.upto(L, h + 1))
                    scale_by(Q, C2.qg, QROOT, QK, src=qb).then_inc(A.freed(("q", h)), 1)
                    dve.wait_ge(*k_rs.upto(L, h + 1))
                    dve.wait_ge(*kr_rot.upto(L, 1))
                    dve.tensor_tensor(KK[ROPE], KR[ROPE], KROOT[ROPE], ALU.mult)
                    scale_by(KK, C2.kg, KROOT, NOPE, src=kb).then_inc(A.freed(("kv", h)), 1)
                    dve.wait_ge(*T.filled(L, ("vt", h)))
                    dve.tensor_copy(V, psT[:, T.buf(("vt", h)), 0:HALF]).then_inc(T.freed(("vt", h)), 1)
                    rotate(L, ("qswap", h), Q, q_rot.sem)
                    maxima(L, h, 0)
                    for q in range(NT):
                        if q + 1 < NT:
                            maxima(L, h, q + 1)
                        b, n = q % 2, (q + 1) * P
                        dve.wait_ge(*A.drained(L, ("s", h, q)))
                        step(dve.reciprocal(inv[:, b:b + 1], rowsum[:, b:b + 1]))
                        dve.tensor_scalar(PR[b][:, 0:n], PR[b][:, 0:n], inv[:, b:b + 1], None, ALU.mult)\
                            .then_inc(mixed.sem, 1)
                        if q % 4 == 3:
                            use, g = ("av", h, q // 4), q // 4
                            y = ZM[rows, h // 2, g * HALF:(g + 1) * HALF]
                            dve.wait_ge(*T.filled(L, use))
                            dve.tensor_tensor(y, y, psT[rows, T.buf(use), 0:HALF], ALU.mult)\
                                .then_inc(T.freed(use), 1)
                dve.wait_ge(*m_rs.upto(L, 1))
                for t in range(4):
                    scale_by(X[:, 2 + t], C2.bn + 2 + t, QROOT, src=ZM[:, t]).then_inc(m_fin.sem, 1)
                dve.wait_ge(*m_fin.upto(L, 4))
                for i, j in enumerate((0, 1, 6, 7, 2, 3, 4, 5)):
                    dve.wait_ge(*y_hi.upto(L, i + 1))
                    split_low(Hlo[:, j], X[:, j], Hhi[:, j]).then_inc(y_lo.sem, 1)
                with dve.Fori(0, KT // 2) as jj:
                    for b in (0, 1):
                        dve.wait_ge(*out_filled.upto(L, jj * 2 + b + 1))
                        dve.wait_ge(*x_back[b].upto(L, jj * 16 + 16))
                        dve.tensor_tensor(tile_of(X, jj * 2 + b), psA[:, b], wk[:, 4 + b], ALU.add)\
                            .then_inc(x_ready.sem, 1)
            counts["d2"] = dve_step.k
            for t in range(NT):
                dve.wait_ge(turned, t + 1)
                if t >= 2:
                    dve.wait_ge(written[t % 2], 16 * (t // 2))
                dve.tensor_copy(wk[:, t % 2], psA[:, t % 2]).then_inc(copied, 1)


def _tiles(v, n):
    return np.ascontiguousarray(v.reshape(n, P).T)


def _panel(w, nk):
    m = w.shape[1]
    return w.reshape(nk, P, m).transpose(1, 0, 2).reshape(P, nk * m)


def _pack1(w_in, w_branch, w_out):
    starts = dict(zip(("aq", "ak", "av", "az", "cx", "cb", "cc", "cz", "rq", "rk", "rv", "rz", "gate"),
                      np.cumsum([0, 512, 512, 512, 512, 512, 512, 512, 512, 256, 256, 512, 512]).tolist()))
    out = []
    for name, nk, m in P1:
        if name[0] == "branch":
            w = w_branch[name[1]][:, name[2] * P:(name[2] + 1) * P]
        elif name[0] == "out":
            w = w_out[:, name[1] * P:(name[1] + 1) * P]
        else:
            c = starts[name[0]] + (name[1] * D_MODEL + name[2] * P if name[0] == "gate" else name[1] * P)
            w = w_in[:, c:c + P]
        out.append(_panel(w, nk))
    return np.concatenate(out, axis=1)


def _pack2(w_in, w_uq, w_ukv, w_out):
    starts = dict(zip(("a", "g", "zc", "cq", "ckv", "kr", "zm", "u", "v", "zs"),
                      np.cumsum([0, 256, 256, 256, 768, 256, 32, 512, 256, 256]).tolist()))
    out = []
    for name, nk, m in P2:
        i = name[1]
        if name[0] == "q":
            w = w_uq[:, i * M_QK:(i + 1) * M_QK]
        elif name[0] == "kv":
            w = w_ukv[:, i * P:(i + 1) * P]
        elif name[0] == "out":
            w = w_out[:, i * P:(i + 1) * P]
        elif name[0] == "kr":
            c = starts["kr"]
            w = w_in[i * 512:(i + 1) * 512, c - M_NOPE:c + M_ROPE]
        else:
            c = starts[name[0]] + i * P
            w = w_in[:, c:c + P]
        out.append(_panel(w, nk))
    return np.concatenate(out, axis=1)


def _tables():
    f = np.float32
    t = np.zeros((P, K.n), f)
    idx = np.arange(P)
    t[:, K.ident:K.ident + P] = np.eye(P)
    t[:, K.ones:K.ones + P] = 1
    t[:, K.mask:K.mask + P] = np.where(idx[None, :] <= idx[:, None], 0.0, NEG)
    for col, size, half in ((K.swapa, 64, 8), (K.swapr, 64, 32)):
        for m in range(P):
            r = m % size
            if r < 2 * half:
                t[m - r + (r + half) % (2 * half), col + m] = 1
    for r in range(M_ROPE):
        t[M_NOPE + (r + 16) % 32, K.swapm + r] = 1
    t[:, K.causal:K.causal + P] = idx[:, None] <= idx[None, :]
    log_g = np.log(f(1.0) - f(2.0) ** (f(-5.0) - np.arange(HEADS, dtype=f))).astype(f)
    diff = (idx[None, :] - idx[:, None]).astype(f)
    scale = f(A_QK ** -0.5)
    pos = idx.astype(f)
    for h in range(HEADS):
        t[:, K.dmask + h * P:K.dmask + (h + 1) * P] = np.where(diff >= 0, np.exp(np.maximum(diff, 0) * log_g[h]), 0) * scale
        rows, pr = slice((h % 2) * 64, (h % 2 + 1) * 64), h // 2
        t[rows, K.xi + pr * P:K.xi + (pr + 1) * P] = np.exp((pos + 1) * log_g[h])[None]
        t[rows, K.zeta + pr * P:K.zeta + (pr + 1) * P] = (np.exp((R_CHUNK - 1 - pos) * log_g[h]) * scale)[None]
        t[rows, K.decay + pr] = np.exp(f(R_CHUNK) * log_g[h])
    pos = np.arange(SEQ, dtype=f)
    ropes = np.zeros((3, P, 2, SEQ), f)
    ropes[:, :, 0] = 1
    inv_a = f(500000.0) ** (-np.arange(0, 16, 2, dtype=f) / f(16))
    inv_r = f(1.0) / (f(10000.0) ** np.linspace(0.0, 1.0, 32, dtype=f))
    inv_m = f(10000.0) ** (-np.arange(16, dtype=f) / f(16))
    for n, inv, half, size, base in ((0, inv_a, 8, 64, 0), (1, inv_r, 32, 64, 0), (2, inv_m, 16, 128, 64)):
        ang = (pos[None, :] * inv[:, None].astype(f)).astype(f)
        for m in range(P):
            r = (m - base) % size
            if m >= base and r < 2 * half:
                ropes[n, m, 0] = np.cos(ang[r % half])
                ropes[n, m, 1] = np.sin(ang[r % half]) * (-1 if r < half else 1)
    return t, ropes


def _params1(norm_g, attn_subln_g, conv_w):
    out = np.zeros((DEPTH, P, C1.n), np.float32)
    for l in range(DEPTH):
        out[l, :, C1.norm:C1.norm + KT] = _tiles(norm_g[l], KT)
        out[l, :, C1.subln] = attn_subln_g[l]
        for k in range(3):
            out[l, :, C1.conv + 4 * k:C1.conv + 4 * k + 4] = _tiles(conv_w[l, k], 4)
        lam_init = 0.8 - 0.6 * np.exp(-0.3 * l)
        out[l, :, C1.lam_init] = lam_init
        out[l, :, C1.lam_rest] = 1.0 - lam_init
    return out


def _params2(norm_g, conv_w, conv_b, cln_g, cln_b, pwb, qn, kvn, qg, kg, sln_g, sln_b, bn):
    out = np.zeros((DEPTH, P, C2.n), np.float32)
    for l in range(DEPTH):
        o = out[l]
        o[:, C2.norm:C2.norm + 8] = _tiles(norm_g[l], 8)
        for k in range(CONV_K):
            o[:, C2.conv_w + 2 * k:C2.conv_w + 2 * k + 2] = _tiles(conv_w[l, k], 2)
        for col, v in ((C2.conv_b, conv_b), (C2.cln_g, cln_g), (C2.cln_b, cln_b), (C2.pwb, pwb),
                       (C2.sln_g, sln_g), (C2.sln_b, sln_b)):
            o[:, col:col + 2] = _tiles(v[l], 2)
        o[:, C2.qn:C2.qn + 6] = _tiles(qn[l], 6)
        o[:, C2.kvn:C2.kvn + 2] = _tiles(kvn[l], 2)
        o[:M_QK, C2.qg] = qg[l]
        o[:M_QK, C2.kg] = kg[l]
        o[:, C2.bn:C2.bn + 8] = _tiles(bn[l], 8)
    return out


def kernel(x, norm_g, w_in, attn_lambda, attn_subln_g, conv_w, w_branch, w_out, final_norm_g, norm_g_2,
           w_in_2, conv_w_2, conv_b_2, conv_ln_g_2, conv_ln_b_2, conv_pw_w_2, conv_pw_b_2, q_norm_g_2,
           w_uq_2, kv_norm_g_2, w_ukv_2, qk_q_g_2, qk_k_g_2, sg_ln_g_2, sg_ln_b_2, sg_w_2, sg_b_2,
           branch_norm_g_2, w_out_2):
    import concourse.bacc as bacc
    from concourse.bass_utils import run_bass_kernel_spmd

    def n(a):
        return np.asarray(a)

    consts, ropes = _tables()
    arrays = {
        "x": n(x)[0],
        "w1": np.stack([_pack1(n(w_in)[l], n(w_branch)[l], n(w_out)[l]) for l in range(DEPTH)]),
        "par1": _params1(n(norm_g), n(attn_subln_g), n(conv_w)),
        "lamv": n(attn_lambda).reshape(DEPTH, 4 * A_QK),
        "finalg": _tiles(n(final_norm_g), KT),
        "w2": np.stack([_pack2(n(w_in_2)[l], n(w_uq_2)[l], n(w_ukv_2)[l], n(w_out_2)[l]) for l in range(DEPTH)]),
        "par2": _params2(n(norm_g_2), n(conv_w_2), n(conv_b_2), n(conv_ln_g_2), n(conv_ln_b_2), n(conv_pw_b_2),
                         n(q_norm_g_2), n(kv_norm_g_2), n(qk_q_g_2), n(qk_k_g_2), n(sg_ln_g_2), n(sg_ln_b_2),
                         n(branch_norm_g_2)),
        "pww": np.stack([_panel(n(conv_pw_w_2)[l], 2) for l in range(DEPTH)]),
        "sgw": np.ascontiguousarray(n(sg_w_2).transpose(0, 2, 1, 3)),
        "sgb": n(sg_b_2),
        "consts": consts,
        "ropes": ropes,
    }
    arrays = {f"in_{k}": np.ascontiguousarray(v) for k, v in arrays.items()}

    def program(per1, per2):
        nc = bacc.Bacc("TRN2", target_bir_lowering=False, num_devices=1)
        args = {k[3:]: nc.dram_tensor(k, v.shape, F32, kind="ExternalInput").ap() for k, v in arrays.items()}
        out = nc.dram_tensor("out", (SEQ, D_MODEL), F32, kind="ExternalOutput").ap()
        xs = nc.dram_tensor("xs", (KT, P, SEQ), F32, kind="Internal").ap()
        return nc, build(nc, per1, per2, out=out, xs=xs, **args)

    _, counted = program({}, {})
    nc, _ = program(counted, counted)
    r = run_bass_kernel_spmd(nc, [arrays], core_ids=[0])
    return r.results[0]["out"].reshape(1, SEQ, D_MODEL)
```

```python
from contextlib import ExitStack

import numpy as np
import concourse.bass as bass
from concourse import mybir

F32 = mybir.dt.float32
F32R = mybir.dt.float32r
BF16 = mybir.dt.bfloat16
ALU = mybir.AluOpType
ACT = mybir.ActivationFunctionType
AX_X = mybir.AxisListType.X



class Group:
    pass


P = 128
SEQ, D_MODEL, DEPTH = 1024, 1024, 2
KT = D_MODEL // P
NT = SEQ // P
HALF = SEQ // 2
EPS = 1e-6
NEG = -1e30

HEADS = 4
A_QK = 64
B1_TILES = 4
R_CHUNK = 128
M_HEADS, M_NOPE, M_ROPE, M_V = 8, 64, 32, 64
M_QK = M_NOPE + M_ROPE
Q_LORA_T, KV_LORA_T = 6, 2
CONV_K = 31
PAD = CONV_K - 1


B1_PRELUDE = [("q", 0, 0), ("q", 0, 1), ("sq", 0, 0), ("k", 0, 0), ("sq", 0, 1), ("k", 0, 1), ("sk", 0, 0),
              ("sk", 0, 1), ("v", 0, 0), ("v", 0, 1)]
B1_SLOTS = [([("vt", 0, 0)], [("q", 1, 0)]),
            ([("vt", 0, 1)], [("q", 1, 1)]),
            ([("sq", 1, 0), ("ss", -1, 1)], [("k", 1, 0)]),
            ([("sq", 1, 1)], [("k", 1, 1)]),
            ([("sk", 1, 0)], [("z", 0, 0)]),
            ([("sk", 1, 1)], [("z", 0, 1)]),
            ([("ss", 0, 0)], [("v", 1, 0)]),
            ([], [("v", 1, 1)])]
B2_PRELUDE = [("q", 0, 0), ("q", 0, 1), ("qs", 0, 0), ("kv", 0, 0), ("qs", 0, 1), ("kv", 0, 1), ("ks", 0, 0),
              ("ks", 0, 1), ("vt", 0, 0), ("sq", 0, 0), ("sq", 0, 1)]
B2_SLOTS = [([], [("q", 1, 0)]),
            ([("qs", 1, 0)], [("q", 1, 1), ("kv", 1, 0)]),
            ([("qs", 1, 1), ("ks", 1, 0)], [("kv", 1, 1)]),
            ([("ks", 1, 1)], [("vt", 1, 0)]),
            ([], []),
            ([("sq", 1, 0)], []),
            ([("sq", 1, 1)], []),
            ([], [])]


def pieces(slots, heads, h, q, after):
    return [(kind, h + d, half) for kind, d, half in slots[q][after] if 0 <= h + d < heads]


def all_pieces(prelude, slots, heads):
    out = list(prelude)
    for h in range(heads):
        for q in range(NT):
            out += pieces(slots, heads, h, q, 0) + pieces(slots, heads, h, q, 1)
    return out


def panels_of_block1():
    out = []
    for kind, h, half in all_pieces(B1_PRELUDE, B1_SLOTS, HEADS):
        if kind in ("q", "k", "v", "z") and half == 0:
            out += [(("a" + kind, h), KT, P)]
    out += merge_panels(0)
    for t in range(B1_TILES):
        out += [(("cx", t), KT, P), (("cc", t), KT, P), (("cb", t), KT, P), (("cz", t), KT, P)]
    out += merge_panels(1)
    for pr in range(HEADS // 2):
        out += [(("rq", pr), KT, P), (("rk", pr), KT, P)]
        for h in (2 * pr, 2 * pr + 1):
            out += [(("rv", h), KT, P), (("rz", h), KT, P)]
    out += merge_panels(2)
    out += [(("out", j), KT, P) for j in range(KT)]
    return out


def merge_panels(i):
    out = []
    for j in range(KT):
        out += [(("gate", i, j), KT, P), (("branch", i, j), B1_TILES, P)]
    return out


def panels_of_block2():
    out = []
    for t in (0, 1):
        out += [(("g", t), KT, P), (("a", t), KT, P)]
    out += [(("zc", t), KT, P) for t in (0, 1)]
    out += [(("cq", t), KT, P) for t in range(Q_LORA_T)]
    out += [(("ckv", t), KT, P) for t in range(KV_LORA_T)]
    out += [(("kr", 0), KT // 2, M_QK), (("kr", 1), KT // 2, M_QK)]
    out += [(("zm", t), KT, P) for t in range(4)]
    for n in ("v", "u", "zs"):
        out += [((n, t), KT, P) for t in (0, 1)]
    for h in range(M_HEADS):
        out += [(("q", h), Q_LORA_T, M_QK), (("kv", h), KV_LORA_T, P)]
    out += [(("out", j), KT, P) for j in range(KT)]
    return out


def runs(panels):
    out, off = [], 0
    for p in range(0, len(panels), 2):
        sizes = [panels[p + b][1] * panels[p + b][2] for b in (0, 1)]
        if out and out[-1][2] == sizes:
            out[-1][1] += 1
        else:
            out.append([p, 1, sizes, off])
        off += sum(sizes)
    return out, off


def uses_of_block1():
    a = [("s", h, q, c) for h in range(HEADS) for q in range(NT) for c in (0, 1)]
    t = []
    a += [x[0] for x in merge_panels(0)]
    for c in range(B1_TILES):
        a += [("cx", c), ("cc", c), ("cb", c), ("cz", c)]
    a += [x[0] for x in merge_panels(1)]
    for pr in range(HEADS // 2):
        a += [("rq", pr), ("rk", pr)]
        t += [("swaprq", pr), ("swaprk", pr), ("ks", pr)]
        for h in (2 * pr, 2 * pr + 1):
            a += [("rv", h), ("rz", h), ("rs", h), ("ro", h)]
            t += [("rvt", h), ("kv", h), ("rss", h)]
    a += [x[0] for x in merge_panels(2)]
    return a, t


def uses_of_block2():
    a = []
    for c in (0, 1):
        a += [("g", c), ("a", c)]
    a += [("zc", c) for c in (0, 1)] + [("cq", c) for c in range(Q_LORA_T)] + [("ckv", c) for c in range(KV_LORA_T)]
    a += [("zm", c) for c in range(4)] + [(n, c) for n in ("v", "u", "zs") for c in (0, 1)]
    a += [("pw", 0), ("pw", 1), ("sg", 0), ("sg", 1)]
    t = ["kr", "cqs", "ckvs", "cmean", "cvar", "cbn", "smean", "svar", ("vst", 0), ("vst", 1), "wgt", "sbn",
         "krswap", "mbn"]
    a += [("s", h, q) for h in range(M_HEADS) for q in range(NT)]
    return a, t


def uses_of_attention(prelude, slots, heads):
    tp = [(h, q) for h in range(heads) for q in range(NT)]
    av = [(h, g) for h in range(heads) for g in (0, 1)]
    f = all_pieces(prelude, slots, heads)
    if ("ss", heads - 2, 1) in f:
        f.append(("ss", heads - 1, 1))
    return tp, av, f


class Ring:

    def __init__(self, name, uses, sem, buffers=2):
        assert len(uses) % buffers == 0, (name, len(uses))
        self.n, self.buffers = len(uses), buffers
        self.at = {u: i for i, u in enumerate(uses)}
        self.filled_sem = sem(f"{name}_filled")
        self.drained_sem = [sem(f"{name}{b}_drained") for b in range(buffers)]

    def buf(self, use):
        return self.at[use] % self.buffers

    def filled(self, L, use, j=0):
        return self.filled_sem, L * self.n + self.at[use] + 1 + 2 * j

    def drained(self, L, use, j=0):
        u = self.at[use]
        return self.drained_sem[u % self.buffers], L * (self.n // self.buffers) + u // self.buffers + 1 + j

    def before(self, use):
        return self.at[use] >= self.buffers

    def room(self, L, use, j=0):
        u = self.at[use]
        return self.drained_sem[u % self.buffers], L * (self.n // self.buffers) + u // self.buffers + j

    def freed(self, use):
        return self.drained_sem[self.at[use] % self.buffers]


class Tally:

    def __init__(self, sem, per_layer, before=0):
        self.sem, self.per, self.before = sem, per_layer, before

    def upto(self, L, k):
        return self.sem, L * self.per + k + self.before


class Chain:

    def __init__(self, sem, per_layer, base=0):
        self.sem, self.per, self.k, self.L, self.base = sem, per_layer, 0, 0, base

    def step(self, eng, ins):
        ins.then_inc(self.sem, 1)
        self.k += 1
        eng.wait_ge(self.sem, self.L * self.per + self.k + self.base)

    def layer(self, L):
        self.k, self.L = 0, L


P1, P2 = panels_of_block1(), panels_of_block2()
PAN1 = {p[0]: i for i, p in enumerate(P1)}
PAN2 = {p[0]: i for i, p in enumerate(P2)}
RUNS1, COLS1 = runs(P1)
RUNS2, COLS2 = runs(P2)

class C1:
    norm = 0
    subln = KT
    conv = KT + 1
    lam_init = KT + 13
    lam_rest = KT + 14
    n = KT + 15


class C2:
    norm = 0
    conv_w = 8
    conv_b = 8 + 62
    cln_g = 72
    cln_b = 74
    pwb = 76
    qn = 78
    kvn = 84
    qg = 86
    kg = 87
    sln_g = 88
    sln_b = 90
    bn = 92
    n = 100


class K:
    ident = 0
    ones = 128
    mask = 256
    swapa = 384
    swapr = 512
    swapm = 640
    causal = 768
    dmask = 896
    xi = 896 + 512
    zeta = 896 + 768
    decay = 896 + 1024
    n = 896 + 1024 + 2




def build(nc, per1, per2, x, w1, par1, lamv, finalg, w2, par2, pww, sgw, sgb, consts, ropes, out, xs):
    counts = {}
    with ExitStack() as top:
        def sem(name):
            return top.enter_context(nc.semaphore(name))

        def sb(name, shape, dt=F32):
            return top.enter_context(nc.sbuf_tensor(name, shape, dt))

        X = sb("X", [P, KT, SEQ])
        Hhi = sb("Hhi", [P, KT, SEQ], F32R)
        Hlo = sb("Hlo", [P, KT, SEQ], F32R)
        stage = sb("stage", [P, 2, KT * P])
        Whi = sb("Whi", [P, 2, KT * P], F32R)
        Wlo = sb("Wlo", [P, 2, KT * P], F32R)
        ident = sb("ident", [P, P])
        ones = sb("ones", [P, P])
        identb = sb("identb", [P, P], BF16)
        maskb = sb("maskb", [P, P], BF16)
        rope = sb("rope", [P, 2, SEQ])
        epsc = sb("epsc", [P, 1])
        psA = top.enter_context(nc.psum_tensor("psA", [P, 2, SEQ], F32))
        psT = top.enter_context(nc.psum_tensor("psT", [P, 2, SEQ], F32))
        env = Group()
        env.nc, env.x, env.w1, env.par1, env.lamv, env.finalg = nc, x, w1, par1, lamv, finalg
        env.w2, env.par2, env.pww, env.sgw, env.sgb, env.consts = w2, par2, pww, sgw, sgb, consts
        env.ropes, env.out, env.xs, env.X, env.Hhi, env.Hlo = ropes, out, xs, X, Hhi, Hlo
        env.stage, env.Whi, env.Wlo, env.ident, env.ones, env.identb = stage, Whi, Wlo, ident, ones, identb
        env.maskb, env.rope, env.epsc, env.psA, env.psT = maskb, rope, epsc, psA, psT
        first_block(env, per1, counts)
        second_block(env, per2, counts)
    return counts


def halves(ps, m=P, lo=0):
    return [ps[lo:lo + m, h * HALF:(h + 1) * HALF] for h in (0, 1)]


def three_pass_half(pe, dst, whi, wlo, rhi, rlo, nk, M, half, begun):
    c = slice(half * HALF, (half + 1) * HALF)
    for k in range(nk):
        cols = slice(k * M, (k + 1) * M)
        for w, r, end in ((whi, rhi, False), (whi, rlo, False), (wlo, rhi, True)):
            mm = pe.matmul(dst[0:M], w[:, cols], r[k][:, c], start=k == 0 and w is whi and r is rhi,
                           stop=k == nk - 1 and end)
            if begun is not None:
                mm.then_inc(begun, 1)
                begun = None
    return mm


def three_pass(pe, ps, whi, wlo, rhi, rlo, nk, M, begun, first=True, last=True):
    dst = halves(ps, M)
    for k in range(nk):
        cols = slice(k * M, (k + 1) * M)
        for w, r, end in ((whi, rhi, False), (whi, rlo, False), (wlo, rhi, True)):
            for h in (0, 1):
                mm = pe.matmul(dst[h], w[:, cols], r[k][:, h * HALF:(h + 1) * HALF],
                               start=first and k == 0 and r is rhi and w is whi,
                               stop=last and k == nk - 1 and end)
                if begun is not None:
                    mm.then_inc(begun, 1)
                    begun = None
    return mm


def weight_engines(block, s, w_dram, stage, Whi, Wlo, panels, the_runs, load_inputs):
    NP = len(panels)

    @block.sync
    def _(sp):
        load_inputs(sp)
        with sp.Fori(0, DEPTH) as L:
            for p0, pairs, sizes, off in the_runs:
                with sp.Fori(0, pairs) as i:
                    for b in (0, 1):
                        sp.wait_ge(s.w_split, L * NP + p0 + b + 1 + i * 2)
                        start = off + b * sizes[0] + i * sum(sizes)
                        sp.dma_start(stage[:, b, 0:sizes[b]], w_dram[L, :, bass.ds(start, sizes[b])])\
                            .then_inc(s.w_loaded[b], 16)

    @block.gpsimd
    def _(pool):
        pool.memset(s.credit[:, 0:1], 0.0).then_inc(s.w_split, 2)
        pool.memset(s.credit[:, 1:2], 0.0).then_inc(s.panel_begun, 1)
        pool.wait_ge(s.w_split, 2)
        with pool.Fori(0, DEPTH) as L:
            for p0, pairs, sizes, off in the_runs:
                with pool.Fori(0, pairs) as i:
                    for b in (0, 1):
                        n = sizes[b]
                        pool.wait_ge(s.w_loaded[b], (L * (NP // 2) + p0 // 2 + 1 + i) * 16)
                        pool.wait_ge(s.panel_begun, L * NP + p0 + b + 1 + i * 2)
                        pool.tensor_tensor(Whi[:, b, 0:n], stage[:, b, 0:n], s.credit[:, 0:1].broadcast_to([P, n]),
                                           ALU.add).then_inc(s.w_hi, 1)
                        pool.wait_ge(s.w_hi, L * NP + p0 + b + 1 + i * 2)
                        pool.tensor_tensor(Wlo[:, b, 0:n], stage[:, b, 0:n], Whi[:, b, 0:n].bitcast(F32),
                                           ALU.subtract).then_inc(s.w_split, 1)




def first_block(env, per, counts):
    nc, X, Hhi, Hlo, rope, ident, ones = env.nc, env.X, env.Hhi, env.Hlo, env.rope, env.ident, env.ones
    psA, psT, identb, maskb, epsc = env.psA, env.psT, env.identb, env.maskb, env.epsc
    SCALE = A_QK ** -0.5
    with ExitStack() as ctx:
        def sem(name):
            return ctx.enter_context(nc.semaphore("b1_" + name))

        def sb(name, shape, dt=F32):
            return ctx.enter_context(nc.sbuf_tensor("b1_" + name, shape, dt))

        Bhi = sb("Bhi", [P, B1_TILES, SEQ], F32R)
        Blo = sb("Blo", [P, B1_TILES, SEQ], F32R)
        wk = sb("wk", [P, 8, SEQ])
        upad = sb("upad", [P, SEQ + 2])
        par = sb("par", [P, DEPTH, C1.n])
        cur = sb("cur", [P, C1.n])
        fing = sb("fing", [P, KT])
        lamraw = sb("lamraw", [P, DEPTH, 4 * A_QK])
        lamt = sb("lamt", [P, 2 * A_QK])
        lam = sb("lam", [P, 6])
        gcol = sb("gcol", [P, 1])
        swapa = sb("swapa", [P, P])
        swapr = sb("swapr", [P, P])
        rtab = sb("rtab", [P, K.n - K.dmask])
        rowmax = sb("rowmax", [P, 2])
        negmax = sb("negmax", [P, 2, 2])
        rowsum = sb("rowsum", [P, 2, 2])
        inv = sb("inv", [P, 2, 2])
        credit = sb("credit", [P, 2])

        a_uses, t_uses = uses_of_block1()
        A = Ring("b1A", a_uses, lambda n: ctx.enter_context(nc.semaphore(n)))
        T = Ring("b1T", t_uses, lambda n: ctx.enter_context(nc.semaphore(n)))
        tp, av, f = uses_of_attention(B1_PRELUDE, B1_SLOTS, HEADS)
        TP = Ring("b1TP", tp, lambda n: ctx.enter_context(nc.semaphore(n)), 1)
        AV = Ring("b1AV", av, lambda n: ctx.enter_context(nc.semaphore(n)), 1)
        F = Ring("b1F", f, lambda n: ctx.enter_context(nc.semaphore(n)), 1)
        psTP, psAV, psF = psT[:, 0], psT[:, 1, 0:HALF], psT[:, 1, HALF:]
        NP = len(P1)
        s = Group()
        s.credit, s.w_split, s.w_hi, s.panel_begun = credit, sem("w_split"), sem("w_hi"), sem("panel_begun")
        s.w_loaded = [sem("w_loaded0"), sem("w_loaded1")]
        consts_in, params_in, mask_in = sem("consts_in"), sem("params_in"), sem("mask_in")
        x_in = [sem("x_in0"), sem("x_in1")]
        x_turned, setup = sem("x_turned"), sem("setup")
        rope_in = Tally(sem("rope_in"), 2 * 16)
        x_ready = Tally(sem("x_ready"), KT)
        out_filled = Tally(sem("out_filled"), KT)
        x_saved = Tally(sem("x_saved"), 16)
        x_back = [Tally(sem(f"x_back{b}"), 16 * KT // 2) for b in (0, 1)]
        sq_done, sq_used = Tally(sem("sq_done"), KT), Tally(sem("sq_used"), KT)
        rstd = Tally(sem("rstd"), 1)
        h_scaled, h_hi, h_lo = (Tally(sem(n), KT) for n in ("h_scaled", "h_hi", "h_lo"))
        lam_sum, lam_exp = Tally(sem("lam_sum"), 1), Tally(sem("lam_exp"), 1)
        rotated = Tally(sem("rotated"), 4 * HEADS)
        nmax = Tally(sem("nmax"), HEADS * NT)
        mixed = Tally(sem("mixed"), HEADS * NT)
        a_sq, a_rs, a_out = (Tally(sem(n), 2 * HEADS) for n in ("a_sq", "a_rs", "a_out"))
        b_hi, b_lo = (Tally(sem(n), 2 * HEADS + 2 * B1_TILES) for n in ("b_hi", "b_lo"))
        merged = Tally(sem("merged"), 2 * KT)
        c_out = Tally(sem("c_out"), B1_TILES)
        rk_scaled, r_rot = Tally(sem("rk_scaled"), HEADS // 2), Tally(sem("r_rot"), HEADS)
        r_sq, r_rs, r_out = (Tally(sem(n), HEADS) for n in ("r_sq", "r_rs", "r_out"))
        m_hi, m_lo = Tally(sem("m_hi"), KT), Tally(sem("m_lo"), KT)
        f_sq, f_used, f_sum, f_rs = (sem(n) for n in ("f_sq", "f_used", "f_sum", "f_rs"))
        dve_step = Chain(sem("dve_step"), per.get("d1", 1), 2)
        act_step = Chain(sem("act_step"), 1)

        AQ, AK, AVAL, Z = [wk[:, 0], wk[:, 4]], [wk[:, 1], wk[:, 5]], [wk[:, 2], wk[:, 6]], wk[:, 3]
        RAW = wk[:, 7]
        WT = X[:, 0:4].rearrange("p a b -> p (a b)").rearrange("p (k q) -> p k q", k=NT)
        PR = [[X[:, 4], X[:, 5]], [X[:, 6], X[:, 7]]]
        TMP, ROT = upad[:, 2:2 + HALF], upad[:, 2 + HALF:]
        Q, KK, V, R_ROT = wk[:, 0], wk[:, 1], wk[:, 2], wk[:, 7]
        RSQ, R_RAWQ, R_RAWK, R_RAWV = upad[:, 2:], wk[:, 4], wk[:, 5], wk[:, 6]
        KZ, SM, KS, ST, QX = wk[:, 4], wk[:, 4], wk[:, 5], wk[:, 6], wk[:, 7]
        DM = rtab[:, 0:HEADS * P].rearrange("p (h c) -> p h c", h=HEADS)
        XI = rtab[:, K.xi - K.dmask:K.zeta - K.dmask].rearrange("p (h c) -> p h c", h=2)
        ZE = rtab[:, K.zeta - K.dmask:K.decay - K.dmask].rearrange("p (h c) -> p h c", h=2)
        DEC = rtab[:, K.decay - K.dmask:]
        x_tiles = env.x.rearrange("(t p) d -> t p d", p=P)
        xs_v = env.xs.rearrange("j p n -> p j n")

        def by_chunk(ap):
            return ap.rearrange("p (n c) -> p n c", n=NT)

        def every_chunk(ap):
            return ap.unsqueeze(1).broadcast_to([ap.shape[0], NT, ap.shape[1]])

        def tile_of(ap, j):
            return ap[:, bass.ds(j, 1), :].rearrange("p a b -> p (a b)")

        def head_rows(h):
            return slice((h % 2) * A_QK, (h % 2 + 1) * A_QK)

        block = ctx.enter_context(nc.Block())

        def load_inputs(sp):
            for k, dst in ((K.ident, ident), (K.ones, ones), (K.swapa, swapa), (K.swapr, swapr)):
                sp.dma_start(dst[:], env.consts[:, k:k + P]).then_inc(consts_in, 16)
            sp.dma_start(wk[:, 0, 0:P], env.consts[:, K.mask:K.mask + P]).then_inc(mask_in, 16)
            for t in range(NT):
                if t >= 2:
                    sp.wait_ge(x_turned, t - 1)
                sp.dma_start(wk[:, 2 + t % 2], x_tiles[t]).then_inc(x_in[t % 2], 16)
            sp.dma_start(rtab[:], env.consts[:, K.dmask:K.n]).then_inc(params_in, 16)
            sp.dma_start(par[:], env.par1.rearrange("l p c -> p l c")).then_inc(params_in, 16)
            sp.dma_start(fing[:], env.finalg).then_inc(params_in, 16)
            sp.dma_start(lamraw[:], env.lamv.rearrange("l c -> (l c)").partition_broadcast(P)
                         .rearrange("p (l c) -> p l c", l=DEPTH)).then_inc(params_in, 16)

        weight_engines(block, s, env.w1, env.stage, env.Whi, env.Wlo, P1, RUNS1, load_inputs)

        @block.tensor
        def _(pe):
            def panel(L, name, rhi, rlo, nk=KT, j=0):
                p = PAN1[name]
                pe.wait_ge(s.w_split, L * NP + p + 3 + j * 2)
                if name[0] == "out":
                    pe.wait_ge(*x_ready.upto(L + 1, name[1] - 1 + j * 2))
                    dst, done = psA[:, name[1] % 2], out_filled.sem
                else:
                    if A.before(name):
                        pe.wait_ge(*A.room(L, name, j))
                    dst, done = psA[:, A.buf(name)], A.filled_sem
                three_pass(pe, dst, env.Whi[:, p % 2], env.Wlo[:, p % 2], [rhi[:, k] for k in range(nk)],
                           [rlo[:, k] for k in range(nk)], nk, P, s.panel_begun).then_inc(done, 1)

            def full(dst, lhsT, rhs, start=True, stop=True):
                for h in (0, 1):
                    c = slice(h * HALF, (h + 1) * HALF)
                    mm = pe.matmul(dst[:, c], lhsT, rhs[:, c], start=start, stop=stop)
                return mm

            def turn(dst, src, blocks):
                for i in range(blocks):
                    mm = pe.transpose(dst[:, i * P:(i + 1) * P], src[:, i * P:(i + 1) * P], ident[:])
                return mm

            def swap(L, use, raw, mat, raw_tile):
                pe.wait_ge(*A.drained(L, raw))
                if T.before(use):
                    pe.wait_ge(*T.room(L, use))
                full(psT[:, T.buf(use)], mat[:], raw_tile).then_inc(T.filled_sem, 1)

            def scores(L, h, q):
                for c in (0, 1):
                    use = ("s", h, q, c)
                    if A.before(use):
                        pe.wait_ge(*A.room(L, use))
                    if q == 0 and c == 0:
                        pe.wait_ge(*rotated.upto(L, 4 * h + 4))
                    dst, rows = psA[:, A.buf(use)], slice(c * A_QK, (c + 1) * A_QK)
                    n = (q + 1) * P
                    for k0 in range(0, n, HALF):
                        k1 = min(n, k0 + HALF)
                        pe.matmul(dst[:, k0:k1], AQ[h % 2][rows, q * P:n], AK[h % 2][rows, k0:k1], start=True,
                                  stop=k1 < n)
                    pe.matmul(dst[:, q * P:n], identb[:], maskb[:], start=False, stop=True)\
                        .then_inc(A.filled_sem, 1)

            def piece(L, use):
                kind, h, half = use
                c = slice(half * HALF, (half + 1) * HALF)
                if kind in ("q", "k", "v", "z"):
                    p = PAN1[("a" + kind, h)]
                    pe.wait_ge(s.w_split, L * NP + p + 3)
                if F.before(use):
                    pe.wait_ge(*F.room(L, use))
                if kind in ("q", "k", "v", "z"):
                    mm = three_pass_half(pe, psF, env.Whi[:, p % 2], env.Wlo[:, p % 2],
                                         [Hhi[:, k] for k in range(KT)], [Hlo[:, k] for k in range(KT)], KT, P,
                                         half, None if half else s.panel_begun)
                elif kind in ("sq", "sk"):
                    mm = pe.matmul(psF, swapa[:], RAW[:, c], start=True, stop=True)
                elif kind == "vt":
                    mm = turn(psF, RAW[:, c], NT // 2)
                else:
                    pe.wait_ge(*a_sq.upto(L, 2 * h + half + 1))
                    mm = pe.matmul(psF, ones[:], TMP, start=True, stop=True)
                mm.then_inc(F.filled_sem, 1)

            def values(L, h, g):
                pe.wait_ge(*TP.drained(L, (h, 4 * g + 3)))
                pe.wait_ge(*F.drained(L, ("vt", h, 1)))
                if AV.before((h, g)):
                    pe.wait_ge(*AV.room(L, (h, g)))
                for k in range(4 * g + 4):
                    c0 = max(0, k - 4 * g) * P
                    mm = pe.matmul(psAV[:, c0:], AVAL[h % 2][:, k * P:(k + 1) * P], WT[:, k, c0:],
                                   start=k == 0, stop=k == 4 * g + 3)
                mm.then_inc(AV.filled_sem, 1)

            def attention(L):
                for use in B1_PRELUDE:
                    piece(L, use)
                scores(L, 0, 0)
                for h in range(HEADS):
                    for q in range(NT):
                        if q + 1 < NT:
                            scores(L, h, q + 1)
                        elif h + 1 < HEADS:
                            scores(L, h + 1, 0)
                        for use in pieces(B1_SLOTS, HEADS, h, q, 0):
                            piece(L, use)
                        if q == 4:
                            values(L, h, 0)
                        if q == 0 and h:
                            values(L, h - 1, 1)
                        if TP.before((h, q)):
                            pe.wait_ge(*TP.room(L, (h, q)))
                        pe.wait_ge(*mixed.upto(L, h * NT + q + 1))
                        turn(psTP, PR[q % 2][0], q + 1).then_inc(TP.filled_sem, 1)
                        for use in pieces(B1_SLOTS, HEADS, h, q, 1):
                            piece(L, use)
                values(L, HEADS - 1, 1)
                piece(L, ("ss", HEADS - 1, 1))

            def merge(L, i):
                with pe.Fori(0, KT) as j:
                    pe.wait_ge(*b_lo.upto(L, (8, 12, 16)[i]))
                    pe.wait_ge(*b_hi.upto(L, (8, 12, 16)[i]))
                    panel(L, ("gate", i, 0), Hhi, Hlo, j=j)
                    panel(L, ("branch", i, 0), Bhi, Blo, B1_TILES, j=j)

            def retain(L, pr, h):
                rows = head_rows(h)
                if h % 2 == 0:
                    use = ("ks", pr)
                    pe.wait_ge(*rk_scaled.upto(L, pr + 1))
                    pe.wait_ge(*T.room(L, use))
                    turn(psT[:, T.buf(use)], KZ, NT).then_inc(T.filled_sem, 1)
                use = ("rvt", h)
                pe.wait_ge(*A.drained(L, ("rv", h)))
                pe.wait_ge(*T.room(L, use))
                turn(psT[:, T.buf(use)], R_RAWV, NT).then_inc(T.filled_sem, 1)
                use = ("rs", h)
                pe.wait_ge(*r_rot.upto(L, 2 * pr + 2))
                pe.wait_ge(*A.room(L, use))
                for n in range(NT):
                    c = slice(n * P, (n + 1) * P)
                    mm = pe.matmul(psA[:, A.buf(use), c], KK[rows, c], Q[rows, c], start=True, stop=True)
                mm.then_inc(A.filled_sem, 1)
                use = ("kv", h)
                pe.wait_ge(*T.drained(L, ("rvt", h)))
                pe.wait_ge(*T.drained(L, ("ks", pr)))
                pe.wait_ge(*T.room(L, use))
                for n in range(NT - 1):
                    mm = pe.matmul(psT[rows, T.buf(use), n * P:(n + 1) * P],
                                   KS[:, n * P + (h % 2) * A_QK:n * P + (h % 2 + 1) * A_QK],
                                   V[:, n * P:(n + 1) * P], start=True, stop=True)
                mm.then_inc(T.filled_sem, 1)
                use = ("ro", h)
                pe.wait_ge(*A.room(L, use))
                pe.wait_ge(*A.drained(L, ("rs", h)))
                pe.wait_ge(*T.drained(L, ("kv", h)))
                for n in range(NT):
                    c = slice(n * P, (n + 1) * P)
                    mm = pe.matmul(psA[:, A.buf(use), c], V[:, c], SM[:, c], start=True, stop=n == 0)
                    if n:
                        mm = pe.matmul(psA[:, A.buf(use), c], ST[rows, c], QX[rows, c], start=False, stop=True)
                mm.then_inc(A.filled_sem, 1)
                use = ("rss", h)
                pe.wait_ge(*r_sq.upto(L, h + 1))
                pe.wait_ge(*T.room(L, use))
                full(psT[:, T.buf(use)], ones[:], RSQ).then_inc(T.filled_sem, 1)

            pe.wait_ge(consts_in, 64)
            for t in range(NT):
                pe.wait_ge(x_in[t % 2], 16 * (t // 2 + 1))
                if t >= 2:
                    pe.wait_ge(x_ready.sem, t - 1)
                turn(psA[:, t % 2], wk[:, 2 + t % 2], KT).then_inc(x_turned, 1)
            pe.wait_ge(setup, 1)

            with pe.Fori(0, DEPTH) as L:
                for j in range(KT):
                    pe.wait_ge(*sq_done.upto(L, j + 1))
                    full(psT[:, 0], ones[:], wk[:, j % 2], j == 0, j == KT - 1).then_inc(sq_used.sem, 1)
                pe.wait_ge(*h_hi.upto(L, KT))
                pe.wait_ge(*h_lo.upto(L, KT))
                attention(L)
                merge(L, 0)
                for c in range(B1_TILES):
                    for n in ("cx", "cc", "cb", "cz"):
                        panel(L, (n, c), Hhi, Hlo)
                merge(L, 1)
                for pr in range(HEADS // 2):
                    panel(L, ("rq", pr), Hhi, Hlo)
                    panel(L, ("rk", pr), Hhi, Hlo)
                    swap(L, ("swaprq", pr), ("rq", pr), swapr, R_RAWQ)
                    swap(L, ("swaprk", pr), ("rk", pr), swapr, R_RAWK)
                    for h in (2 * pr, 2 * pr + 1):
                        panel(L, ("rv", h), Hhi, Hlo)
                        panel(L, ("rz", h), Hhi, Hlo)
                        retain(L, pr, h)
                merge(L, 2)
                with pe.Fori(0, KT // 2) as jj:
                    pe.wait_ge(*m_hi.upto(L, KT))
                    pe.wait_ge(*m_lo.upto(L, KT))
                    for b in (0, 1):
                        panel(L, ("out", b), Hhi, Hlo, j=jj)

            for j in range(KT):
                pe.wait_ge(f_sq, j + 1)
                full(psT[:, 0], ones[:], wk[:, j % 2], j == 0, j == KT - 1).then_inc(f_used, 1)

        @block.scalar
        def _(act):
            def root(L, use, dst, mean, done, cols=SEQ):
                act.wait_ge(*T.filled(L, use))
                act.activation(dst, psT[:, T.buf(use), 0:cols], ACT.Ln, bias=epsc[:, 0:1], scale=mean)\
                    .then_inc(T.freed(use), 1)
                act.wait_ge(*T.drained(L, use))
                act.activation(dst, dst, ACT.Exp, scale=-0.5).then_inc(done, 1)

            def take(L, use, dst, func=ACT.Copy, j=0):
                act.wait_ge(*A.filled(L, use, j))
                act.activation(dst, psA[:, A.buf(use)], func).then_inc(A.freed(use), 1)

            def exps(L, h, q):
                act.wait_ge(*nmax.upto(L, h * NT + q + 1))
                n = (q + 1) * P
                for c in (0, 1):
                    use = ("s", h, q, c)
                    act.activation(PR[q % 2][c][:, 0:n], psA[:, A.buf(use), 0:n], ACT.Exp,
                                   bias=negmax[:, q % 2, c:c + 1], scale=SCALE,
                                   accum_out=rowsum[:, q % 2, c:c + 1]).then_inc(A.freed(use), 1)

            def piece(L, use):
                kind, h, half = use
                c = slice(half * HALF, (half + 1) * HALF)
                if kind in ("q", "k", "v"):
                    act.wait_ge(*F.filled(L, use))
                    if kind != "q":
                        act.wait_ge(*rotated.upto(L, 4 * h + half + (1 if kind == "k" else 3)))
                    act.activation(RAW[:, c], psF, ACT.Copy).then_inc(F.freed(use), 1)
                elif kind == "z":
                    act.wait_ge(*F.filled(L, use))
                    if h:
                        act.wait_ge(*a_out.upto(L, 2 * h - 1 + half))
                    act.activation(Z[:, c], psF, ACT.Silu).then_inc(F.freed(use), 1)
                elif kind == "ss":
                    n = 2 * h + half
                    act.wait_ge(*F.filled(L, use))
                    act.activation(TMP, psF, ACT.Ln, bias=epsc[:, 0:1], scale=1.0 / P).then_inc(F.freed(use), 1)
                    act.wait_ge(*F.drained(L, use))
                    act.activation(TMP, TMP, ACT.Exp, scale=-0.5).then_inc(a_rs.sem, 1)
                    act.wait_ge(*a_out.upto(L, n + 1))
                    act.activation(Bhi[:, h, c], ROT, ACT.Copy).then_inc(b_hi.sem, 1)

            def values(L, h, g):
                act.wait_ge(*AV.filled(L, (h, g)))
                act.activation(TMP, psAV, ACT.Square).then_inc(a_sq.sem, 1)

            def attention(L):
                for use in B1_PRELUDE:
                    piece(L, use)
                exps(L, 0, 0)
                for h in range(HEADS):
                    for q in range(NT):
                        if q + 1 < NT:
                            exps(L, h, q + 1)
                        elif h + 1 < HEADS:
                            exps(L, h + 1, 0)
                        for use in pieces(B1_SLOTS, HEADS, h, q, 0):
                            piece(L, use)
                        if q == 4:
                            values(L, h, 0)
                        if q == 0 and h:
                            values(L, h - 1, 1)
                        act.wait_ge(*TP.filled(L, (h, q)))
                        act.activation(WT[:, 0:q + 1, (q % 4) * P:(q % 4 + 1) * P],
                                       psTP[:, 0:(q + 1) * P].rearrange("p (k c) -> p k c", c=P),
                                       ACT.Copy).then_inc(TP.freed((h, q)), 1)
                        for use in pieces(B1_SLOTS, HEADS, h, q, 1):
                            piece(L, use)
                values(L, HEADS - 1, 1)
                piece(L, ("ss", HEADS - 1, 1))

            def gates(L, i):
                with act.Fori(0, KT // 2) as jj:
                    for b in (0, 1):
                        use = ("gate", i, b)
                        act.wait_ge(*A.drained(L, ("branch", i, 0), jj * 2 + b - 2))
                        act.wait_ge(*A.filled(L, use, jj * 2))
                        act.activation(wk[:, b], psA[:, A.buf(use)], ACT.Sigmoid).then_inc(A.freed(use), 1)

            with act.Fori(0, DEPTH) as L:
                act_step.layer(L)
                act.wait_ge(*x_ready.upto(L, KT))
                act.dma_start(xs_v, X[:]).then_inc(x_saved.sem, 16)
                act.dma_start(rope[:], env.ropes[0]).then_inc(rope_in.sem, 16)
                for j in range(KT):
                    if j >= 2:
                        act.wait_ge(*sq_used.upto(L, j - 1))
                    act.activation(wk[:, j % 2], X[:, j], ACT.Square).then_inc(sq_done.sem, 1)
                act.wait_ge(*sq_used.upto(L, KT))
                act_step.step(act, act.activation(wk[:, 2], psT[:, 0], ACT.Ln, bias=epsc[:, 0:1],
                                                  scale=1.0 / D_MODEL))
                act.activation(wk[:, 2], wk[:, 2], ACT.Exp, scale=-0.5).then_inc(rstd.sem, 1)
                for j in range(KT):
                    act.wait_ge(*h_scaled.upto(L, j + 1))
                    act.activation(Hhi[:, j], X[:, j], ACT.Copy).then_inc(h_hi.sem, 1)
                act.wait_ge(*h_lo.upto(L, KT))
                act.wait_ge(*lam_sum.upto(L, 1))
                act.activation(lam[:, 2:4], lam[:, 0:2], ACT.Exp).then_inc(lam_exp.sem, 1)
                attention(L)
                act.wait_ge(*rotated.upto(L, 4 * HEADS))
                act.dma_start(rope[:], env.ropes[1]).then_inc(rope_in.sem, 16)
                gates(L, 0)
                for c in range(B1_TILES):
                    if c:
                        act.wait_ge(*A.drained(L, ("cc", c - 1)))
                    take(L, ("cx", c), wk[:, 4])
                    if c:
                        act.wait_ge(*c_out.upto(L, c))
                    take(L, ("cb", c), wk[:, 5])
                    take(L, ("cz", c), wk[:, 6], ACT.Silu)
                    act.wait_ge(*c_out.upto(L, c + 1))
                    act.activation(Bhi[:, c], wk[:, 7], ACT.Copy).then_inc(b_hi.sem, 1)
                gates(L, 1)
                act.wait_ge(*merged.upto(L, KT))
                for pr in range(HEADS // 2):
                    take(L, ("rq", pr), R_RAWQ)
                    take(L, ("rk", pr), R_RAWK)
                    for h in (2 * pr, 2 * pr + 1):
                        take(L, ("rv", h), R_RAWV)
                        if h:
                            act.wait_ge(*r_out.upto(L, h))
                        take(L, ("rz", h), Z, ACT.Silu)
                        if h % 2 == 0:
                            act.wait_ge(*T.filled(L, ("ks", pr)))
                            act.activation(KS, psT[:, T.buf(("ks", pr))], ACT.Copy).then_inc(T.freed(("ks", pr)), 1)
                        use = ("ro", h)
                        act.wait_ge(*A.filled(L, use))
                        if h:
                            act.wait_ge(*b_lo.upto(L, 12 + h))
                        act.activation(RSQ, psA[:, A.buf(use)], ACT.Square).then_inc(r_sq.sem, 1)
                        root(L, ("rss", h), RSQ, 1.0 / P, r_rs.sem)
                        act.wait_ge(*r_out.upto(L, h + 1))
                        act.activation(Bhi[:, h], RSQ, ACT.Copy).then_inc(b_hi.sem, 1)
                gates(L, 2)
                for j in range(KT):
                    act.wait_ge(*merged.upto(L, KT + j + 1))
                    if j == 0:
                        act.wait_ge(*A.filled(L, ("gate", 2, 0), KT - 1))
                    act.activation(Hhi[:, j], X[:, j], ACT.Copy).then_inc(m_hi.sem, 1)
                with act.Fori(0, KT // 2) as jj:
                    for b in (0, 1):
                        act.wait_ge(*x_ready.upto(L + 1, jj * 2 + b - 1))
                        act.dma_start(wk[:, 4 + b], tile_of(xs_v, jj * 2 + b)).then_inc(x_back[b].sem, 16)

            act.wait_ge(*x_ready.upto(DEPTH, KT))
            for j in range(KT):
                if j >= 2:
                    act.wait_ge(f_used, j - 1)
                act.activation(wk[:, j % 2], X[:, j], ACT.Square).then_inc(f_sq, 1)
            act.wait_ge(f_used, KT)
            act.activation(wk[:, 2], psT[:, 0], ACT.Ln, bias=epsc[:, 0:1], scale=1.0 / D_MODEL).then_inc(f_sum, 1)
            act.wait_ge(f_sum, 1)
            act.activation(wk[:, 2], wk[:, 2], ACT.Exp, scale=-0.5).then_inc(f_rs, 1)

        @block.vector
        def _(dve):
            def step(ins):
                dve_step.step(dve, ins)

            def rotate(L, use, raw, raw_tile, dst, done):
                dve.wait_ge(*A.drained(L, raw))
                step(dve.tensor_tensor(dst, raw_tile, rope[:, 0], ALU.mult))
                dve.wait_ge(*T.filled(L, use))
                dve.tensor_tensor(R_ROT, psT[:, T.buf(use)], rope[:, 1], ALU.mult).then_inc(T.freed(use), 1)
                dve.wait_ge(*T.drained(L, use))
                dve.tensor_tensor(dst, dst, R_ROT, ALU.add).then_inc(done, 1)

            def maxima(L, h, q):
                n = (q + 1) * P
                for c in (0, 1):
                    use = ("s", h, q, c)
                    dve.wait_ge(*A.filled(L, use))
                    step(dve.reduce_max(rowmax[:, c:c + 1], psA[:, A.buf(use), 0:n], AX_X))
                dve.tensor_scalar(negmax[:, q % 2], rowmax[:], -SCALE, None, ALU.mult).then_inc(nmax.sem, 1)

            def mix(L, h, q):
                n = (q + 1) * P
                p0, p1 = PR[q % 2][0][:, 0:n], PR[q % 2][1][:, 0:n]
                dve.wait_ge(*A.drained(L, ("s", h, q, 0)))
                dve.wait_ge(*A.drained(L, ("s", h, q, 1)))
                step(dve.reciprocal(inv[:, q % 2], rowsum[:, q % 2]))
                step(dve.tensor_scalar(p1, p1, inv[:, q % 2, 1:2], lam[:, 4:5], ALU.mult, ALU.mult))
                dve.scalar_tensor_tensor(out=p0, in0=p0, scalar=inv[:, q % 2, 0:1], in1=p1, op0=ALU.mult, op1=ALU.add)\
                    .then_inc(mixed.sem, 1)

            def piece(L, use):
                kind, h, half = use
                c = slice(half * HALF, (half + 1) * HALF)
                if kind in ("sq", "sk"):
                    dst = (AQ if kind == "sq" else AK)[h % 2][:, c]
                    dve.wait_ge(*F.filled(L, use))
                    dve.tensor_tensor(ROT, psF, rope[:, 1, c], ALU.mult).then_inc(F.freed(use), 1)
                    step(dve.tensor_tensor(dst, RAW[:, c], rope[:, 0, c], ALU.mult))
                    dve.wait_ge(*F.drained(L, use))
                    dve.tensor_tensor(dst, dst, ROT, ALU.add).then_inc(rotated.sem, 1)
                    dve.wait_ge(*rotated.upto(L, 4 * h + half + (1 if kind == "sq" else 3)))
                elif kind == "vt":
                    dve.wait_ge(*F.filled(L, use))
                    dve.tensor_copy(AVAL[h % 2][:, c], psF).then_inc(F.freed(use), 1)
                elif kind == "ss":
                    n = 2 * h + half
                    dve.wait_ge(*a_rs.upto(L, n + 1))
                    dve.scalar_tensor_tensor(out=ROT, in0=psAV, scalar=gcol[:, 0:1], in1=TMP, op0=ALU.mult,
                                             op1=ALU.mult).then_inc(AV.freed((h, half)), 1)
                    dve.wait_ge(*AV.drained(L, (h, half)))
                    dve.wait_ge(*F.drained(L, ("z", h, half)))
                    dve.tensor_tensor(ROT, ROT, Z[:, c], ALU.mult).then_inc(a_out.sem, 1)
                    dve.wait_ge(*b_hi.upto(L, n + 1))
                    dve.tensor_tensor(Blo[:, h, c], ROT, Bhi[:, h, c].bitcast(F32), ALU.subtract)\
                        .then_inc(b_lo.sem, 1)

            def attention(L):
                for use in B1_PRELUDE:
                    piece(L, use)
                maxima(L, 0, 0)
                for h in range(HEADS):
                    for q in range(NT):
                        mix(L, h, q)
                        if q + 1 < NT:
                            maxima(L, h, q + 1)
                        elif h + 1 < HEADS:
                            maxima(L, h + 1, 0)
                        for after in (0, 1):
                            for use in pieces(B1_SLOTS, HEADS, h, q, after):
                                piece(L, use)
                piece(L, ("ss", HEADS - 1, 1))

            def merge(L, i):
                with dve.Fori(0, KT // 2) as jj:
                    if i == 2:
                        dve.wait_ge(*merged.upto(L, KT))
                    for b in (0, 1):
                        use, j = ("branch", i, b), jj * 2 + b
                        dve.wait_ge(*A.filled(L, use, jj * 2))
                        dve.wait_ge(*A.drained(L, ("gate", i, b), jj * 2))
                        if i == 0:
                            dve.tensor_tensor(tile_of(X, j), wk[:, b], psA[:, A.buf(use)], ALU.mult)\
                                .then_inc(A.freed(use), 1)
                        else:
                            dve.tensor_tensor(wk[:, 2 + b], wk[:, b], psA[:, A.buf(use)], ALU.mult)\
                                .then_inc(A.freed(use), 1)
                            dve.wait_ge(*A.drained(L, use, jj * 2))
                            dve.tensor_tensor(tile_of(X, j), tile_of(X, j), wk[:, 2 + b], ALU.add)\
                                .then_inc(merged.sem, 1)

            def retain(L, pr, h):
                rows = head_rows(h)
                use = ("rvt", h)
                dve.wait_ge(*T.filled(L, use))
                dve.tensor_copy(V, psT[:, T.buf(use)]).then_inc(T.freed(use), 1)
                use = ("rs", h)
                dve.wait_ge(*A.filled(L, use))
                dve.tensor_tensor(by_chunk(SM), by_chunk(psA[:, A.buf(use)]), every_chunk(DM[:, h]), ALU.mult)\
                    .then_inc(A.freed(use), 1)
                use = ("kv", h)
                kv = psT[:, T.buf(use)]
                dve.wait_ge(*T.filled(L, use))
                step(dve.tensor_copy(ST[rows, P:2 * P], kv[rows, 0:P]))
                for n in range(1, NT - 1):
                    ins = dve.scalar_tensor_tensor(out=ST[rows, (n + 1) * P:(n + 2) * P],
                                                   in0=ST[rows, n * P:(n + 1) * P], scalar=DEC[rows, pr:pr + 1],
                                                   in1=kv[rows, n * P:(n + 1) * P], op0=ALU.mult, op1=ALU.add)
                    if n < NT - 2:
                        step(ins)
                    else:
                        ins.then_inc(T.freed(use), 1)
                use = ("ro", h)
                dve.wait_ge(*r_rs.upto(L, h + 1))
                dve.tensor_tensor(RSQ, psA[:, A.buf(use)], RSQ, ALU.mult).then_inc(A.freed(use), 1)
                dve.wait_ge(*A.drained(L, use))
                dve.wait_ge(*A.drained(L, ("rz", h)))
                dve.tensor_tensor(RSQ, RSQ, Z, ALU.mult).then_inc(r_out.sem, 1)
                dve.wait_ge(*b_hi.upto(L, 12 + h + 1))
                dve.tensor_tensor(Blo[:, h], RSQ, Bhi[:, h].bitcast(F32), ALU.subtract).then_inc(b_lo.sem, 1)

            dve.memset(upad[:, 0:2], 0.0).then_inc(dve_step.sem, 1)
            dve.memset(epsc[:], EPS).then_inc(dve_step.sem, 1)
            dve.wait_ge(consts_in, 64)
            dve.wait_ge(mask_in, 16)
            dve.wait_ge(dve_step.sem, 2)
            for t in range(NT):
                dve.wait_ge(x_turned, t + 1)
                dve.tensor_copy(X[:, :, t * P:(t + 1) * P], by_chunk(psA[:, t % 2])).then_inc(x_ready.sem, 1)
                if t == 0:
                    dve.tensor_copy(maskb[:], wk[:, 0, 0:P])
                    dve.tensor_copy(identb[:], ident[:]).then_inc(setup, 1)
            dve.wait_ge(params_in, 64)
            with dve.Fori(0, DEPTH) as L:
                dve_step.layer(L)
                step(dve.tensor_copy(cur[:], par[:, bass.ds(L, 1), :].rearrange("p a c -> p (a c)")))
                raw = lamraw[:, bass.ds(L, 1), :].rearrange("p a (m two c) -> p (a m) two c", m=2, two=2)
                step(dve.tensor_tensor(lamt[:].rearrange("p (m c) -> p m c", m=2), raw[:, :, 0], raw[:, :, 1],
                                       ALU.mult))
                dve.reduce_sum(lam[:, 0:2], lamt[:].rearrange("p (m c) -> p m c", m=2), AX_X)\
                    .then_inc(lam_sum.sem, 1)
                step(dve.tensor_tensor(gcol[:], cur[:, C1.subln:C1.subln + 1],
                                       cur[:, C1.lam_rest:C1.lam_rest + 1], ALU.mult))
                dve.wait_ge(*rstd.upto(L, 1))
                dve.wait_ge(*x_saved.upto(L, 16))
                for j in range(KT + 1):
                    if j < KT:
                        dve.scalar_tensor_tensor(out=X[:, j], in0=X[:, j], scalar=cur[:, C1.norm + j:C1.norm + j + 1],
                                                 in1=wk[:, 2], op0=ALU.mult, op1=ALU.mult).then_inc(h_scaled.sem, 1)
                    if j:
                        dve.wait_ge(*h_hi.upto(L, j))
                        dve.tensor_tensor(Hlo[:, j - 1], X[:, j - 1], Hhi[:, j - 1].bitcast(F32), ALU.subtract)\
                            .then_inc(h_lo.sem, 1)
                dve.wait_ge(*lam_exp.upto(L, 1))
                step(dve.tensor_tensor(lam[:, 5:6], lam[:, 3:4], lam[:, 2:3], ALU.subtract))
                step(dve.tensor_tensor(lam[:, 4:5], lam[:, 5:6], cur[:, C1.lam_init:C1.lam_init + 1],
                                       ALU.subtract))
                dve.wait_ge(*rope_in.upto(L, 16))
                attention(L)
                merge(L, 0)
                for c in range(B1_TILES):
                    dve.wait_ge(*A.filled(L, ("cc", c)))
                    dve.wait_ge(*A.drained(L, ("cx", c)))
                    dve.tensor_tensor(upad[:, 2:], psA[:, A.buf(("cc", c))], wk[:, 4], ALU.mult)\
                        .then_inc(A.freed(("cc", c)), 1)
                    dve.wait_ge(*A.drained(L, ("cc", c)))
                    for k in range(3):
                        w = cur[:, C1.conv + 4 * k + c:C1.conv + 4 * k + c + 1]
                        if k == 0:
                            step(dve.tensor_scalar(wk[:, 7], upad[:, 0:SEQ], w, None, ALU.mult))
                        else:
                            step(dve.scalar_tensor_tensor(out=wk[:, 7], in0=upad[:, k:k + SEQ], scalar=w,
                                                          in1=wk[:, 7], op0=ALU.mult, op1=ALU.add))
                    dve.wait_ge(*A.drained(L, ("cb", c)))
                    step(dve.tensor_tensor(wk[:, 7], wk[:, 7], wk[:, 5], ALU.mult))
                    dve.wait_ge(*A.drained(L, ("cz", c)))
                    dve.tensor_tensor(wk[:, 7], wk[:, 7], wk[:, 6], ALU.mult).then_inc(c_out.sem, 1)
                    dve.wait_ge(*b_hi.upto(L, 8 + c + 1))
                    dve.tensor_tensor(Blo[:, c], wk[:, 7], Bhi[:, c].bitcast(F32), ALU.subtract)\
                        .then_inc(b_lo.sem, 1)
                merge(L, 1)
                dve.wait_ge(*rope_in.upto(L, 32))
                for pr in range(HEADS // 2):
                    rotate(L, ("swaprq", pr), ("rq", pr), R_RAWQ, Q, r_rot.sem)
                    rotate(L, ("swaprk", pr), ("rk", pr), R_RAWK, KK, r_rot.sem)
                    dve.wait_ge(*r_rot.upto(L, 2 * pr + 2))
                    step(dve.tensor_tensor(by_chunk(QX), by_chunk(Q), every_chunk(XI[:, pr]), ALU.mult))
                    dve.tensor_tensor(by_chunk(KZ), by_chunk(KK), every_chunk(ZE[:, pr]), ALU.mult)\
                        .then_inc(rk_scaled.sem, 1)
                    for h in (2 * pr, 2 * pr + 1):
                        retain(L, pr, h)
                merge(L, 2)
                for j in range(KT):
                    dve.wait_ge(*m_hi.upto(L, j + 1))
                    dve.tensor_tensor(Hlo[:, j], X[:, j], Hhi[:, j].bitcast(F32), ALU.subtract)\
                        .then_inc(m_lo.sem, 1)
                with dve.Fori(0, KT // 2) as jj:
                    for b in (0, 1):
                        dve.wait_ge(*out_filled.upto(L, jj * 2 + b + 1))
                        dve.wait_ge(*x_back[b].upto(L, jj * 16 + 16))
                        dve.tensor_tensor(tile_of(X, jj * 2 + b), psA[:, b], wk[:, 4 + b], ALU.add)\
                            .then_inc(x_ready.sem, 1)
            counts["d1"] = dve_step.k
            dve.wait_ge(f_rs, 1)
            dve.wait_ge(*x_ready.upto(DEPTH, KT))
            for j in range(KT):
                dve.scalar_tensor_tensor(out=X[:, j], in0=X[:, j], scalar=fing[:, j:j + 1], in1=wk[:, 2],
                                         op0=ALU.mult, op1=ALU.mult).then_inc(x_ready.sem, 1)
            dve.wait_ge(x_ready.sem, (DEPTH + 2) * KT)


def second_block(env, per, counts):
    nc, X, Hhi, Hlo, rope, ident, ones = env.nc, env.X, env.Hhi, env.Hlo, env.rope, env.ident, env.ones
    psA, psT, identb, maskb, epsc = env.psA, env.psT, env.identb, env.maskb, env.epsc
    SCALE = M_QK ** -0.5
    with ExitStack() as ctx:
        def sem(name):
            return ctx.enter_context(nc.semaphore("b2_" + name))

        def sb(name, shape, dt=F32):
            return ctx.enter_context(nc.sbuf_tensor("b2_" + name, shape, dt))

        wk = sb("wk", [P, 14, SEQ])
        ypad = sb("ypad", [P, 2, SEQ + PAD])
        par = sb("par", [P, DEPTH, C2.n])
        cur = sb("cur", [P, C2.n])
        pww = sb("pww", [P, 4 * P])
        sgw = sb("sgw", [P, 4, P])
        sgb = sb("sgb", [P, 2, P])
        swapm = sb("swapm", [P, M_ROPE])
        causal = sb("causal", [P, P])
        rowmax = sb("rowmax", [P, 2])
        negmax = sb("negmax", [P, 2])
        rowsum = sb("rowsum", [P, 2])
        inv = sb("inv", [P, 2])
        credit = sb("credit", [P, 2])

        a_uses, t_uses = uses_of_block2()
        A = Ring("b2A", a_uses, lambda n: ctx.enter_context(nc.semaphore(n)))
        T = Ring("b2T", t_uses, lambda n: ctx.enter_context(nc.semaphore(n)))
        tp, av, f = uses_of_attention(B2_PRELUDE, B2_SLOTS, M_HEADS)
        TP = Ring("b2TP", tp, lambda n: ctx.enter_context(nc.semaphore(n)), 1)
        AV = Ring("b2AV", av, lambda n: ctx.enter_context(nc.semaphore(n)), 1)
        F = Ring("b2F", f, lambda n: ctx.enter_context(nc.semaphore(n)), 1)
        psTP, psAV, psF = psT[:, 0], psT[:, 1, 0:HALF], psT[:, 1, HALF:]
        NP = len(P2)
        s = Group()
        s.credit, s.w_split, s.w_hi, s.panel_begun = credit, sem("w_split"), sem("w_hi"), sem("panel_begun")
        s.w_loaded = [sem("w_loaded0"), sem("w_loaded1")]
        params_in = sem("params_in")
        layer_in = Tally(sem("layer_in"), 4 * 16)
        x_ready = Tally(sem("x_ready"), KT)
        out_filled = Tally(sem("out_filled"), KT)
        x_saved = Tally(sem("x_saved"), 16)
        x_back = [Tally(sem(f"x_back{b}"), 16 * KT // 2) for b in (0, 1)]
        sq_done, sq_used = Tally(sem("sq_done"), KT), Tally(sem("sq_used"), KT)
        rstd = Tally(sem("rstd"), 1)
        h_scaled, h_hi, h_lo = (Tally(sem(n), KT) for n in ("h_scaled", "h_hi", "h_lo"))
        conv_done = Tally(sem("conv_done"), 2)
        uz_done = Tally(sem("uz_done"), 2)
        l_sq, l_used = Tally(sem("l_sq"), KT), Tally(sem("l_used"), KT - 2)
        l_rs = Tally(sem("l_rs"), 2)
        l_scaled, l_hi, l_lo = (Tally(sem(n), KT) for n in ("l_scaled", "l_hi", "l_lo"))
        sq2 = Tally(sem("sq2"), 4)
        roots = Tally(sem("roots"), 4)
        normed = Tally(sem("normed"), 4)
        c_act, s_act = Tally(sem("c_act"), 2), Tally(sem("s_act"), 2)
        s_out = Tally(sem("s_out"), 2)
        c_fin, s_fin = Tally(sem("c_fin"), 2), Tally(sem("s_fin"), 2)
        kr_sq, kr_g, kr_rot = Tally(sem("kr_sq"), 1), Tally(sem("kr_g"), 1), Tally(sem("kr_rot"), 1)
        qk_ln, qk_rs = Tally(sem("qk_ln"), M_HEADS), Tally(sem("qk_rs"), M_HEADS)
        q_scaled, k_scaled = Tally(sem("q_scaled"), M_HEADS), Tally(sem("k_scaled"), M_HEADS)
        q_rot = Tally(sem("q_rot"), 2 * M_HEADS)
        nmax, mixed = Tally(sem("nmax"), M_HEADS * NT), Tally(sem("mixed"), M_HEADS * NT)
        m_sq, m_used, m_rs, m_fin = Tally(sem("m_sq"), 4), Tally(sem("m_used"), 3), Tally(sem("m_rs"), 1), \
            Tally(sem("m_fin"), 4)
        y_hi, y_lo = Tally(sem("y_hi"), KT), Tally(sem("y_lo"), KT)
        turned, copied, written = sem("turned"), sem("copied"), [sem("written0"), sem("written1")]
        dve_step = Chain(sem("dve_step"), per.get("d2", 1), 2)
        act_step = Chain(sem("act_step"), 1)

        ZM, ZC, UZ, YC, VG = (wk[:, a:b] for a, b in ((0, 4), (4, 6), (6, 8), (8, 10), (10, 12)))
        KR, SQK = wk[:, 12], wk[:, 13]
        ZS = [wk[:, 13], ypad[:, 1, PAD:]]
        LSQ, LROOT = [wk[:, 13], ypad[:, 0, PAD:]], ypad[:, 1, PAD:]
        S2, SROOT = [X[:, 2], X[:, 3]], X[:, 4]
        WG = wk[:, 9, 0:4 * P]
        Q, KK, PR = [wk[:, 4], wk[:, 5]], [wk[:, 6], wk[:, 7]], [wk[:, 8], wk[:, 9]]
        QROOT, KROOT, KROT = wk[:, 10], wk[:, 11], wk[:, 9]
        V = [ypad[:, 0, PAD:PAD + HALF], ypad[:, 0, PAD + HALF:]]
        RAWKV = ypad[:, 1, PAD:]
        WT = X[:, 2:6].rearrange("p a b -> p (a b)").rearrange("p (k q) -> p k q", k=NT)
        NOPE, ROPE, QK = slice(0, M_NOPE), slice(M_NOPE, M_QK), slice(0, M_QK)
        xs_v = env.xs.rearrange("j p n -> p j n")

        def by_chunk(ap):
            return ap.rearrange("p (n c) -> p n c", n=NT)

        def every_chunk(ap):
            return ap.unsqueeze(1).broadcast_to([ap.shape[0], NT, ap.shape[1]])

        def tile_of(ap, j):
            return ap[:, bass.ds(j, 1), :].rearrange("p a b -> p (a b)")

        def col(k):
            return cur[:, k:k + 1]

        def head_rows(h):
            return slice((h % 2) * M_V, (h % 2 + 1) * M_V)

        block = ctx.enter_context(nc.Block())

        def load_inputs(sp):
            sp.dma_start(par[:], env.par2.rearrange("l p c -> p l c")).then_inc(params_in, 16)
            sp.dma_start(swapm[:], env.consts[:, K.swapm:K.swapm + M_ROPE]).then_inc(params_in, 16)
            sp.dma_start(causal[:], env.consts[:, K.causal:K.causal + P]).then_inc(params_in, 16)
            sp.dma_start(rope[:], env.ropes[2]).then_inc(params_in, 16)

        weight_engines(block, s, env.w2, env.stage, env.Whi, env.Wlo, P2, RUNS2, load_inputs)

        @block.tensor
        def _(pe):
            def panel(L, name, nk=KT, M=P, j=0, tiles=None, dst=None, done=None, first=True, last=True):
                p = PAN2[name]
                pe.wait_ge(s.w_split, L * NP + p + 3 + j * 2)
                if dst is None:
                    if A.before(name):
                        pe.wait_ge(*A.room(L, name, j))
                    dst, done = psA[:, A.buf(name)], A.filled_sem
                tiles = tiles or range(nk)
                mm = three_pass(pe, dst, env.Whi[:, p % 2], env.Wlo[:, p % 2], [Hhi[:, k] for k in tiles],
                                [Hlo[:, k] for k in tiles], nk, M, s.panel_begun, first, last)
                if done is not None:
                    mm.then_inc(done, 1)

            def full(dst, lhsT, rhs, start=True, stop=True):
                for h in (0, 1):
                    c = slice(h * HALF, (h + 1) * HALF)
                    mm = pe.matmul(dst[:, c], lhsT, rhs[:, c], start=start, stop=stop)
                return mm

            def turn(dst, src, blocks):
                for i in range(blocks):
                    mm = pe.transpose(dst[:, i * P:(i + 1) * P], src[:, i * P:(i + 1) * P], ident[:])
                return mm

            def pair_sum(L, use, tiles):
                pe.wait_ge(*T.room(L, use))
                full(psT[:, T.buf(use)], ones[:], tiles[0], True, False)
                full(psT[:, T.buf(use)], ones[:], tiles[1], False, True).then_inc(T.filled_sem, 1)

            def latent(L, use, first, n):
                pe.wait_ge(*T.room(L, use))
                for j in range(first, first + n):
                    pe.wait_ge(*l_sq.upto(L, j + 1))
                    mm = full(psT[:, T.buf(use)], ones[:], LSQ[j % 2], j == first, j == first + n - 1)
                    mm.then_inc(l_used.sem if j < first + n - 1 else T.filled_sem, 1)

            def scores(L, h, q):
                use = ("s", h, q)
                pe.wait_ge(*A.room(L, use))
                if q == 0:
                    pe.wait_ge(*q_rot.upto(L, 2 * h + 2))
                dst, n = psA[:, A.buf(use)], (q + 1) * P
                for k0 in range(0, n, HALF):
                    k1 = min(n, k0 + HALF)
                    pe.matmul(dst[:, k0:k1], Q[h % 2][QK, q * P:n], KK[h % 2][QK, k0:k1], start=True, stop=k1 < n)
                pe.matmul(dst[:, q * P:n], identb[:], maskb[:], start=False, stop=True).then_inc(A.filled_sem, 1)

            def piece(L, use):
                kind, h, half = use
                c = slice(half * HALF, (half + 1) * HALF)
                if kind in ("q", "kv"):
                    p = PAN2[(kind, h)]
                    pe.wait_ge(s.w_split, L * NP + p + 3)
                if kind == "sq":
                    pe.wait_ge(*q_scaled.upto(L, h + 1))
                if F.before(use):
                    pe.wait_ge(*F.room(L, use))
                if kind in ("q", "kv"):
                    nk, M, t0 = (Q_LORA_T, M_QK, 0) if kind == "q" else (KV_LORA_T, P, Q_LORA_T)
                    mm = three_pass_half(pe, psF, env.Whi[:, p % 2], env.Wlo[:, p % 2],
                                         [Hhi[:, t0 + k] for k in range(nk)], [Hlo[:, t0 + k] for k in range(nk)],
                                         nk, M, half, None if half else s.panel_begun)
                elif kind == "qs":
                    mm = pe.matmul(psF[QK], ones[QK, QK], QROOT[QK, c], start=True, stop=True)
                elif kind == "ks":
                    mm = pe.matmul(psF[QK], ones[QK, QK], SQK[QK, c], start=True, stop=True)
                elif kind == "sq":
                    mm = pe.matmul(psF[ROPE], swapm[QK, :], Q[h % 2][QK, c], start=True, stop=True)
                else:
                    for n in range(NT):
                        dst, src = psF[:, n * M_V:(n + 1) * M_V], RAWKV[M_NOPE:P, n * P:(n + 1) * P]
                        if n == 0:
                            pe.matmul(dst, src, ident[M_NOPE:P, M_NOPE:P], start=True, stop=True)
                        else:
                            mm = pe.transpose(dst, src, ident[M_NOPE:P, M_NOPE:P])
                mm.then_inc(F.filled_sem, 1)

            def values(L, h, g):
                rows = head_rows(h)
                pe.wait_ge(*TP.drained(L, (h, 4 * g + 3)))
                pe.wait_ge(*F.drained(L, ("vt", h, 0)))
                if AV.before((h, g)):
                    pe.wait_ge(*AV.room(L, (h, g)))
                for k in range(4 * g + 4):
                    c0 = max(0, k - 4 * g) * P
                    mm = pe.matmul(psAV[rows, c0:], V[h % 2][:, k * M_V:(k + 1) * M_V], WT[:, k, c0:],
                                   start=k == 0, stop=k == 4 * g + 3)
                mm.then_inc(AV.filled_sem, 1)

            def attention(L):
                for use in B2_PRELUDE:
                    piece(L, use)
                scores(L, 0, 0)
                for h in range(M_HEADS):
                    for q in range(NT):
                        if q + 1 < NT:
                            scores(L, h, q + 1)
                        elif h + 1 < M_HEADS:
                            scores(L, h + 1, 0)
                        for use in pieces(B2_SLOTS, M_HEADS, h, q, 0):
                            piece(L, use)
                        if q == 4:
                            values(L, h, 0)
                        if q == 0 and h:
                            values(L, h - 1, 1)
                        if TP.before((h, q)):
                            pe.wait_ge(*TP.room(L, (h, q)))
                        pe.wait_ge(*mixed.upto(L, h * NT + q + 1))
                        turn(psTP, PR[q % 2], q + 1).then_inc(TP.filled_sem, 1)
                        for use in pieces(B2_SLOTS, M_HEADS, h, q, 1):
                            piece(L, use)
                values(L, M_HEADS - 1, 1)

            with pe.Fori(0, DEPTH) as L:
                for j in range(KT):
                    pe.wait_ge(*sq_done.upto(L, j + 1))
                    full(psT[:, 0], ones[:], wk[:, j % 2], j == 0, j == KT - 1).then_inc(sq_used.sem, 1)
                pe.wait_ge(*h_hi.upto(L, KT))
                pe.wait_ge(*h_lo.upto(L, KT))
                for name, nk, M in P2[:PAN2[("kr", 0)]]:
                    panel(L, name)
                panel(L, ("kr", 0), KT // 2, M_QK, dst=psT[:, T.buf("kr")], last=False)
                panel(L, ("kr", 1), KT // 2, M_QK, tiles=range(KT // 2, KT), dst=psT[:, T.buf("kr")],
                      done=T.filled_sem, first=False)
                for name, nk, M in P2[PAN2[("zm", 0)]:PAN2[("q", 0)]]:
                    panel(L, name)
                latent(L, "cqs", 0, Q_LORA_T)
                latent(L, "ckvs", Q_LORA_T, KV_LORA_T)
                pe.wait_ge(*conv_done.upto(L, 2))
                pair_sum(L, "cmean", [YC[:, 0], YC[:, 1]])
                pe.wait_ge(*sq2.upto(L, 1))
                pair_sum(L, "cvar", S2)
                pe.wait_ge(*c_act.upto(L, 2))
                pe.wait_ge(*layer_in.upto(L, 64))
                for m in (0, 1):
                    pe.wait_ge(*A.room(L, ("pw", m)))
                    for k in (0, 1):
                        mm = full(psA[:, A.buf(("pw", m))], pww[:, k * 2 * P + m * P:k * 2 * P + (m + 1) * P],
                                  YC[:, k], k == 0, k == 1)
                    mm.then_inc(A.filled_sem, 1)
                pe.wait_ge(*sq2.upto(L, 2))
                pair_sum(L, "cbn", S2)
                pair_sum(L, "smean", [VG[:, 0], VG[:, 1]])
                pe.wait_ge(*sq2.upto(L, 3))
                pair_sum(L, "svar", S2)
                for t in (0, 1):
                    pe.wait_ge(*s_act.upto(L, t + 1))
                    pe.wait_ge(*T.room(L, ("vst", t)))
                    turn(psT[:, T.buf(("vst", t))], VG[:, t], NT).then_inc(T.filled_sem, 1)
                pe.wait_ge(*T.room(L, "wgt"))
                for g in range(4):
                    mm = pe.transpose(psT[:, T.buf("wgt"), g * P:(g + 1) * P], sgw[:, g], ident[:])
                mm.then_inc(T.filled_sem, 1)
                pe.wait_ge(*T.drained(L, "wgt"))
                for t in (0, 1):
                    pe.wait_ge(*T.drained(L, ("vst", t)))
                    pe.wait_ge(*A.room(L, ("sg", t)))
                    for n in range(NT):
                        for g in (0, 1):
                            mm = pe.matmul(psA[g * 64:(g + 1) * 64, A.buf(("sg", t)), n * P:(n + 1) * P],
                                           VG[:, t, n * P + g * 64:n * P + (g + 1) * 64],
                                           WG[:, (2 * t + g) * P:(2 * t + g + 1) * P], start=True, stop=True)
                    mm.then_inc(A.filled_sem, 1)
                pe.wait_ge(*sq2.upto(L, 4))
                pair_sum(L, "sbn", S2)
                pe.wait_ge(*kr_g.upto(L, 1))
                pe.wait_ge(*T.room(L, "krswap"))
                full(psT[ROPE, T.buf("krswap")], swapm[QK, :], KR[QK]).then_inc(T.filled_sem, 1)
                pe.wait_ge(*l_lo.upto(L, KT))
                pe.wait_ge(*l_hi.upto(L, KT))
                pe.wait_ge(*T.room(L, "mbn"))
                attention(L)
                for t in range(4):
                    pe.wait_ge(*m_sq.upto(L, t + 1))
                    full(psT[:, T.buf("mbn")], ones[:], PR[t % 2], t == 0, t == 3)\
                        .then_inc(m_used.sem if t < 3 else T.filled_sem, 1)
                with pe.Fori(0, KT // 2) as jj:
                    pe.wait_ge(*y_hi.upto(L, KT))
                    pe.wait_ge(*y_lo.upto(L, KT))
                    for b in (0, 1):
                        pe.wait_ge(*x_ready.upto(L + 1, jj * 2 + b - 1))
                        panel(L, ("out", b), j=jj, dst=psA[:, b], done=out_filled.sem)

            pe.wait_ge(*x_ready.upto(DEPTH, KT))
            for t in range(NT):
                if t >= 2:
                    pe.wait_ge(copied, t - 1)
                for j in range(KT):
                    mm = pe.transpose(psA[:, t % 2, j * P:(j + 1) * P], X[:, j, t * P:(t + 1) * P], ident[:])
                mm.then_inc(turned, 1)

        @block.scalar
        def _(act):
            def root(L, use, dst, mean, done, rows=slice(0, P)):
                act.wait_ge(*T.filled(L, use))
                act.activation(dst[rows], psT[rows, T.buf(use)], ACT.Ln, bias=epsc[rows, 0:1], scale=mean)\
                    .then_inc(T.freed(use), 1)
                act.wait_ge(*T.drained(L, use))
                act.activation(dst[rows], dst[rows], ACT.Exp, scale=-0.5).then_inc(done, 1)

            def take(L, use, dst, func=ACT.Copy):
                act.wait_ge(*A.filled(L, use))
                act.activation(dst, psA[:, A.buf(use)], func).then_inc(A.freed(use), 1)

            def squares(tiles):
                act.activation(S2[0], tiles[0], ACT.Square)
                act.activation(S2[1], tiles[1], ACT.Square).then_inc(sq2.sem, 1)

            def exps(L, h, q):
                use, n = ("s", h, q), (q + 1) * P
                act.wait_ge(*nmax.upto(L, h * NT + q + 1))
                act.activation(PR[q % 2][:, 0:n], psA[:, A.buf(use), 0:n], ACT.Exp, bias=negmax[:, q % 2:q % 2 + 1],
                               scale=SCALE, accum_out=rowsum[:, q % 2:q % 2 + 1]).then_inc(A.freed(use), 1)

            def piece(L, use):
                kind, h, half = use
                c = slice(half * HALF, (half + 1) * HALF)
                if kind == "q":
                    act.wait_ge(*F.filled(L, use))
                    if h:
                        act.wait_ge(*q_rot.upto(L, 2 * h))
                    act.activation(QROOT[QK, c], psF[QK], ACT.Square)
                    act.activation(Q[h % 2][QK, c], psF[QK], ACT.Copy).then_inc(F.freed(use), 1)
                elif kind == "kv":
                    act.wait_ge(*F.filled(L, use))
                    if h:
                        act.wait_ge(*k_scaled.upto(L, h))
                    act.activation(SQK[NOPE, c], psF[NOPE], ACT.Square)
                    act.activation(RAWKV[:, c], psF, ACT.Copy).then_inc(F.freed(use), 1)

            def qk_roots(L, h):
                both = wk[QK, 10:12]
                act.wait_ge(*F.drained(L, ("ks", h, 1)))
                act.activation(both, both, ACT.Ln, bias=epsc[QK, 0:1], scale=1.0 / M_QK).then_inc(qk_ln.sem, 1)
                act.wait_ge(*qk_ln.upto(L, h + 1))
                act.activation(both, both, ACT.Exp, scale=-0.5).then_inc(qk_rs.sem, 1)

            def attention(L):
                for use in B2_PRELUDE:
                    piece(L, use)
                qk_roots(L, 0)
                exps(L, 0, 0)
                for h in range(M_HEADS):
                    for q in range(NT):
                        if q + 1 < NT:
                            exps(L, h, q + 1)
                        elif h + 1 < M_HEADS:
                            exps(L, h + 1, 0)
                        for use in pieces(B2_SLOTS, M_HEADS, h, q, 0):
                            piece(L, use)
                        act.wait_ge(*TP.filled(L, (h, q)))
                        act.activation(WT[:, 0:q + 1, (q % 4) * P:(q % 4 + 1) * P],
                                       psTP[:, 0:(q + 1) * P].rearrange("p (k c) -> p k c", c=P),
                                       ACT.Copy).then_inc(TP.freed((h, q)), 1)
                        for use in pieces(B2_SLOTS, M_HEADS, h, q, 1):
                            piece(L, use)
                        if q == 3 and h + 1 < M_HEADS:
                            qk_roots(L, h + 1)

            with act.Fori(0, DEPTH) as L:
                act_step.layer(L)
                act.wait_ge(*x_ready.upto(L, KT))
                act.dma_start(xs_v, X[:]).then_inc(x_saved.sem, 16)
                act.dma_start(pww[:], env.pww[L]).then_inc(layer_in.sem, 16)
                act.dma_start(sgw[:], env.sgw[L]).then_inc(layer_in.sem, 16)
                for b in (0, 1):
                    src = env.sgb[L].rearrange("(two b) t -> b two t", b=2)[b]
                    act.dma_start(sgb[b * 64:(b + 1) * 64], src.partition_broadcast(64)).then_inc(layer_in.sem, 16)
                for j in range(KT):
                    if j >= 2:
                        act.wait_ge(*sq_used.upto(L, j - 1))
                    act.activation(wk[:, j % 2], X[:, j], ACT.Square).then_inc(sq_done.sem, 1)
                act.wait_ge(*sq_used.upto(L, KT))
                act_step.step(act, act.activation(wk[:, 2], psT[:, 0], ACT.Ln, bias=epsc[:, 0:1],
                                                  scale=1.0 / D_MODEL))
                act.activation(wk[:, 2], wk[:, 2], ACT.Exp, scale=-0.5).then_inc(rstd.sem, 1)
                for j in range(KT):
                    act.wait_ge(*h_scaled.upto(L, j + 1))
                    act.activation(Hhi[:, j], X[:, j], ACT.Copy).then_inc(h_hi.sem, 1)
                act.wait_ge(*h_lo.upto(L, KT))
                for t in (0, 1):
                    take(L, ("g", t), VG[:, t], ACT.Sigmoid)
                for t in (0, 1):
                    take(L, ("zc", t), ZC[:, t], ACT.Silu)
                for t in range(Q_LORA_T):
                    take(L, ("cq", t), X[:, t])
                for t in range(KV_LORA_T):
                    take(L, ("ckv", t), X[:, Q_LORA_T + t])
                act.wait_ge(*T.filled(L, "kr"))
                act.activation(KR[ROPE], psT[ROPE, T.buf("kr")], ACT.Copy).then_inc(T.freed("kr"), 1)
                for t in range(4):
                    take(L, ("zm", t), ZM[:, t], ACT.Silu)
                for t in (0, 1):
                    act.wait_ge(*A.drained(L, ("a", t)))
                    take(L, ("v", t), VG[:, t], ACT.Gelu_apprx_tanh)
                for t in (0, 1):
                    take(L, ("u", t), UZ[:, t], ACT.Gelu_apprx_tanh)
                act.wait_ge(*conv_done.upto(L, 2))
                for t in (0, 1):
                    take(L, ("zs", t), ZS[t], ACT.Silu)
                act.wait_ge(*uz_done.upto(L, 2))
                for j in range(KT):
                    if j >= 2 and j != Q_LORA_T + 1:
                        act.wait_ge(*(T.filled(L, "cqs") if j >= Q_LORA_T else l_used.upto(L, j - 1)))
                    act.activation(LSQ[j % 2], X[:, j], ACT.Square).then_inc(l_sq.sem, 1)
                    if j == Q_LORA_T - 1:
                        root(L, "cqs", LROOT, 1.0 / (Q_LORA_T * P), l_rs.sem)
                for j in range(Q_LORA_T):
                    act.wait_ge(*l_scaled.upto(L, j + 1))
                    act.activation(Hhi[:, j], X[:, j], ACT.Copy).then_inc(l_hi.sem, 1)
                root(L, "ckvs", LROOT, 1.0 / (KV_LORA_T * P), l_rs.sem)
                for j in range(Q_LORA_T, KT):
                    act.wait_ge(*l_scaled.upto(L, j + 1))
                    act.activation(Hhi[:, j], X[:, j], ACT.Copy).then_inc(l_hi.sem, 1)
                act.wait_ge(*l_lo.upto(L, KT))
                act.wait_ge(*T.drained(L, "cmean"))
                squares([YC[:, 0], YC[:, 1]])
                root(L, "cvar", SROOT, 1.0 / 256, roots.sem)
                for t in (0, 1):
                    act.wait_ge(*normed.upto(L, t + 1))
                    act.activation(YC[:, t], YC[:, t], ACT.Silu, bias=col(C2.cln_b + t)).then_inc(c_act.sem, 1)
                act.wait_ge(*A.drained(L, ("pw", 0)))
                act.wait_ge(*A.drained(L, ("pw", 1)))
                squares([X[:, 0], X[:, 1]])
                root(L, "cbn", SROOT, 1.0 / 256, roots.sem)
                act.wait_ge(*T.drained(L, "smean"))
                act.wait_ge(*c_fin.upto(L, 2))
                squares([VG[:, 0], VG[:, 1]])
                root(L, "svar", SROOT, 1.0 / 256, roots.sem)
                for t in (0, 1):
                    act.wait_ge(*normed.upto(L, t + 3))
                    act.activation(VG[:, t], VG[:, t], ACT.Identity, bias=col(C2.sln_b + t)).then_inc(s_act.sem, 1)
                for t in (0, 1):
                    act.wait_ge(*T.filled(L, ("vst", t)))
                    act.activation(VG[:, t], psT[:, T.buf(("vst", t))], ACT.Copy).then_inc(T.freed(("vst", t)), 1)
                act.wait_ge(*s_out.upto(L, 2))
                squares([X[:, 6], X[:, 7]])
                root(L, "sbn", SROOT, 1.0 / 256, roots.sem)
                act.activation(SQK[ROPE], KR[ROPE], ACT.Square).then_inc(kr_sq.sem, 1)
                act.wait_ge(*s_fin.upto(L, 2))
                attention(L)
                for t in range(4):
                    if t == 0:
                        act.wait_ge(*AV.drained(L, (M_HEADS - 1, 1)))
                    if t >= 2:
                        act.wait_ge(*m_used.upto(L, t - 1))
                    act.activation(PR[t % 2], ZM[:, t], ACT.Square).then_inc(m_sq.sem, 1)
                root(L, "mbn", QROOT, 1.0 / 512, m_rs.sem)
                for j in (0, 1, 6, 7, 2, 3, 4, 5):
                    if 2 <= j < 6:
                        act.wait_ge(*m_fin.upto(L, j - 1))
                    act.activation(Hhi[:, j], X[:, j], ACT.Copy).then_inc(y_hi.sem, 1)
                with act.Fori(0, KT // 2) as jj:
                    for b in (0, 1):
                        act.wait_ge(*x_ready.upto(L + 1, jj * 2 + b - 1))
                        act.dma_start(wk[:, 4 + b], tile_of(xs_v, jj * 2 + b)).then_inc(x_back[b].sem, 16)

            out_tiles = env.out.rearrange("(t p) d -> t p d", p=P)
            for t in range(NT):
                act.wait_ge(copied, t + 1)
                act.dma_start(out_tiles[t], wk[:, t % 2]).then_inc(written[t % 2], 16)
            for b in (0, 1):
                act.wait_ge(written[b], 16 * NT // 2)

        @block.vector
        def _(dve):
            def step(ins):
                dve_step.step(dve, ins)

            def scale_by(dst, g, root_tile, rows=slice(0, P), src=None):
                return dve.scalar_tensor_tensor(out=dst[rows], in0=(dst if src is None else src)[rows],
                                                scalar=cur[rows, g:g + 1], in1=root_tile[rows], op0=ALU.mult,
                                                op1=ALU.mult)

            def split_low(dst, src, hi):
                return dve.tensor_tensor(dst, src, hi.bitcast(F32), ALU.subtract)

            def centre(L, use, tiles):
                dve.wait_ge(*T.filled(L, use))
                dve.scalar_tensor_tensor(out=tiles[:, 0], in0=psT[:, T.buf(use)], scalar=-1.0 / 256,
                                         in1=tiles[:, 0], op0=ALU.mult, op1=ALU.add)
                dve.scalar_tensor_tensor(out=tiles[:, 1], in0=psT[:, T.buf(use)], scalar=-1.0 / 256,
                                         in1=tiles[:, 1], op0=ALU.mult, op1=ALU.add).then_inc(T.freed(use), 1)

            def rotate_key(L):
                use = "krswap"
                dve.wait_ge(*T.filled(L, use))
                dve.tensor_tensor(KROT[ROPE], psT[ROPE, T.buf(use)], rope[ROPE, 1], ALU.mult)\
                    .then_inc(T.freed(use), 1)
                step(dve.tensor_tensor(KR[ROPE], KR[ROPE], rope[ROPE, 0], ALU.mult))
                dve.tensor_tensor(KR[ROPE], KR[ROPE], KROT[ROPE], ALU.add).then_inc(kr_rot.sem, 1)

            def piece(L, use):
                kind, h, half = use
                c = slice(half * HALF, (half + 1) * HALF)
                if kind in ("qs", "ks"):
                    dve.wait_ge(*F.filled(L, use))
                    dve.tensor_copy((QROOT if kind == "qs" else KROOT)[QK, c], psF[QK]).then_inc(F.freed(use), 1)
                elif kind == "vt":
                    dve.wait_ge(*F.filled(L, use))
                    dve.tensor_copy(V[h % 2], psF).then_inc(F.freed(use), 1)
                elif kind == "sq":
                    rot, q = QROOT[ROPE, c], Q[h % 2][ROPE, c]
                    dve.wait_ge(*F.filled(L, use))
                    dve.tensor_tensor(rot, psF[ROPE], rope[ROPE, 1, c], ALU.mult).then_inc(F.freed(use), 1)
                    step(dve.tensor_tensor(q, q, rope[ROPE, 0, c], ALU.mult))
                    dve.tensor_tensor(q, q, rot, ALU.add).then_inc(q_rot.sem, 1)

            def scale(L, h):
                dve.wait_ge(*qk_rs.upto(L, h + 1))
                scale_by(Q[h % 2], C2.qg, QROOT, QK).then_inc(q_scaled.sem, 1)
                dve.tensor_tensor(KK[h % 2][ROPE], KR[ROPE], KROOT[ROPE], ALU.mult)
                scale_by(KK[h % 2], C2.kg, KROOT, NOPE, src=RAWKV).then_inc(k_scaled.sem, 1)

            def values(L, h, g):
                rows = head_rows(h)
                y = ZM[rows, h // 2, g * HALF:(g + 1) * HALF]
                dve.wait_ge(*AV.filled(L, (h, g)))
                dve.tensor_tensor(y, y, psAV[rows], ALU.mult).then_inc(AV.freed((h, g)), 1)

            def attention(L):
                for use in B2_PRELUDE:
                    if use == ("sq", 0, 0):
                        scale(L, 0)
                    piece(L, use)
                maxima(L, 0, 0)
                for h in range(M_HEADS):
                    for q in range(NT):
                        b, n = q % 2, (q + 1) * P
                        dve.wait_ge(*A.drained(L, ("s", h, q)))
                        step(dve.reciprocal(inv[:, b:b + 1], rowsum[:, b:b + 1]))
                        dve.tensor_scalar(PR[b][:, 0:n], PR[b][:, 0:n], inv[:, b:b + 1], None, ALU.mult)\
                            .then_inc(mixed.sem, 1)
                        if q + 1 < NT:
                            maxima(L, h, q + 1)
                        elif h + 1 < M_HEADS:
                            maxima(L, h + 1, 0)
                        for use in pieces(B2_SLOTS, M_HEADS, h, q, 0):
                            piece(L, use)
                        if q == 4:
                            values(L, h, 0)
                        if q == 0 and h:
                            values(L, h - 1, 1)
                        for use in pieces(B2_SLOTS, M_HEADS, h, q, 1):
                            piece(L, use)
                        if q == 4 and h + 1 < M_HEADS:
                            scale(L, h + 1)
                values(L, M_HEADS - 1, 1)

            def maxima(L, h, q):
                use, b = ("s", h, q), q % 2
                dve.wait_ge(*A.filled(L, use))
                step(dve.reduce_max(rowmax[:, b:b + 1], psA[:, A.buf(use), 0:(q + 1) * P], AX_X))
                dve.tensor_scalar(negmax[:, b:b + 1], rowmax[:, b:b + 1], -SCALE, None, ALU.mult)\
                    .then_inc(nmax.sem, 1)

            dve.memset(ypad[:, :, 0:PAD], 0.0).then_inc(dve_step.sem, 1)
            dve.memset(KR[NOPE], 0.0).then_inc(dve_step.sem, 1)
            dve.memset(rowmax[:], 0.0).then_inc(x_ready.sem, KT)
            dve.wait_ge(params_in, 64)
            with dve.Fori(0, DEPTH) as L:
                dve_step.layer(L)
                step(dve.tensor_copy(cur[:], par[:, bass.ds(L, 1), :].rearrange("p a c -> p (a c)")))
                dve.wait_ge(*rstd.upto(L, 1))
                dve.wait_ge(*x_saved.upto(L, 16))
                for j in range(KT + 1):
                    if j < KT:
                        scale_by(X[:, j], C2.norm + j, wk[:, 2]).then_inc(h_scaled.sem, 1)
                    if j:
                        dve.wait_ge(*h_hi.upto(L, j))
                        split_low(Hlo[:, j - 1], X[:, j - 1], Hhi[:, j - 1]).then_inc(h_lo.sem, 1)
                for t in (0, 1):
                    dve.wait_ge(*A.filled(L, ("a", t)))
                    dve.wait_ge(*A.drained(L, ("g", t)))
                    dve.tensor_tensor(ypad[:, t, PAD:], psA[:, A.buf(("a", t))], VG[:, t], ALU.mult)\
                        .then_inc(A.freed(("a", t)), 1)
                for t in (0, 1):
                    dve.wait_ge(*A.drained(L, ("a", t)))
                    step(dve.tensor_scalar(YC[:, t], ypad[:, t, 0:SEQ], col(C2.conv_w + t), col(C2.conv_b + t),
                                           ALU.mult, ALU.add))
                    for k in range(1, CONV_K):
                        ins = dve.scalar_tensor_tensor(out=YC[:, t], in0=ypad[:, t, k:k + SEQ],
                                                       scalar=col(C2.conv_w + 2 * k + t), in1=YC[:, t],
                                                       op0=ALU.mult, op1=ALU.add)
                        if k < CONV_K - 1:
                            step(ins)
                        else:
                            ins.then_inc(conv_done.sem, 1)
                for t in (0, 1):
                    dve.wait_ge(*A.drained(L, ("zs", t)))
                    dve.tensor_tensor(UZ[:, t], UZ[:, t], ZS[t], ALU.mult).then_inc(uz_done.sem, 1)
                for use, n0, n1, g in (("cqs", 0, Q_LORA_T, C2.qn), ("ckvs", Q_LORA_T, KT, C2.kvn - Q_LORA_T)):
                    dve.wait_ge(*l_rs.upto(L, 1 if n0 == 0 else 2))
                    for j in range(n0, n1 + 1):
                        if j < n1:
                            scale_by(X[:, j], g + j, LROOT).then_inc(l_scaled.sem, 1)
                        if j > n0:
                            dve.wait_ge(*l_hi.upto(L, j))
                            split_low(Hlo[:, j - 1], X[:, j - 1], Hhi[:, j - 1]).then_inc(l_lo.sem, 1)
                centre(L, "cmean", YC)
                dve.wait_ge(*roots.upto(L, 1))
                for t in (0, 1):
                    scale_by(YC[:, t], C2.cln_g + t, SROOT).then_inc(normed.sem, 1)
                for m in (0, 1):
                    dve.wait_ge(*A.filled(L, ("pw", m)))
                    dve.scalar_tensor_tensor(out=X[:, m], in0=psA[:, A.buf(("pw", m))], scalar=col(C2.pwb + m),
                                             in1=ZC[:, m], op0=ALU.add, op1=ALU.mult).then_inc(A.freed(("pw", m)), 1)
                dve.wait_ge(*roots.upto(L, 2))
                for m in (0, 1):
                    scale_by(X[:, m], C2.bn + m, SROOT).then_inc(c_fin.sem, 1)
                centre(L, "smean", VG)
                dve.wait_ge(*roots.upto(L, 3))
                for t in (0, 1):
                    scale_by(VG[:, t], C2.sln_g + t, SROOT).then_inc(normed.sem, 1)
                dve.wait_ge(*T.filled(L, "wgt"))
                dve.tensor_tensor(WG.rearrange("p (g t) -> p g t", g=4),
                                  psT[:, T.buf("wgt"), 0:4 * P].rearrange("p (g t) -> p g t", g=4),
                                  causal[:].unsqueeze(1).broadcast_to([P, 4, P]), ALU.mult)\
                    .then_inc(T.freed("wgt"), 1)
                for t in (0, 1):
                    dve.wait_ge(*A.filled(L, ("sg", t)))
                    dve.tensor_tensor(by_chunk(X[:, 6 + t]), by_chunk(psA[:, A.buf(("sg", t))]),
                                      every_chunk(sgb[:, t]), ALU.add).then_inc(A.freed(("sg", t)), 1)
                    dve.wait_ge(*A.drained(L, ("sg", t)))
                    dve.tensor_tensor(X[:, 6 + t], X[:, 6 + t], UZ[:, t], ALU.mult).then_inc(s_out.sem, 1)
                dve.wait_ge(*roots.upto(L, 4))
                for t in (0, 1):
                    scale_by(X[:, 6 + t], C2.bn + 6 + t, SROOT).then_inc(s_fin.sem, 1)
                dve.wait_ge(*kr_sq.upto(L, 1))
                dve.tensor_scalar(KR[ROPE], KR[ROPE], cur[ROPE, C2.kg:C2.kg + 1], None, ALU.mult)\
                    .then_inc(kr_g.sem, 1)
                rotate_key(L)
                dve.wait_ge(*kr_rot.upto(L, 1))
                attention(L)
                dve.wait_ge(*m_rs.upto(L, 1))
                for t in range(4):
                    scale_by(X[:, 2 + t], C2.bn + 2 + t, QROOT, src=ZM[:, t]).then_inc(m_fin.sem, 1)
                dve.wait_ge(*m_fin.upto(L, 4))
                for i, j in enumerate((0, 1, 6, 7, 2, 3, 4, 5)):
                    dve.wait_ge(*y_hi.upto(L, i + 1))
                    split_low(Hlo[:, j], X[:, j], Hhi[:, j]).then_inc(y_lo.sem, 1)
                with dve.Fori(0, KT // 2) as jj:
                    for b in (0, 1):
                        dve.wait_ge(*out_filled.upto(L, jj * 2 + b + 1))
                        dve.wait_ge(*x_back[b].upto(L, jj * 16 + 16))
                        dve.tensor_tensor(tile_of(X, jj * 2 + b), psA[:, b], wk[:, 4 + b], ALU.add)\
                            .then_inc(x_ready.sem, 1)
            counts["d2"] = dve_step.k
            for t in range(NT):
                dve.wait_ge(turned, t + 1)
                if t >= 2:
                    dve.wait_ge(written[t % 2], 16 * (t // 2))
                dve.tensor_copy(wk[:, t % 2], psA[:, t % 2]).then_inc(copied, 1)


def _tiles(v, n):
    return np.ascontiguousarray(v.reshape(n, P).T)


def _panel(w, nk):
    m = w.shape[1]
    return w.reshape(nk, P, m).transpose(1, 0, 2).reshape(P, nk * m)


def _pack1(w_in, w_branch, w_out):
    starts = dict(zip(("aq", "ak", "av", "az", "cx", "cb", "cc", "cz", "rq", "rk", "rv", "rz", "gate"),
                      np.cumsum([0, 512, 512, 512, 512, 512, 512, 512, 512, 256, 256, 512, 512]).tolist()))
    out = []
    for name, nk, m in P1:
        if name[0] == "branch":
            w = w_branch[name[1]][:, name[2] * P:(name[2] + 1) * P]
        elif name[0] == "out":
            w = w_out[:, name[1] * P:(name[1] + 1) * P]
        else:
            c = starts[name[0]] + (name[1] * D_MODEL + name[2] * P if name[0] == "gate" else name[1] * P)
            w = w_in[:, c:c + P]
        out.append(_panel(w, nk))
    return np.concatenate(out, axis=1)


def _pack2(w_in, w_uq, w_ukv, w_out):
    starts = dict(zip(("a", "g", "zc", "cq", "ckv", "kr", "zm", "u", "v", "zs"),
                      np.cumsum([0, 256, 256, 256, 768, 256, 32, 512, 256, 256]).tolist()))
    out = []
    for name, nk, m in P2:
        i = name[1]
        if name[0] == "q":
            w = w_uq[:, i * M_QK:(i + 1) * M_QK]
        elif name[0] == "kv":
            w = w_ukv[:, i * P:(i + 1) * P]
        elif name[0] == "out":
            w = w_out[:, i * P:(i + 1) * P]
        elif name[0] == "kr":
            c = starts["kr"]
            w = w_in[i * 512:(i + 1) * 512, c - M_NOPE:c + M_ROPE]
        else:
            c = starts[name[0]] + i * P
            w = w_in[:, c:c + P]
        out.append(_panel(w, nk))
    return np.concatenate(out, axis=1)


def _tables():
    f = np.float32
    t = np.zeros((P, K.n), f)
    idx = np.arange(P)
    t[:, K.ident:K.ident + P] = np.eye(P)
    t[:, K.ones:K.ones + P] = 1
    t[:, K.mask:K.mask + P] = np.where(idx[None, :] <= idx[:, None], 0.0, NEG)
    for col, size, half in ((K.swapa, 64, 8), (K.swapr, 64, 32)):
        for m in range(P):
            r = m % size
            if r < 2 * half:
                t[m - r + (r + half) % (2 * half), col + m] = 1
    for r in range(M_ROPE):
        t[M_NOPE + (r + 16) % 32, K.swapm + r] = 1
    t[:, K.causal:K.causal + P] = idx[:, None] <= idx[None, :]
    log_g = np.log(f(1.0) - f(2.0) ** (f(-5.0) - np.arange(HEADS, dtype=f))).astype(f)
    diff = (idx[None, :] - idx[:, None]).astype(f)
    scale = f(A_QK ** -0.5)
    pos = idx.astype(f)
    for h in range(HEADS):
        t[:, K.dmask + h * P:K.dmask + (h + 1) * P] = np.where(diff >= 0, np.exp(np.maximum(diff, 0) * log_g[h]), 0) * scale
        rows, pr = slice((h % 2) * 64, (h % 2 + 1) * 64), h // 2
        t[rows, K.xi + pr * P:K.xi + (pr + 1) * P] = np.exp((pos + 1) * log_g[h])[None]
        t[rows, K.zeta + pr * P:K.zeta + (pr + 1) * P] = (np.exp((R_CHUNK - 1 - pos) * log_g[h]) * scale)[None]
        t[rows, K.decay + pr] = np.exp(f(R_CHUNK) * log_g[h])
    pos = np.arange(SEQ, dtype=f)
    ropes = np.zeros((3, P, 2, SEQ), f)
    ropes[:, :, 0] = 1
    inv_a = f(500000.0) ** (-np.arange(0, 16, 2, dtype=f) / f(16))
    inv_r = f(1.0) / (f(10000.0) ** np.linspace(0.0, 1.0, 32, dtype=f))
    inv_m = f(10000.0) ** (-np.arange(16, dtype=f) / f(16))
    for n, inv, half, size, base in ((0, inv_a, 8, 64, 0), (1, inv_r, 32, 64, 0), (2, inv_m, 16, 128, 64)):
        ang = (pos[None, :] * inv[:, None].astype(f)).astype(f)
        for m in range(P):
            r = (m - base) % size
            if m >= base and r < 2 * half:
                ropes[n, m, 0] = np.cos(ang[r % half])
                ropes[n, m, 1] = np.sin(ang[r % half]) * (-1 if r < half else 1)
    return t, ropes


def _params1(norm_g, attn_subln_g, conv_w):
    out = np.zeros((DEPTH, P, C1.n), np.float32)
    for l in range(DEPTH):
        out[l, :, C1.norm:C1.norm + KT] = _tiles(norm_g[l], KT)
        out[l, :, C1.subln] = attn_subln_g[l]
        for k in range(3):
            out[l, :, C1.conv + 4 * k:C1.conv + 4 * k + 4] = _tiles(conv_w[l, k], 4)
        lam_init = 0.8 - 0.6 * np.exp(-0.3 * l)
        out[l, :, C1.lam_init] = lam_init
        out[l, :, C1.lam_rest] = 1.0 - lam_init
    return out


def _params2(norm_g, conv_w, conv_b, cln_g, cln_b, pwb, qn, kvn, qg, kg, sln_g, sln_b, bn):
    out = np.zeros((DEPTH, P, C2.n), np.float32)
    for l in range(DEPTH):
        o = out[l]
        o[:, C2.norm:C2.norm + 8] = _tiles(norm_g[l], 8)
        for k in range(CONV_K):
            o[:, C2.conv_w + 2 * k:C2.conv_w + 2 * k + 2] = _tiles(conv_w[l, k], 2)
        for col, v in ((C2.conv_b, conv_b), (C2.cln_g, cln_g), (C2.cln_b, cln_b), (C2.pwb, pwb),
                       (C2.sln_g, sln_g), (C2.sln_b, sln_b)):
            o[:, col:col + 2] = _tiles(v[l], 2)
        o[:, C2.qn:C2.qn + 6] = _tiles(qn[l], 6)
        o[:, C2.kvn:C2.kvn + 2] = _tiles(kvn[l], 2)
        o[:M_QK, C2.qg] = qg[l]
        o[:M_QK, C2.kg] = kg[l]
        o[:, C2.bn:C2.bn + 8] = _tiles(bn[l], 8)
    return out


def kernel(x, norm_g, w_in, attn_lambda, attn_subln_g, conv_w, w_branch, w_out, final_norm_g, norm_g_2,
           w_in_2, conv_w_2, conv_b_2, conv_ln_g_2, conv_ln_b_2, conv_pw_w_2, conv_pw_b_2, q_norm_g_2,
           w_uq_2, kv_norm_g_2, w_ukv_2, qk_q_g_2, qk_k_g_2, sg_ln_g_2, sg_ln_b_2, sg_w_2, sg_b_2,
           branch_norm_g_2, w_out_2):
    import concourse.bacc as bacc
    from concourse.bass_utils import run_bass_kernel_spmd

    def n(a):
        return np.asarray(a)

    consts, ropes = _tables()
    arrays = {
        "x": n(x)[0],
        "w1": np.stack([_pack1(n(w_in)[l], n(w_branch)[l], n(w_out)[l]) for l in range(DEPTH)]),
        "par1": _params1(n(norm_g), n(attn_subln_g), n(conv_w)),
        "lamv": n(attn_lambda).reshape(DEPTH, 4 * A_QK),
        "finalg": _tiles(n(final_norm_g), KT),
        "w2": np.stack([_pack2(n(w_in_2)[l], n(w_uq_2)[l], n(w_ukv_2)[l], n(w_out_2)[l]) for l in range(DEPTH)]),
        "par2": _params2(n(norm_g_2), n(conv_w_2), n(conv_b_2), n(conv_ln_g_2), n(conv_ln_b_2), n(conv_pw_b_2),
                         n(q_norm_g_2), n(kv_norm_g_2), n(qk_q_g_2), n(qk_k_g_2), n(sg_ln_g_2), n(sg_ln_b_2),
                         n(branch_norm_g_2)),
        "pww": np.stack([_panel(n(conv_pw_w_2)[l], 2) for l in range(DEPTH)]),
        "sgw": np.ascontiguousarray(n(sg_w_2).transpose(0, 2, 1, 3)),
        "sgb": n(sg_b_2),
        "consts": consts,
        "ropes": ropes,
    }
    arrays = {f"in_{k}": np.ascontiguousarray(v) for k, v in arrays.items()}

    def program(per1, per2):
        nc = bacc.Bacc("TRN2", target_bir_lowering=False, num_devices=1)
        args = {k[3:]: nc.dram_tensor(k, v.shape, F32, kind="ExternalInput").ap() for k, v in arrays.items()}
        out = nc.dram_tensor("out", (SEQ, D_MODEL), F32, kind="ExternalOutput").ap()
        xs = nc.dram_tensor("xs", (KT, P, SEQ), F32, kind="Internal").ap()
        return nc, build(nc, per1, per2, out=out, xs=xs, **args)

    _, counted = program({}, {})
    nc, _ = program(counted, counted)
    r = run_bass_kernel_spmd(nc, [arrays], core_ids=[0])
    return r.results[0]["out"].reshape(1, SEQ, D_MODEL)
```

```python
from contextlib import ExitStack

import numpy as np
import concourse.bass as bass
from concourse import mybir

F32 = mybir.dt.float32
F32R = mybir.dt.float32r
BF16 = mybir.dt.bfloat16
ALU = mybir.AluOpType
ACT = mybir.ActivationFunctionType
AX_X = mybir.AxisListType.X


class Group:
    pass


P = 128
SEQ, D_MODEL, DEPTH = 1024, 1024, 2
KT = D_MODEL // P
NT = SEQ // P
HALF = SEQ // 2
EPS = 1e-6
NEG = -1e30

HEADS = 4
A_QK = 64
B1_TILES = 4
R_CHUNK = 128
M_HEADS, M_NOPE, M_ROPE, M_V = 8, 64, 32, 64
M_QK = M_NOPE + M_ROPE
Q_LORA_T, KV_LORA_T = 6, 2
CONV_K = 31
PAD = CONV_K - 1


B1_PRELUDE = [("q", 0, 0), ("q", 0, 1), ("sq", 0, 0), ("k", 0, 0), ("sq", 0, 1), ("k", 0, 1), ("sk", 0, 0),
              ("sk", 0, 1), ("v", 0, 0), ("v", 0, 1)]
B1_SLOTS = [([("vt", 0, 0)], [("q", 1, 0)]),
            ([("vt", 0, 1)], [("q", 1, 1)]),
            ([("sq", 1, 0)], [("k", 1, 0), ("ss", -1, 1)]),
            ([], [("sq", 1, 1), ("k", 1, 1)]),
            ([("sk", 1, 0)], [("z", 0, 0)]),
            ([("sk", 1, 1)], [("z", 0, 1, False)]),
            ([("v", 1, 0)], [("ss", 0, 0)]),
            ([], [("v", 1, 1), ("z", 0, 1, True)])]
B2_PRELUDE = [("q", 0, 0), ("q", 0, 1), ("sq", 0, 0), ("kv", 0, 0), ("sq", 0, 1), ("kv", 0, 1), ("st", 0, 0),
              ("vt", 0, 0), ("kb", 0, 0), ("kb", 0, 1)]
B2_SLOTS = [([("q", 1, 0)], [("q", 1, 1)]),
            ([("sq", 1, 0)], [("kv", 1, 0)]),
            ([("sq", 1, 1)], [("kv", 1, 1)]),
            ([("st", 1, 0)], [("vt", 1, 0)]),
            ([], [("kb", 1, 0)]),
            ([("kb", 1, 1)], []),
            ([], []),
            ([], [])]


def pieces(slots, heads, h, q, after):
    return [(p[0], h + p[1], p[2]) for p in slots[q][after]
            if 0 <= h + p[1] < heads and (len(p) == 3 or p[3] == (h == heads - 1))]


def all_pieces(prelude, slots, heads):
    out = list(prelude)
    for h in range(heads):
        for q in range(NT):
            out += pieces(slots, heads, h, q, 0) + pieces(slots, heads, h, q, 1)
    return out


def panels_of_block1():
    out = []
    for kind, h, half in all_pieces(B1_PRELUDE, B1_SLOTS, HEADS):
        if kind in ("q", "k", "v", "z") and half == 0:
            out += [(("a" + kind, h), KT, P)]
    out += merge_panels(0)
    for t in range(B1_TILES):
        out += [(("cx", t), KT, P), (("cc", t), KT, P), (("cb", t), KT, P), (("cz", t), KT, P)]
    out += merge_panels(1)
    for pr in range(HEADS // 2):
        out += [(("rq", pr), KT, P), (("rk", pr), KT, P)]
        for h in (2 * pr, 2 * pr + 1):
            out += [(("rv", h), KT, P), (("rz", h), KT, P)]
    out += merge_panels(2)
    out += [(("out", j), KT, P) for j in range(KT)]
    return out


def merge_panels(i):
    out = []
    for j in range(KT):
        out += [(("gate", i, j), KT, P), (("branch", i, j), B1_TILES, P)]
    return out


def panels_of_block2():
    out = []
    for t in (0, 1):
        out += [(("g", t), KT, P), (("a", t), KT, P)]
    for n in ("v", "u", "zs", "zc"):
        out += [((n, t), KT, P) for t in (0, 1)]
    out += [(("cq", t), KT, P) for t in range(Q_LORA_T)]
    out += [(("ckv", t), KT, P) for t in range(KV_LORA_T)]
    out += [(("kr", 0), KT // 2, M_QK), (("kr", 1), KT // 2, M_QK)]
    out += [(("zm", t), KT, P) for t in range(4)]
    for h in range(M_HEADS):
        out += [(("q", h), Q_LORA_T, M_QK), (("kv", h), KV_LORA_T, P)]
    out += [(("out", j), KT, P) for j in range(KT)]
    return out


def runs(panels):
    out, off = [], 0
    for p in range(0, len(panels), 2):
        sizes = [panels[p + b][1] * panels[p + b][2] for b in (0, 1)]
        if out and out[-1][2] == sizes:
            out[-1][1] += 1
        else:
            out.append([p, 1, sizes, off])
        off += sum(sizes)
    return out, off


def uses_of_block1():
    a = [("s", h, q, c) for h in range(HEADS) for q in range(NT) for c in (0, 1)]
    t = []
    a += [x[0] for x in merge_panels(0)]
    for c in range(B1_TILES):
        a += [("cx", c), ("cc", c), ("cb", c), ("cz", c)]
    a += [x[0] for x in merge_panels(1)]
    for pr in range(HEADS // 2):
        a += [("rq", pr), ("rk", pr)]
        t += [("swaprq", pr), ("swaprk", pr), ("ks", pr)]
        for h in (2 * pr, 2 * pr + 1):
            a += [("rv", h), ("rz", h), ("rs", h), ("ro", h)]
            t += [("rvt", h), ("kv", h), ("rss", h)]
    a += [x[0] for x in merge_panels(2)]
    return a, t


def uses_of_block2():
    a = []
    for c in (0, 1):
        a += [("g", c), ("a", c)]
    a += [(n, c) for n in ("v", "u", "zs", "zc") for c in (0, 1)]
    a += [("cq", 0), ("cq", 1), ("pw", 0), ("pw", 1), ("cq", 2), ("cq", 3), ("sg", 0), ("sg", 1), ("cq", 4), ("cq", 5)]
    a += [("ckv", 0), ("ckv", 1)] + [("zm", c) for c in range(4)]
    t = ["cmean", "smean", "cvar", "svar", "cbn", ("vst", 0), ("vst", 1), "wgt", "sbn", "cqs", "kr", "ckvs",
         "krswap", "mbn"]
    a += [("s", h, q) for h in range(M_HEADS) for q in range(NT)]
    return a, t


def uses_of_attention(prelude, slots, heads):
    tp = [(h, q) for h in range(heads) for q in range(NT)]
    av = [(h, g) for h in range(heads) for g in (0, 1)]
    f = all_pieces(prelude, slots, heads)
    if ("ss", heads - 2, 1) in f:
        f.append(("ss", heads - 1, 1))
    return tp, av, f


class Ring:

    def __init__(self, name, uses, sem, buffers=2):
        assert len(uses) % buffers == 0, (name, len(uses))
        self.n, self.buffers = len(uses), buffers
        self.at = {u: i for i, u in enumerate(uses)}
        self.filled_sem = sem(f"{name}_filled")
        self.drained_sem = [sem(f"{name}{b}_drained") for b in range(buffers)]

    def buf(self, use):
        return self.at[use] % self.buffers

    def filled(self, L, use, j=0):
        return self.filled_sem, L * self.n + self.at[use] + 1 + 2 * j

    def drained(self, L, use, j=0):
        u = self.at[use]
        return self.drained_sem[u % self.buffers], L * (self.n // self.buffers) + u // self.buffers + 1 + j

    def before(self, use):
        return self.at[use] >= self.buffers

    def room(self, L, use, j=0):
        u = self.at[use]
        return self.drained_sem[u % self.buffers], L * (self.n // self.buffers) + u // self.buffers + j

    def freed(self, use):
        return self.drained_sem[self.at[use] % self.buffers]


class Tally:

    def __init__(self, sem, per_layer, before=0):
        self.sem, self.per, self.before = sem, per_layer, before

    def upto(self, L, k):
        return self.sem, L * self.per + k + self.before


class Chain:

    def __init__(self, sem, per_layer, base=0):
        self.sem, self.per, self.k, self.L, self.base = sem, per_layer, 0, 0, base

    def step(self, eng, ins):
        ins.then_inc(self.sem, 1)
        self.k += 1
        eng.wait_ge(self.sem, self.L * self.per + self.k + self.base)

    def layer(self, L):
        self.k, self.L = 0, L


P1, P2 = panels_of_block1(), panels_of_block2()
PAN1 = {p[0]: i for i, p in enumerate(P1)}
PAN2 = {p[0]: i for i, p in enumerate(P2)}
RUNS1, COLS1 = runs(P1)
RUNS2, COLS2 = runs(P2)

class C1:
    norm = 0
    subln = KT
    conv = KT + 1
    lam_init = KT + 13
    lam_rest = KT + 14
    n = KT + 15


class C2:
    norm = 0
    conv_w = 8
    conv_b = 8 + 62
    cln_g = 72
    cln_b = 74
    pwb = 76
    qn = 78
    kvn = 84
    qg = 86
    kg = 87
    sln_g = 88
    sln_b = 90
    bn = 92
    n = 100


class K:
    ident = 0
    ones = 128
    mask = 256
    swapa = 384
    swapr = 512
    swapm = 640
    causal = 768
    dmask = 896
    xi = 896 + 512
    zeta = 896 + 768
    decay = 896 + 1024
    n = 896 + 1024 + 2


def build(nc, per1, per2, x, w1, par1, lamv, finalg, w2, par2, pww, sgw, sgb, consts, ropes, out, xs):
    counts = {}
    with ExitStack() as top:
        def sem(name):
            return top.enter_context(nc.semaphore(name))

        def sb(name, shape, dt=F32):
            return top.enter_context(nc.sbuf_tensor(name, shape, dt))

        X = sb("X", [P, KT, SEQ])
        Hhi = sb("Hhi", [P, KT, SEQ], F32R)
        Hlo = sb("Hlo", [P, KT, SEQ], F32R)
        stage = sb("stage", [P, 2, KT * P])
        Whi = sb("Whi", [P, 2, KT * P], F32R)
        Wlo = sb("Wlo", [P, 2, KT * P], F32R)
        ident = sb("ident", [P, P])
        ones = sb("ones", [P, P])
        identb = sb("identb", [P, P], BF16)
        maskb = sb("maskb", [P, P], BF16)
        rope = sb("rope", [P, 2, SEQ])
        epsc = sb("epsc", [P, 1])
        psA = top.enter_context(nc.psum_tensor("psA", [P, 2, SEQ], F32))
        psT = top.enter_context(nc.psum_tensor("psT", [P, 2, SEQ], F32))
        env = Group()
        env.nc, env.x, env.w1, env.par1, env.lamv, env.finalg = nc, x, w1, par1, lamv, finalg
        env.w2, env.par2, env.pww, env.sgw, env.sgb, env.consts = w2, par2, pww, sgw, sgb, consts
        env.ropes, env.out, env.xs, env.X, env.Hhi, env.Hlo = ropes, out, xs, X, Hhi, Hlo
        env.stage, env.Whi, env.Wlo, env.ident, env.ones, env.identb = stage, Whi, Wlo, ident, ones, identb
        env.maskb, env.rope, env.epsc, env.psA, env.psT = maskb, rope, epsc, psA, psT
        first_block(env, per1, counts)
        second_block(env, per2, counts)
    return counts


def halves(ps, m=P, lo=0):
    return [ps[lo:lo + m, h * HALF:(h + 1) * HALF] for h in (0, 1)]


def three_pass_half(pe, dst, whi, wlo, rhi, rlo, nk, M, half, begun, arrived=None):
    c = slice(half * HALF, (half + 1) * HALF)
    for k in range(nk):
        if arrived is not None:
            arrived(k)
        cols = slice(k * M, (k + 1) * M)
        for w, r, end in ((whi, rhi, False), (whi, rlo, False), (wlo, rhi, True)):
            mm = pe.matmul(dst[0:M], w[:, cols], r[k][:, c], start=k == 0 and w is whi and r is rhi,
                           stop=k == nk - 1 and end)
            if begun is not None:
                mm.then_inc(begun, 1)
                begun = None
    return mm


def three_pass(pe, ps, whi, wlo, rhi, rlo, nk, M, begun, first=True, last=True, arrived=None,
               order=None):
    dst = halves(ps, M)
    order = order or range(nk)
    for k in order:
        if arrived is not None:
            arrived(k)
        cols = slice(k * M, (k + 1) * M)
        for w, r, end in ((whi, rhi, False), (whi, rlo, False), (wlo, rhi, True)):
            for h in (0, 1):
                mm = pe.matmul(dst[h], w[:, cols], r[k][:, h * HALF:(h + 1) * HALF],
                               start=first and k == order[0] and r is rhi and w is whi,
                               stop=last and k == order[-1] and end)
                if begun is not None:
                    mm.then_inc(begun, 1)
                    begun = None
    return mm


def weight_engines(block, s, w_dram, stage, Whi, Wlo, panels, the_runs, load_inputs):
    NP = len(panels)

    @block.sync
    def _(sp):
        load_inputs(sp)
        with sp.Fori(0, DEPTH) as L:
            for p0, pairs, sizes, off in the_runs:
                with sp.Fori(0, pairs) as i:
                    for b in (0, 1):
                        sp.wait_ge(s.w_split, L * NP + p0 + b + 1 + i * 2)
                        start = off + b * sizes[0] + i * sum(sizes)
                        sp.dma_start(stage[:, b, 0:sizes[b]], w_dram[L, :, bass.ds(start, sizes[b])])\
                            .then_inc(s.w_loaded[b], 16)

    @block.gpsimd
    def _(pool):
        pool.memset(s.credit[:, 0:1], 0.0).then_inc(s.w_split, 2)
        pool.memset(s.credit[:, 1:2], 0.0).then_inc(s.panel_begun, 1)
        pool.wait_ge(s.w_split, 2)
        with pool.Fori(0, DEPTH) as L:
            for p0, pairs, sizes, off in the_runs:
                with pool.Fori(0, pairs) as i:
                    for b in (0, 1):
                        n = sizes[b]
                        pool.wait_ge(s.w_loaded[b], (L * (NP // 2) + p0 // 2 + 1 + i) * 16)
                        pool.wait_ge(s.panel_begun, L * NP + p0 + b + 1 + i * 2)
                        pool.tensor_tensor(Whi[:, b, 0:n], stage[:, b, 0:n], s.credit[:, 0:1].broadcast_to([P, n]),
                                           ALU.add).then_inc(s.w_hi, 1)
                        pool.wait_ge(s.w_hi, L * NP + p0 + b + 1 + i * 2)
                        pool.tensor_tensor(Wlo[:, b, 0:n], stage[:, b, 0:n], Whi[:, b, 0:n].bitcast(F32),
                                           ALU.subtract).then_inc(s.w_split, 1)




def first_block(env, per, counts):
    nc, X, Hhi, Hlo, rope, ident, ones = env.nc, env.X, env.Hhi, env.Hlo, env.rope, env.ident, env.ones
    psA, psT, identb, maskb, epsc = env.psA, env.psT, env.identb, env.maskb, env.epsc
    SCALE = A_QK ** -0.5
    with ExitStack() as ctx:
        def sem(name):
            return ctx.enter_context(nc.semaphore("b1_" + name))

        def sb(name, shape, dt=F32):
            return ctx.enter_context(nc.sbuf_tensor("b1_" + name, shape, dt))

        Bhi = sb("Bhi", [P, B1_TILES, SEQ], F32R)
        Blo = sb("Blo", [P, B1_TILES, SEQ], F32R)
        wk = sb("wk", [P, 8, SEQ])
        upad = sb("upad", [P, SEQ + 2])
        par = sb("par", [P, DEPTH, C1.n])
        cur = sb("cur", [P, C1.n])
        fing = sb("fing", [P, KT])
        lamraw = sb("lamraw", [P, DEPTH, 4 * A_QK])
        lamt = sb("lamt", [P, 2 * A_QK])
        lam = sb("lam", [P, 6])
        gcol = sb("gcol", [P, 1])
        swapa = sb("swapa", [P, P])
        swapr = sb("swapr", [P, P])
        rtab = sb("rtab", [P, K.n - K.dmask])
        rowmax = sb("rowmax", [P, 2])
        negmax = sb("negmax", [P, 2, 2])
        rowsum = sb("rowsum", [P, 2, 2])
        inv = sb("inv", [P, 2, 2])
        credit = sb("credit", [P, 2])

        a_uses, t_uses = uses_of_block1()
        A = Ring("b1A", a_uses, lambda n: ctx.enter_context(nc.semaphore(n)))
        T = Ring("b1T", t_uses, lambda n: ctx.enter_context(nc.semaphore(n)))
        tp, av, f = uses_of_attention(B1_PRELUDE, B1_SLOTS, HEADS)
        TP = Ring("b1TP", tp, lambda n: ctx.enter_context(nc.semaphore(n)), 1)
        AV = Ring("b1AV", av, lambda n: ctx.enter_context(nc.semaphore(n)), 1)
        F = Ring("b1F", f, lambda n: ctx.enter_context(nc.semaphore(n)), 1)
        psTP, psAV, psF = psT[:, 0], psT[:, 1, 0:HALF], psT[:, 1, HALF:]
        NP = len(P1)
        s = Group()
        s.credit, s.w_split, s.w_hi, s.panel_begun = credit, sem("w_split"), sem("w_hi"), sem("panel_begun")
        s.w_loaded = [sem("w_loaded0"), sem("w_loaded1")]
        consts_in, params_in, mask_in = sem("consts_in"), sem("params_in"), sem("mask_in")
        x_in = [sem("x_in0"), sem("x_in1")]
        x_turned, setup = sem("x_turned"), sem("setup")
        rope_in = Tally(sem("rope_in"), 2 * 16)
        x_ready = Tally(sem("x_ready"), KT)
        out_filled = Tally(sem("out_filled"), KT)
        x_saved = Tally(sem("x_saved"), 16)
        x_back = [Tally(sem(f"x_back{b}"), 16 * KT // 2) for b in (0, 1)]
        sq_done, sq_added = Tally(sem("sq_done"), KT), Tally(sem("sq_added"), KT)
        summed, rstd = Tally(sem("summed"), 1), Tally(sem("rstd"), 1)
        h_scaled, h_hi, h_lo = (Tally(sem(n), KT) for n in ("h_scaled", "h_hi", "h_lo"))
        lam_sum, lam_exp = Tally(sem("lam_sum"), 1), Tally(sem("lam_exp"), 1)
        rotated = Tally(sem("rotated"), 4 * HEADS)
        nmax = Tally(sem("nmax"), HEADS * NT)
        mixed = Tally(sem("mixed"), HEADS * NT)
        a_sq, a_rs, a_out = (Tally(sem(n), 2 * HEADS) for n in ("a_sq", "a_rs", "a_out"))
        b_hi, b_lo = (Tally(sem(n), 2 * HEADS + 2 * B1_TILES) for n in ("b_hi", "b_lo"))
        merged = Tally(sem("merged"), 2 * KT)
        c_out = Tally(sem("c_out"), B1_TILES)
        rk_scaled, r_rot = Tally(sem("rk_scaled"), HEADS // 2), Tally(sem("r_rot"), HEADS)
        r_sq, r_rs, r_out = (Tally(sem(n), HEADS) for n in ("r_sq", "r_rs", "r_out"))
        m_hi, m_lo = Tally(sem("m_hi"), KT), Tally(sem("m_lo"), KT)
        f_sum, f_rs = sem("f_sum"), sem("f_rs")
        dve_step = Chain(sem("dve_step"), per.get("d1", 1), 2)
        act_step = Chain(sem("act_step"), 1)

        AQ, AK, AVAL, Z = [wk[:, 0], wk[:, 4]], [wk[:, 1], wk[:, 5]], [wk[:, 2], wk[:, 6]], wk[:, 3]
        RAW = wk[:, 7]
        WT = X[:, 0:4].rearrange("p a b -> p (a b)").rearrange("p (k q) -> p k q", k=NT)
        PR = [[X[:, 4], X[:, 5]], [X[:, 6], X[:, 7]]]
        TMP, ROT = upad[:, 2:2 + HALF], upad[:, 2 + HALF:]
        SQSUM = wk[:, 7]
        Q, KK, V, R_ROT = wk[:, 0], wk[:, 1], wk[:, 2], wk[:, 7]
        RSQ, R_RAWQ, R_RAWK, R_RAWV = upad[:, 2:], wk[:, 4], wk[:, 5], wk[:, 6]
        KZ, SM, KS, ST, QX = wk[:, 4], wk[:, 4], wk[:, 5], wk[:, 6], wk[:, 7]
        DM = rtab[:, 0:HEADS * P].rearrange("p (h c) -> p h c", h=HEADS)
        XI = rtab[:, K.xi - K.dmask:K.zeta - K.dmask].rearrange("p (h c) -> p h c", h=2)
        ZE = rtab[:, K.zeta - K.dmask:K.decay - K.dmask].rearrange("p (h c) -> p h c", h=2)
        DEC = rtab[:, K.decay - K.dmask:]
        x_tiles = env.x.rearrange("(t p) d -> t p d", p=P)
        xs_v = env.xs.rearrange("j p n -> p j n")

        def by_chunk(ap):
            return ap.rearrange("p (n c) -> p n c", n=NT)

        def every_chunk(ap):
            return ap.unsqueeze(1).broadcast_to([ap.shape[0], NT, ap.shape[1]])

        def tile_of(ap, j):
            return ap[:, bass.ds(j, 1), :].rearrange("p a b -> p (a b)")

        def head_rows(h):
            return slice((h % 2) * A_QK, (h % 2 + 1) * A_QK)

        block = ctx.enter_context(nc.Block())

        def load_inputs(sp):
            for k, dst in ((K.ident, ident), (K.ones, ones), (K.swapa, swapa), (K.swapr, swapr)):
                sp.dma_start(dst[:], env.consts[:, k:k + P]).then_inc(consts_in, 16)
            sp.dma_start(wk[:, 0, 0:P], env.consts[:, K.mask:K.mask + P]).then_inc(mask_in, 16)
            for t in range(NT):
                if t >= 2:
                    sp.wait_ge(x_turned, t - 1)
                sp.dma_start(wk[:, 2 + t % 2], x_tiles[t]).then_inc(x_in[t % 2], 16)
            sp.dma_start(rtab[:], env.consts[:, K.dmask:K.n]).then_inc(params_in, 16)
            sp.dma_start(par[:], env.par1.rearrange("l p c -> p l c")).then_inc(params_in, 16)
            sp.dma_start(fing[:], env.finalg).then_inc(params_in, 16)
            sp.dma_start(lamraw[:], env.lamv.rearrange("l c -> (l c)").partition_broadcast(P)
                         .rearrange("p (l c) -> p l c", l=DEPTH)).then_inc(params_in, 16)

        weight_engines(block, s, env.w1, env.stage, env.Whi, env.Wlo, P1, RUNS1, load_inputs)

        @block.tensor
        def _(pe):
            def panel(L, name, rhi, rlo, nk=KT, j=0, arrived=None):
                p = PAN1[name]
                pe.wait_ge(s.w_split, L * NP + p + 3 + j * 2)
                if name[0] == "out":
                    pe.wait_ge(*x_ready.upto(L + 1, name[1] - 1 + j * 2))
                    dst, done = psA[:, name[1] % 2], out_filled.sem
                else:
                    if A.before(name):
                        pe.wait_ge(*A.room(L, name, j))
                    dst, done = psA[:, A.buf(name)], A.filled_sem
                three_pass(pe, dst, env.Whi[:, p % 2], env.Wlo[:, p % 2], [rhi[:, k] for k in range(nk)],
                           [rlo[:, k] for k in range(nk)], nk, P, s.panel_begun, arrived=arrived).then_inc(done, 1)

            def full(dst, lhsT, rhs, start=True, stop=True):
                for h in (0, 1):
                    c = slice(h * HALF, (h + 1) * HALF)
                    mm = pe.matmul(dst[:, c], lhsT, rhs[:, c], start=start, stop=stop)
                return mm

            def turn(dst, src, blocks):
                for i in range(blocks):
                    mm = pe.transpose(dst[:, i * P:(i + 1) * P], src[:, i * P:(i + 1) * P], ident[:])
                return mm

            def swap(L, use, raw, mat, raw_tile):
                pe.wait_ge(*A.drained(L, raw))
                if T.before(use):
                    pe.wait_ge(*T.room(L, use))
                full(psT[:, T.buf(use)], mat[:], raw_tile).then_inc(T.filled_sem, 1)

            def scores(L, h, q):
                for c in (0, 1):
                    use = ("s", h, q, c)
                    if A.before(use):
                        pe.wait_ge(*A.room(L, use))
                    if q == 0 and c == 0:
                        pe.wait_ge(*rotated.upto(L, 4 * h + 4))
                    dst, rows = psA[:, A.buf(use)], slice(c * A_QK, (c + 1) * A_QK)
                    n = (q + 1) * P
                    for k0 in range(0, n, HALF):
                        k1 = min(n, k0 + HALF)
                        pe.matmul(dst[:, k0:k1], AQ[h % 2][rows, q * P:n], AK[h % 2][rows, k0:k1], start=True,
                                  stop=k1 < n)
                    pe.matmul(dst[:, q * P:n], identb[:], maskb[:], start=False, stop=True)\
                        .then_inc(A.filled_sem, 1)

            def piece(L, use):
                def arrived(k):
                    pe.wait_ge(*h_hi.upto(L, k + 1))
                    pe.wait_ge(*h_lo.upto(L, k + 1))

                kind, h, half = use
                c = slice(half * HALF, (half + 1) * HALF)
                if kind in ("q", "k", "v", "z"):
                    p = PAN1[("a" + kind, h)]
                    pe.wait_ge(s.w_split, L * NP + p + 3)
                if F.before(use):
                    pe.wait_ge(*F.room(L, use))
                if kind in ("q", "k", "v", "z"):
                    mm = three_pass_half(pe, psF, env.Whi[:, p % 2], env.Wlo[:, p % 2],
                                         [Hhi[:, k] for k in range(KT)], [Hlo[:, k] for k in range(KT)], KT, P,
                                         half, None if half else s.panel_begun, arrived if use == B1_PRELUDE[0] else None)
                elif kind in ("sq", "sk"):
                    mm = pe.matmul(psF, swapa[:], RAW[:, c], start=True, stop=True)
                elif kind == "vt":
                    mm = turn(psF, RAW[:, c], NT // 2)
                else:
                    pe.wait_ge(*a_sq.upto(L, 2 * h + half + 1))
                    mm = pe.matmul(psF, ones[:], TMP, start=True, stop=True)
                mm.then_inc(F.filled_sem, 1)

            def values(L, h, g):
                pe.wait_ge(*TP.drained(L, (h, 4 * g + 3)))
                pe.wait_ge(*F.drained(L, ("vt", h, 1)))
                if AV.before((h, g)):
                    pe.wait_ge(*AV.room(L, (h, g)))
                for k in range(4 * g + 4):
                    c0 = max(0, k - 4 * g) * P
                    mm = pe.matmul(psAV[:, c0:], AVAL[h % 2][:, k * P:(k + 1) * P], WT[:, k, c0:],
                                   start=k == 0, stop=k == 4 * g + 3)
                mm.then_inc(AV.filled_sem, 1)

            def attention(L):
                for use in B1_PRELUDE:
                    piece(L, use)
                scores(L, 0, 0)
                for h in range(HEADS):
                    for q in range(NT):
                        if q + 1 < NT:
                            scores(L, h, q + 1)
                        elif h + 1 < HEADS:
                            scores(L, h + 1, 0)
                        for use in pieces(B1_SLOTS, HEADS, h, q, 0):
                            piece(L, use)
                        if q == 4:
                            values(L, h, 0)
                        if q == 0 and h:
                            values(L, h - 1, 1)
                        if TP.before((h, q)):
                            pe.wait_ge(*TP.room(L, (h, q)))
                        pe.wait_ge(*mixed.upto(L, h * NT + q + 1))
                        turn(psTP, PR[q % 2][0], q + 1).then_inc(TP.filled_sem, 1)
                        for use in pieces(B1_SLOTS, HEADS, h, q, 1):
                            piece(L, use)
                values(L, HEADS - 1, 1)
                piece(L, ("ss", HEADS - 1, 1))

            def merge(L, i):
                with pe.Fori(0, KT) as j:
                    panel(L, ("gate", i, 0), Hhi, Hlo, j=j)
                    pe.wait_ge(*b_lo.upto(L, (8, 12, 16)[i]))
                    pe.wait_ge(*b_hi.upto(L, (8, 12, 16)[i]))
                    panel(L, ("branch", i, 0), Bhi, Blo, B1_TILES, j=j)

            def retain(L, pr, h):
                rows = head_rows(h)
                if h % 2 == 0:
                    use = ("ks", pr)
                    pe.wait_ge(*rk_scaled.upto(L, pr + 1))
                    pe.wait_ge(*T.room(L, use))
                    turn(psT[:, T.buf(use)], KZ, NT).then_inc(T.filled_sem, 1)
                use = ("rvt", h)
                pe.wait_ge(*A.drained(L, ("rv", h)))
                pe.wait_ge(*T.room(L, use))
                turn(psT[:, T.buf(use)], R_RAWV, NT).then_inc(T.filled_sem, 1)
                use = ("rs", h)
                pe.wait_ge(*r_rot.upto(L, 2 * pr + 2))
                pe.wait_ge(*A.room(L, use))
                for n in range(NT):
                    c = slice(n * P, (n + 1) * P)
                    mm = pe.matmul(psA[:, A.buf(use), c], KK[rows, c], Q[rows, c], start=True, stop=True)
                mm.then_inc(A.filled_sem, 1)
                use = ("kv", h)
                pe.wait_ge(*T.drained(L, ("rvt", h)))
                pe.wait_ge(*T.drained(L, ("ks", pr)))
                pe.wait_ge(*T.room(L, use))
                for n in range(NT - 1):
                    mm = pe.matmul(psT[rows, T.buf(use), n * P:(n + 1) * P],
                                   KS[:, n * P + (h % 2) * A_QK:n * P + (h % 2 + 1) * A_QK],
                                   V[:, n * P:(n + 1) * P], start=True, stop=True)
                mm.then_inc(T.filled_sem, 1)
                use = ("ro", h)
                pe.wait_ge(*A.room(L, use))
                pe.wait_ge(*A.drained(L, ("rs", h)))
                pe.wait_ge(*T.drained(L, ("kv", h)))
                for n in range(NT):
                    c = slice(n * P, (n + 1) * P)
                    mm = pe.matmul(psA[:, A.buf(use), c], V[:, c], SM[:, c], start=True, stop=n == 0)
                    if n:
                        mm = pe.matmul(psA[:, A.buf(use), c], ST[rows, c], QX[rows, c], start=False, stop=True)
                mm.then_inc(A.filled_sem, 1)
                use = ("rss", h)
                pe.wait_ge(*r_sq.upto(L, h + 1))
                pe.wait_ge(*T.room(L, use))
                full(psT[:, T.buf(use)], ones[:], RSQ).then_inc(T.filled_sem, 1)

            pe.wait_ge(consts_in, 64)
            for t in range(NT):
                pe.wait_ge(x_in[t % 2], 16 * (t // 2 + 1))
                if t >= 2:
                    pe.wait_ge(x_ready.sem, t - 1)
                turn(psA[:, t % 2], wk[:, 2 + t % 2], KT).then_inc(x_turned, 1)
            pe.wait_ge(setup, 1)

            with pe.Fori(0, DEPTH) as L:
                pe.wait_ge(*sq_added.upto(L, KT))
                full(psT[:, 0], ones[:], SQSUM).then_inc(summed.sem, 1)
                attention(L)
                merge(L, 0)
                for c in range(B1_TILES):
                    for n in ("cx", "cc", "cb", "cz"):
                        panel(L, (n, c), Hhi, Hlo)
                merge(L, 1)
                for pr in range(HEADS // 2):
                    panel(L, ("rq", pr), Hhi, Hlo)
                    panel(L, ("rk", pr), Hhi, Hlo)
                    swap(L, ("swaprq", pr), ("rq", pr), swapr, R_RAWQ)
                    swap(L, ("swaprk", pr), ("rk", pr), swapr, R_RAWK)
                    for h in (2 * pr, 2 * pr + 1):
                        panel(L, ("rv", h), Hhi, Hlo)
                        panel(L, ("rz", h), Hhi, Hlo)
                        retain(L, pr, h)
                merge(L, 2)
                def arrived(k):
                    pe.wait_ge(*m_hi.upto(L, k + 1))
                    pe.wait_ge(*m_lo.upto(L, k + 1))

                with pe.Fori(0, KT // 2) as jj:
                    for b in (0, 1):
                        panel(L, ("out", b), Hhi, Hlo, j=jj, arrived=arrived)

            pe.wait_ge(*sq_added.upto(DEPTH, KT))
            full(psT[:, 0], ones[:], SQSUM).then_inc(summed.sem, 1)

        @block.scalar
        def _(act):
            def root(L, use, dst, mean, done, cols=SEQ):
                act.wait_ge(*T.filled(L, use))
                act.activation(dst, psT[:, T.buf(use), 0:cols], ACT.Ln, bias=epsc[:, 0:1], scale=mean)\
                    .then_inc(T.freed(use), 1)
                act.wait_ge(*T.drained(L, use))
                act.activation(dst, dst, ACT.Exp, scale=-0.5).then_inc(done, 1)

            def take(L, use, dst, func=ACT.Copy, j=0):
                act.wait_ge(*A.filled(L, use, j))
                act.activation(dst, psA[:, A.buf(use)], func).then_inc(A.freed(use), 1)

            def exps(L, h, q):
                act.wait_ge(*nmax.upto(L, h * NT + q + 1))
                n = (q + 1) * P
                for c in (0, 1):
                    use = ("s", h, q, c)
                    act.activation(PR[q % 2][c][:, 0:n], psA[:, A.buf(use), 0:n], ACT.Exp,
                                   bias=negmax[:, q % 2, c:c + 1], scale=SCALE,
                                   accum_out=rowsum[:, q % 2, c:c + 1]).then_inc(A.freed(use), 1)

            def piece(L, use):
                kind, h, half = use
                c = slice(half * HALF, (half + 1) * HALF)
                if kind in ("q", "k", "v"):
                    act.wait_ge(*F.filled(L, use))
                    if kind != "q":
                        act.wait_ge(*rotated.upto(L, 4 * h + half + (1 if kind == "k" else 3)))
                    act.activation(RAW[:, c], psF, ACT.Copy).then_inc(F.freed(use), 1)
                elif kind == "z":
                    act.wait_ge(*F.filled(L, use))
                    if h:
                        act.wait_ge(*a_out.upto(L, 2 * h - 1 + half))
                    act.activation(Z[:, c], psF, ACT.Silu).then_inc(F.freed(use), 1)
                elif kind == "ss":
                    n = 2 * h + half
                    act.wait_ge(*F.filled(L, use))
                    act.activation(TMP, psF, ACT.Ln, bias=epsc[:, 0:1], scale=1.0 / P).then_inc(F.freed(use), 1)
                    act.wait_ge(*F.drained(L, use))
                    act.activation(TMP, TMP, ACT.Exp, scale=-0.5).then_inc(a_rs.sem, 1)

            def split(L, h, half):
                c = slice(half * HALF, (half + 1) * HALF)
                act.wait_ge(*a_out.upto(L, 2 * h + half + 1))
                act.activation(Bhi[:, h, c], TMP, ACT.Copy).then_inc(b_hi.sem, 1)

            def values(L, h, g):
                act.wait_ge(*AV.filled(L, (h, g)))
                if (h, g) != (0, 0):
                    act.wait_ge(*b_lo.upto(L, 2 * h + g))
                act.activation(TMP, psAV, ACT.Square).then_inc(a_sq.sem, 1)

            def attention(L):
                for use in B1_PRELUDE:
                    piece(L, use)
                exps(L, 0, 0)
                late = []
                for h in range(HEADS):
                    for q in range(NT):
                        if q + 1 < NT:
                            exps(L, h, q + 1)
                        elif h + 1 < HEADS:
                            exps(L, h + 1, 0)
                        for use in late:
                            piece(L, use)
                        for use in pieces(B1_SLOTS, HEADS, h, q, 0):
                            piece(L, use)
                        if q == 4:
                            values(L, h, 0)
                        if q == 0 and h:
                            values(L, h - 1, 1)
                        act.wait_ge(*TP.filled(L, (h, q)))
                        act.activation(WT[:, 0:q + 1, (q % 4) * P:(q % 4 + 1) * P],
                                       psTP[:, 0:(q + 1) * P].rearrange("p (k c) -> p k c", c=P),
                                       ACT.Copy).then_inc(TP.freed((h, q)), 1)
                        for _, head, half in late:
                            split(L, head, half)
                        late = []
                        for use in pieces(B1_SLOTS, HEADS, h, q, 1):
                            if use[0] == "ss":
                                late.append(use)
                            else:
                                piece(L, use)
                values(L, HEADS - 1, 1)
                piece(L, ("ss", HEADS - 1, 1))
                split(L, HEADS - 1, 1)

            def gates(L, i):
                with act.Fori(0, KT // 2) as jj:
                    for b in (0, 1):
                        use = ("gate", i, b)
                        act.wait_ge(*A.drained(L, ("branch", i, 0), jj * 2 + b - 2))
                        act.wait_ge(*A.filled(L, use, jj * 2))
                        act.activation(wk[:, b], psA[:, A.buf(use)], ACT.Sigmoid).then_inc(A.freed(use), 1)

            for t in range(NT):
                act.wait_ge(x_ready.sem, t + 1)
                if t >= 2:
                    act.wait_ge(sq_added.sem, t - 1)
                act.activation(by_chunk(wk[:, 4 + t % 2]), X[:, :, t * P:(t + 1) * P], ACT.Square)\
                    .then_inc(sq_done.sem, 1)
            with act.Fori(0, DEPTH) as L:
                act_step.layer(L)
                act.wait_ge(*x_ready.upto(L, KT))
                act.dma_start(xs_v, X[:]).then_inc(x_saved.sem, 16)
                act.dma_start(rope[:], env.ropes[0]).then_inc(rope_in.sem, 16)
                act.wait_ge(*summed.upto(L, 1))
                act_step.step(act, act.activation(wk[:, 2], psT[:, 0], ACT.Ln, bias=epsc[:, 0:1],
                                                  scale=1.0 / D_MODEL))
                act.activation(wk[:, 2], wk[:, 2], ACT.Exp, scale=-0.5).then_inc(rstd.sem, 1)
                for j in range(KT):
                    act.wait_ge(*h_scaled.upto(L, j + 1))
                    act.activation(Hhi[:, j], X[:, j], ACT.Copy).then_inc(h_hi.sem, 1)
                act.wait_ge(*h_lo.upto(L, KT))
                act.wait_ge(*lam_sum.upto(L, 1))
                act.activation(lam[:, 2:4], lam[:, 0:2], ACT.Exp).then_inc(lam_exp.sem, 1)
                attention(L)
                act.wait_ge(*rotated.upto(L, 4 * HEADS))
                act.dma_start(rope[:], env.ropes[1]).then_inc(rope_in.sem, 16)
                gates(L, 0)
                for c in range(B1_TILES):
                    if c:
                        act.wait_ge(*A.drained(L, ("cc", c - 1)))
                    take(L, ("cx", c), wk[:, 4])
                    if c:
                        act.wait_ge(*c_out.upto(L, c))
                    take(L, ("cb", c), wk[:, 5])
                    take(L, ("cz", c), wk[:, 6], ACT.Silu)
                    act.wait_ge(*c_out.upto(L, c + 1))
                    act.activation(Bhi[:, c], wk[:, 7], ACT.Copy).then_inc(b_hi.sem, 1)
                gates(L, 1)
                act.wait_ge(*merged.upto(L, KT))
                for pr in range(HEADS // 2):
                    take(L, ("rq", pr), R_RAWQ)
                    take(L, ("rk", pr), R_RAWK)
                    for h in (2 * pr, 2 * pr + 1):
                        take(L, ("rv", h), R_RAWV)
                        if h:
                            act.wait_ge(*r_out.upto(L, h))
                        take(L, ("rz", h), Z, ACT.Silu)
                        if h % 2 == 0:
                            act.wait_ge(*T.filled(L, ("ks", pr)))
                            act.activation(KS, psT[:, T.buf(("ks", pr))], ACT.Copy).then_inc(T.freed(("ks", pr)), 1)
                        use = ("ro", h)
                        act.wait_ge(*A.filled(L, use))
                        if h:
                            act.wait_ge(*b_lo.upto(L, 12 + h))
                        act.activation(RSQ, psA[:, A.buf(use)], ACT.Square).then_inc(r_sq.sem, 1)
                        root(L, ("rss", h), RSQ, 1.0 / P, r_rs.sem)
                        act.wait_ge(*r_out.upto(L, h + 1))
                        act.activation(Bhi[:, h], RSQ, ACT.Copy).then_inc(b_hi.sem, 1)
                gates(L, 2)
                for j in range(KT):
                    act.wait_ge(*merged.upto(L, KT + j + 1))
                    if j == 0:
                        act.wait_ge(*A.filled(L, ("gate", 2, 0), KT - 1))
                    act.activation(Hhi[:, j], X[:, j], ACT.Copy).then_inc(m_hi.sem, 1)
                with act.Fori(0, KT // 2) as jj:
                    for b in (0, 1):
                        act.wait_ge(*x_ready.upto(L + 1, jj * 2 + b - 1))
                        act.dma_start(wk[:, 4 + b], tile_of(xs_v, jj * 2 + b)).then_inc(x_back[b].sem, 16)
                        act.wait_ge(*x_ready.upto(L + 1, jj * 2 + b + 1))
                        act.wait_ge(*sq_added.upto(L + 1, jj * 2 + b - 1))
                        act.activation(wk[:, b], tile_of(X, jj * 2 + b), ACT.Square).then_inc(sq_done.sem, 1)

            act.wait_ge(*summed.upto(DEPTH, 1))
            act.activation(wk[:, 2], psT[:, 0], ACT.Ln, bias=epsc[:, 0:1], scale=1.0 / D_MODEL).then_inc(f_sum, 1)
            act.wait_ge(f_sum, 1)
            act.activation(wk[:, 2], wk[:, 2], ACT.Exp, scale=-0.5).then_inc(f_rs, 1)

        @block.vector
        def _(dve):
            def step(ins):
                dve_step.step(dve, ins)

            def rotate(L, use, raw, raw_tile, dst, done):
                dve.wait_ge(*A.drained(L, raw))
                step(dve.tensor_tensor(dst, raw_tile, rope[:, 0], ALU.mult))
                dve.wait_ge(*T.filled(L, use))
                dve.tensor_tensor(R_ROT, psT[:, T.buf(use)], rope[:, 1], ALU.mult).then_inc(T.freed(use), 1)
                dve.wait_ge(*T.drained(L, use))
                dve.tensor_tensor(dst, dst, R_ROT, ALU.add).then_inc(done, 1)

            def maxima(L, h, q):
                n = (q + 1) * P
                for c in (0, 1):
                    use = ("s", h, q, c)
                    dve.wait_ge(*A.filled(L, use))
                    step(dve.reduce_max(rowmax[:, c:c + 1], psA[:, A.buf(use), 0:n], AX_X))
                dve.tensor_scalar(negmax[:, q % 2], rowmax[:], -SCALE, None, ALU.mult).then_inc(nmax.sem, 1)

            def mix(L, h, q):
                n = (q + 1) * P
                p0, p1 = PR[q % 2][0][:, 0:n], PR[q % 2][1][:, 0:n]
                dve.wait_ge(*A.drained(L, ("s", h, q, 0)))
                dve.wait_ge(*A.drained(L, ("s", h, q, 1)))
                step(dve.reciprocal(inv[:, q % 2], rowsum[:, q % 2]))
                step(dve.tensor_scalar(p1, p1, inv[:, q % 2, 1:2], lam[:, 4:5], ALU.mult, ALU.mult))
                dve.scalar_tensor_tensor(out=p0, in0=p0, scalar=inv[:, q % 2, 0:1], in1=p1, op0=ALU.mult, op1=ALU.add)\
                    .then_inc(mixed.sem, 1)

            def piece(L, use):
                kind, h, half = use
                c = slice(half * HALF, (half + 1) * HALF)
                if kind in ("sq", "sk"):
                    dst = (AQ if kind == "sq" else AK)[h % 2][:, c]
                    dve.wait_ge(*F.filled(L, use))
                    dve.tensor_tensor(ROT, psF, rope[:, 1, c], ALU.mult).then_inc(F.freed(use), 1)
                    step(dve.tensor_tensor(dst, RAW[:, c], rope[:, 0, c], ALU.mult))
                    dve.wait_ge(*F.drained(L, use))
                    dve.tensor_tensor(dst, dst, ROT, ALU.add).then_inc(rotated.sem, 1)
                    dve.wait_ge(*rotated.upto(L, 4 * h + half + (1 if kind == "sq" else 3)))
                elif kind == "vt":
                    dve.wait_ge(*F.filled(L, use))
                    dve.tensor_copy(AVAL[h % 2][:, c], psF).then_inc(F.freed(use), 1)
                elif kind == "ss":
                    n = 2 * h + half
                    dve.wait_ge(*a_rs.upto(L, n + 1))
                    dve.scalar_tensor_tensor(out=TMP, in0=psAV, scalar=gcol[:, 0:1], in1=TMP, op0=ALU.mult,
                                             op1=ALU.mult).then_inc(AV.freed((h, half)), 1)
                    dve.wait_ge(*AV.drained(L, (h, half)))
                    dve.wait_ge(*F.drained(L, ("z", h, half)))
                    dve.tensor_tensor(TMP, TMP, Z[:, c], ALU.mult).then_inc(a_out.sem, 1)

            def split(L, h, half):
                c = slice(half * HALF, (half + 1) * HALF)
                dve.wait_ge(*b_hi.upto(L, 2 * h + half + 1))
                dve.tensor_tensor(Blo[:, h, c], TMP, Bhi[:, h, c].bitcast(F32), ALU.subtract)\
                    .then_inc(b_lo.sem, 1)

            def attention(L):
                for use in B1_PRELUDE:
                    piece(L, use)
                maxima(L, 0, 0)
                late = []
                for h in range(HEADS):
                    for q in range(NT):
                        mix(L, h, q)
                        if q + 1 < NT:
                            maxima(L, h, q + 1)
                        elif h + 1 < HEADS:
                            maxima(L, h + 1, 0)
                        for use in late:
                            piece(L, use)
                        done, late = late, []
                        for after in (0, 1):
                            for use in pieces(B1_SLOTS, HEADS, h, q, after):
                                if use[0] == "ss":
                                    late.append(use)
                                else:
                                    piece(L, use)
                        for _, head, half in done:
                            split(L, head, half)
                piece(L, ("ss", HEADS - 1, 1))
                split(L, HEADS - 1, 1)

            def merge(L, i):
                with dve.Fori(0, KT // 2) as jj:
                    if i == 2:
                        dve.wait_ge(*merged.upto(L, KT))
                    for b in (0, 1):
                        use, j = ("branch", i, b), jj * 2 + b
                        dve.wait_ge(*A.filled(L, use, jj * 2))
                        dve.wait_ge(*A.drained(L, ("gate", i, b), jj * 2))
                        if i == 0:
                            dve.tensor_tensor(tile_of(X, j), wk[:, b], psA[:, A.buf(use)], ALU.mult)\
                                .then_inc(A.freed(use), 1)
                        else:
                            dve.tensor_tensor(wk[:, 2 + b], wk[:, b], psA[:, A.buf(use)], ALU.mult)\
                                .then_inc(A.freed(use), 1)
                            dve.wait_ge(*A.drained(L, use, jj * 2))
                            dve.tensor_tensor(tile_of(X, j), tile_of(X, j), wk[:, 2 + b], ALU.add)\
                                .then_inc(merged.sem, 1)

            def retain(L, pr, h):
                rows = head_rows(h)
                use = ("rvt", h)
                dve.wait_ge(*T.filled(L, use))
                dve.tensor_copy(V, psT[:, T.buf(use)]).then_inc(T.freed(use), 1)
                use = ("rs", h)
                dve.wait_ge(*A.filled(L, use))
                dve.tensor_tensor(by_chunk(SM), by_chunk(psA[:, A.buf(use)]), every_chunk(DM[:, h]), ALU.mult)\
                    .then_inc(A.freed(use), 1)
                use = ("kv", h)
                kv = psT[:, T.buf(use)]
                dve.wait_ge(*T.filled(L, use))
                step(dve.tensor_copy(ST[rows, P:2 * P], kv[rows, 0:P]))
                for n in range(1, NT - 1):
                    ins = dve.scalar_tensor_tensor(out=ST[rows, (n + 1) * P:(n + 2) * P],
                                                   in0=ST[rows, n * P:(n + 1) * P], scalar=DEC[rows, pr:pr + 1],
                                                   in1=kv[rows, n * P:(n + 1) * P], op0=ALU.mult, op1=ALU.add)
                    if n < NT - 2:
                        step(ins)
                    else:
                        ins.then_inc(T.freed(use), 1)
                use = ("ro", h)
                dve.wait_ge(*r_rs.upto(L, h + 1))
                dve.tensor_tensor(RSQ, psA[:, A.buf(use)], RSQ, ALU.mult).then_inc(A.freed(use), 1)
                dve.wait_ge(*A.drained(L, use))
                dve.wait_ge(*A.drained(L, ("rz", h)))
                dve.tensor_tensor(RSQ, RSQ, Z, ALU.mult).then_inc(r_out.sem, 1)
                dve.wait_ge(*b_hi.upto(L, 12 + h + 1))
                dve.tensor_tensor(Blo[:, h], RSQ, Bhi[:, h].bitcast(F32), ALU.subtract).then_inc(b_lo.sem, 1)

            def add_squares(t):
                dve.wait_ge(sq_done.sem, t + 1)
                dve.reduce_sum(SQSUM[:, t * P:(t + 1) * P], wk[:, 4 + t % 2].rearrange("p (k c) -> p c k", k=KT),
                               AX_X).then_inc(sq_added.sem, 1)

            dve.memset(upad[:, 0:2], 0.0).then_inc(dve_step.sem, 1)
            dve.memset(epsc[:], EPS).then_inc(dve_step.sem, 1)
            dve.wait_ge(consts_in, 64)
            dve.wait_ge(mask_in, 16)
            dve.wait_ge(dve_step.sem, 2)
            for t in range(NT):
                dve.wait_ge(x_turned, t + 1)
                dve.tensor_copy(X[:, :, t * P:(t + 1) * P], by_chunk(psA[:, t % 2])).then_inc(x_ready.sem, 1)
                if t == 0:
                    dve.tensor_copy(maskb[:], wk[:, 0, 0:P])
                    dve.tensor_copy(identb[:], ident[:]).then_inc(setup, 1)
                if t:
                    add_squares(t - 1)
            add_squares(NT - 1)
            dve.wait_ge(params_in, 64)
            with dve.Fori(0, DEPTH) as L:
                dve_step.layer(L)
                step(dve.tensor_copy(cur[:], par[:, bass.ds(L, 1), :].rearrange("p a c -> p (a c)")))
                raw = lamraw[:, bass.ds(L, 1), :].rearrange("p a (m two c) -> p (a m) two c", m=2, two=2)
                step(dve.tensor_tensor(lamt[:].rearrange("p (m c) -> p m c", m=2), raw[:, :, 0], raw[:, :, 1],
                                       ALU.mult))
                dve.reduce_sum(lam[:, 0:2], lamt[:].rearrange("p (m c) -> p m c", m=2), AX_X)\
                    .then_inc(lam_sum.sem, 1)
                step(dve.tensor_tensor(gcol[:], cur[:, C1.subln:C1.subln + 1],
                                       cur[:, C1.lam_rest:C1.lam_rest + 1], ALU.mult))
                dve.wait_ge(*rstd.upto(L, 1))
                dve.wait_ge(*x_saved.upto(L, 16))
                for j in range(KT + 1):
                    if j < KT:
                        dve.scalar_tensor_tensor(out=X[:, j], in0=X[:, j], scalar=cur[:, C1.norm + j:C1.norm + j + 1],
                                                 in1=wk[:, 2], op0=ALU.mult, op1=ALU.mult).then_inc(h_scaled.sem, 1)
                    if j:
                        dve.wait_ge(*h_hi.upto(L, j))
                        dve.tensor_tensor(Hlo[:, j - 1], X[:, j - 1], Hhi[:, j - 1].bitcast(F32), ALU.subtract)\
                            .then_inc(h_lo.sem, 1)
                dve.wait_ge(*lam_exp.upto(L, 1))
                step(dve.tensor_tensor(lam[:, 5:6], lam[:, 3:4], lam[:, 2:3], ALU.subtract))
                step(dve.tensor_tensor(lam[:, 4:5], lam[:, 5:6], cur[:, C1.lam_init:C1.lam_init + 1],
                                       ALU.subtract))
                dve.wait_ge(*rope_in.upto(L, 16))
                attention(L)
                merge(L, 0)
                for c in range(B1_TILES):
                    dve.wait_ge(*A.filled(L, ("cc", c)))
                    dve.wait_ge(*A.drained(L, ("cx", c)))
                    dve.tensor_tensor(upad[:, 2:], psA[:, A.buf(("cc", c))], wk[:, 4], ALU.mult)\
                        .then_inc(A.freed(("cc", c)), 1)
                    dve.wait_ge(*A.drained(L, ("cc", c)))
                    for k in range(3):
                        w = cur[:, C1.conv + 4 * k + c:C1.conv + 4 * k + c + 1]
                        if k == 0:
                            step(dve.tensor_scalar(wk[:, 7], upad[:, 0:SEQ], w, None, ALU.mult))
                        else:
                            step(dve.scalar_tensor_tensor(out=wk[:, 7], in0=upad[:, k:k + SEQ], scalar=w,
                                                          in1=wk[:, 7], op0=ALU.mult, op1=ALU.add))
                    dve.wait_ge(*A.drained(L, ("cb", c)))
                    step(dve.tensor_tensor(wk[:, 7], wk[:, 7], wk[:, 5], ALU.mult))
                    dve.wait_ge(*A.drained(L, ("cz", c)))
                    dve.tensor_tensor(wk[:, 7], wk[:, 7], wk[:, 6], ALU.mult).then_inc(c_out.sem, 1)
                    dve.wait_ge(*b_hi.upto(L, 8 + c + 1))
                    dve.tensor_tensor(Blo[:, c], wk[:, 7], Bhi[:, c].bitcast(F32), ALU.subtract)\
                        .then_inc(b_lo.sem, 1)
                merge(L, 1)
                dve.wait_ge(*rope_in.upto(L, 32))
                for pr in range(HEADS // 2):
                    rotate(L, ("swaprq", pr), ("rq", pr), R_RAWQ, Q, r_rot.sem)
                    rotate(L, ("swaprk", pr), ("rk", pr), R_RAWK, KK, r_rot.sem)
                    dve.wait_ge(*r_rot.upto(L, 2 * pr + 2))
                    step(dve.tensor_tensor(by_chunk(QX), by_chunk(Q), every_chunk(XI[:, pr]), ALU.mult))
                    dve.tensor_tensor(by_chunk(KZ), by_chunk(KK), every_chunk(ZE[:, pr]), ALU.mult)\
                        .then_inc(rk_scaled.sem, 1)
                    for h in (2 * pr, 2 * pr + 1):
                        retain(L, pr, h)
                merge(L, 2)
                for j in range(KT):
                    dve.wait_ge(*m_hi.upto(L, j + 1))
                    dve.tensor_tensor(Hlo[:, j], X[:, j], Hhi[:, j].bitcast(F32), ALU.subtract)\
                        .then_inc(m_lo.sem, 1)
                dve.memset(SQSUM, 0.0)
                with dve.Fori(0, KT // 2) as jj:
                    for b in (0, 1):
                        dve.wait_ge(*out_filled.upto(L, jj * 2 + b + 1))
                        dve.wait_ge(*x_back[b].upto(L, jj * 16 + 16))
                        dve.tensor_tensor(tile_of(X, jj * 2 + b), psA[:, b], wk[:, 4 + b], ALU.add)\
                            .then_inc(x_ready.sem, 1)
                        dve.wait_ge(*sq_done.upto(L + 1, jj * 2 + b + 1))
                        dve.tensor_tensor(SQSUM, SQSUM, wk[:, b], ALU.add).then_inc(sq_added.sem, 1)
            counts["d1"] = dve_step.k
            dve.wait_ge(f_rs, 1)
            dve.wait_ge(*x_ready.upto(DEPTH, KT))
            for j in range(KT):
                dve.scalar_tensor_tensor(out=X[:, j], in0=X[:, j], scalar=fing[:, j:j + 1], in1=wk[:, 2],
                                         op0=ALU.mult, op1=ALU.mult).then_inc(x_ready.sem, 1)
            dve.wait_ge(x_ready.sem, (DEPTH + 2) * KT)


def second_block(env, per, counts):
    nc, X, Hhi, Hlo, rope, ident, ones = env.nc, env.X, env.Hhi, env.Hlo, env.rope, env.ident, env.ones
    psA, psT, identb, maskb, epsc = env.psA, env.psT, env.identb, env.maskb, env.epsc
    SCALE = M_QK ** -0.5
    with ExitStack() as ctx:
        def sem(name):
            return ctx.enter_context(nc.semaphore("b2_" + name))

        def sb(name, shape, dt=F32):
            return ctx.enter_context(nc.sbuf_tensor("b2_" + name, shape, dt))

        wk = sb("wk", [P, 14, SEQ])
        ypad = sb("ypad", [P, 2, SEQ + PAD])
        par = sb("par", [P, DEPTH, C2.n])
        cur = sb("cur", [P, C2.n])
        pww = sb("pww", [P, 4 * P])
        sgw = sb("sgw", [P, 4, P])
        sgb = sb("sgb", [P, 2, P])
        swapm = sb("swapm", [P, M_ROPE])
        causal = sb("causal", [P, P])
        rowmax = sb("rowmax", [P, 2])
        negmax = sb("negmax", [P, 2])
        rowsum = sb("rowsum", [P, 2])
        inv = sb("inv", [P, 2])
        qk_root = sb("qk_root", [P, 2, NT])
        q_root = sb("q_root", [P, 2, 2, NT])
        credit = sb("credit", [P, 2])

        a_uses, t_uses = uses_of_block2()
        A = Ring("b2A", a_uses, lambda n: ctx.enter_context(nc.semaphore(n)))
        T = Ring("b2T", t_uses, lambda n: ctx.enter_context(nc.semaphore(n)))
        tp, av, f = uses_of_attention(B2_PRELUDE, B2_SLOTS, M_HEADS)
        TP = Ring("b2TP", tp, lambda n: ctx.enter_context(nc.semaphore(n)), 1)
        AV = Ring("b2AV", av, lambda n: ctx.enter_context(nc.semaphore(n)), 1)
        F = Ring("b2F", f, lambda n: ctx.enter_context(nc.semaphore(n)), 1)
        psTP, psAV, psF = psT[:, 0], psT[:, 1, 0:HALF], psT[:, 1, HALF:]
        NP = len(P2)
        s = Group()
        s.credit, s.w_split, s.w_hi, s.panel_begun = credit, sem("w_split"), sem("w_hi"), sem("panel_begun")
        s.w_loaded = [sem("w_loaded0"), sem("w_loaded1")]
        params_in = sem("params_in")
        layer_in = Tally(sem("layer_in"), 4 * 16)
        x_ready = Tally(sem("x_ready"), KT)
        out_filled = Tally(sem("out_filled"), KT)
        x_saved = Tally(sem("x_saved"), 16)
        x_back = [Tally(sem(f"x_back{b}"), 16 * KT // 2) for b in (0, 1)]
        sq_done, sq_added = Tally(sem("sq_done"), KT), Tally(sem("sq_added"), KT)
        summed, rstd = Tally(sem("summed"), 1), Tally(sem("rstd"), 1)
        h_scaled, h_hi, h_lo = (Tally(sem(n), KT) for n in ("h_scaled", "h_hi", "h_lo"))
        conv_done = Tally(sem("conv_done"), 2)
        uz_done = Tally(sem("uz_done"), 2)
        l_sq, l_added = Tally(sem("l_sq"), KT), Tally(sem("l_added"), KT - 2)
        l_rs = Tally(sem("l_rs"), 2)
        l_scaled, l_hi, l_lo = (Tally(sem(n), KT) for n in ("l_scaled", "l_hi", "l_lo"))
        sq2 = Tally(sem("sq2"), 4)
        roots = Tally(sem("roots"), 4)
        normed = Tally(sem("normed"), 4)
        c_act, s_act = Tally(sem("c_act"), 2), Tally(sem("s_act"), 2)
        s_out = Tally(sem("s_out"), 2)
        c_fin, s_fin = Tally(sem("c_fin"), 2), Tally(sem("s_fin"), 2)
        kr_sq, kr_g, kr_rot = Tally(sem("kr_sq"), 1), Tally(sem("kr_g"), 1), Tally(sem("kr_rot"), 1)
        qk_rs = Tally(sem("qk_rs"), M_HEADS)
        k_diag = Tally(sem("k_diag"), M_HEADS)
        q_rot = Tally(sem("q_rot"), 2 * M_HEADS)
        nmax, mixed = Tally(sem("nmax"), M_HEADS * NT), Tally(sem("mixed"), M_HEADS * NT)
        m_sq, m_added, m_rs, m_fin = Tally(sem("m_sq"), 4), Tally(sem("m_added"), 3), Tally(sem("m_rs"), 1), \
            Tally(sem("m_fin"), 4)
        y_hi, y_lo = Tally(sem("y_hi"), KT), Tally(sem("y_lo"), KT)
        turned, copied, written = sem("turned"), sem("copied"), [sem(f"written{b}") for b in range(4)]
        dve_step = Chain(sem("dve_step"), per.get("d2", 1), 3)
        act_step = Chain(sem("act_step"), 1)

        ZM, ZC, UZ, YC, VG = (wk[:, a:b] for a, b in ((0, 4), (4, 6), (6, 8), (8, 10), (10, 12)))
        KR, SQK = wk[:, 12], wk[:, 13]
        ZS = [X[:, 0], X[:, 1]]
        SQ_C, SQ_S = [X[:, 4], X[:, 5]], [X[:, 6], X[:, 7]]
        ROOT, ROOT_C, ROOT_S = ypad[:, 0, PAD:], wk[:, 8], wk[:, 10]
        LSQ, LSUM, LROOT = wk[:, 13], [ypad[:, 1, PAD:], wk[:, 9]], [ypad[:, 0, PAD:], wk[:, 11]]
        SQSUM = wk[:, 2]
        OUT = [wk[:, t] for t in (6, 7, 8, 9)]
        WG = wk[:, 9, 0:4 * P]
        Q, KK, PR = [wk[:, 4], wk[:, 5]], [wk[:, 6], wk[:, 7]], [wk[:, 8], wk[:, 9]]
        QSQ, ROT, KROT = wk[:, 10], wk[:, 11], wk[:, 9]
        MSQ, MSUM = wk[:, 11], wk[:, 10]
        V = [ypad[:, 0, PAD:PAD + HALF], ypad[:, 0, PAD + HALF:]]
        RAWKV = ypad[:, 1, PAD:]
        WT = X[:, 2:6].rearrange("p a b -> p (a b)").rearrange("p (k q) -> p k q", k=NT)
        NOPE, ROPE, QK = slice(0, M_NOPE), slice(M_NOPE, M_QK), slice(0, M_QK)
        xs_v = env.xs.rearrange("j p n -> p j n")

        def by_chunk(ap):
            return ap.rearrange("p (n c) -> p n c", n=NT)

        def every_chunk(ap):
            return ap.unsqueeze(1).broadcast_to([ap.shape[0], NT, ap.shape[1]])

        def tile_of(ap, j):
            return ap[:, bass.ds(j, 1), :].rearrange("p a b -> p (a b)")

        def col(k):
            return cur[:, k:k + 1]

        def head_rows(h):
            return slice((h % 2) * M_V, (h % 2 + 1) * M_V)

        Y_ORDER = (0, 1, 6, 7, 2, 3, 4, 5)

        block = ctx.enter_context(nc.Block())

        def load_inputs(sp):
            sp.dma_start(par[:], env.par2.rearrange("l p c -> p l c")).then_inc(params_in, 16)
            sp.dma_start(swapm[:], env.consts[:, K.swapm:K.swapm + M_ROPE]).then_inc(params_in, 16)
            sp.dma_start(causal[:], env.consts[:, K.causal:K.causal + P]).then_inc(params_in, 16)
            sp.dma_start(rope[:], env.ropes[2]).then_inc(params_in, 16)

        weight_engines(block, s, env.w2, env.stage, env.Whi, env.Wlo, P2, RUNS2, load_inputs)

        @block.tensor
        def _(pe):
            def panel(L, name, nk=KT, M=P, j=0, tiles=None, dst=None, done=None, first=True, last=True, arrived=None,
                      order=None):
                p = PAN2[name]
                pe.wait_ge(s.w_split, L * NP + p + 3 + j * 2)
                if dst is None:
                    if A.before(name):
                        pe.wait_ge(*A.room(L, name, j))
                    dst, done = psA[:, A.buf(name)], A.filled_sem
                tiles = tiles or range(nk)
                mm = three_pass(pe, dst, env.Whi[:, p % 2], env.Wlo[:, p % 2], [Hhi[:, k] for k in tiles],
                                [Hlo[:, k] for k in tiles], nk, M, s.panel_begun, first, last,
                                arrived, order)
                if done is not None:
                    mm.then_inc(done, 1)

            def full(dst, lhsT, rhs, start=True, stop=True):
                for h in (0, 1):
                    c = slice(h * HALF, (h + 1) * HALF)
                    mm = pe.matmul(dst[:, c], lhsT, rhs[:, c], start=start, stop=stop)
                return mm

            def turn(dst, src, blocks):
                for i in range(blocks):
                    mm = pe.transpose(dst[:, i * P:(i + 1) * P], src[:, i * P:(i + 1) * P], ident[:])
                return mm

            def pair_sum(L, use, tiles):
                pe.wait_ge(*T.room(L, use))
                full(psT[:, T.buf(use)], ones[:], tiles[0], True, False)
                full(psT[:, T.buf(use)], ones[:], tiles[1], False, True).then_inc(T.filled_sem, 1)

            def total(L, use, sums):
                pe.wait_ge(*T.room(L, use))
                full(psT[:, T.buf(use)], ones[:], sums).then_inc(T.filled_sem, 1)

            def scores(L, h, q):
                use = ("s", h, q)
                pe.wait_ge(*A.room(L, use))
                if q == 0:
                    pe.wait_ge(*F.drained(L, ("kb", h, 1)))
                dst, n = psA[:, A.buf(use)], (q + 1) * P
                for k0 in range(0, n, HALF):
                    k1 = min(n, k0 + HALF)
                    pe.matmul(dst[:, k0:k1], Q[h % 2][QK, q * P:n], KK[h % 2][QK, k0:k1], start=True, stop=k1 < n)
                pe.matmul(dst[:, q * P:n], identb[:], maskb[:], start=False, stop=True).then_inc(A.filled_sem, 1)

            def piece(L, use):
                def latent_split(k):
                    pe.wait_ge(*l_hi.upto(L, k + 1))
                    pe.wait_ge(*l_lo.upto(L, k + 1))

                kind, h, half = use
                c = slice(half * HALF, (half + 1) * HALF)
                if use == ("kv", 0, 0):
                    latent_split(KT - 1)
                if kind in ("q", "kv"):
                    p = PAN2[(kind, h)]
                    pe.wait_ge(s.w_split, L * NP + p + 3)
                if kind == "kb":
                    pe.wait_ge(*k_diag.upto(L, h + 1))
                if F.before(use):
                    pe.wait_ge(*F.room(L, use))
                if kind in ("q", "kv"):
                    nk, M, t0 = (Q_LORA_T, M_QK, 0) if kind == "q" else (KV_LORA_T, P, Q_LORA_T)
                    mm = three_pass_half(pe, psF, env.Whi[:, p % 2], env.Wlo[:, p % 2],
                                         [Hhi[:, t0 + k] for k in range(nk)], [Hlo[:, t0 + k] for k in range(nk)],
                                         nk, M, half, None if half else s.panel_begun,
                                         latent_split if use == B2_PRELUDE[0] else None)
                elif kind == "st":
                    for i, sq in enumerate((QSQ, SQK)):
                        for t in range(NT):
                            mm = pe.matmul(psF[:, i * NT + t:i * NT + t + 1], sq[QK, t * P:(t + 1) * P],
                                           ones[QK, 0:1], start=True, stop=True)
                elif kind == "kb":
                    mm = pe.matmul(psF[QK], ones[:, QK], QSQ[:, c], start=True, stop=True)
                elif kind == "sq":
                    mm = pe.matmul(psF[ROPE], swapm[QK, :], Q[h % 2][QK, c], start=True, stop=True)
                else:
                    for n in range(NT):
                        dst, src = psF[:, n * M_V:(n + 1) * M_V], RAWKV[M_NOPE:P, n * P:(n + 1) * P]
                        if n == 0:
                            pe.matmul(dst, src, ident[M_NOPE:P, M_NOPE:P], start=True, stop=True)
                        else:
                            mm = pe.transpose(dst, src, ident[M_NOPE:P, M_NOPE:P])
                mm.then_inc(F.filled_sem, 1)

            def values(L, h, g):
                rows = head_rows(h)
                pe.wait_ge(*TP.drained(L, (h, 4 * g + 3)))
                pe.wait_ge(*F.drained(L, ("vt", h, 0)))
                if AV.before((h, g)):
                    pe.wait_ge(*AV.room(L, (h, g)))
                for k in range(4 * g + 4):
                    c0 = max(0, k - 4 * g) * P
                    mm = pe.matmul(psAV[rows, c0:], V[h % 2][:, k * M_V:(k + 1) * M_V], WT[:, k, c0:],
                                   start=k == 0, stop=k == 4 * g + 3)
                mm.then_inc(AV.filled_sem, 1)

            def attention(L):
                for use in B2_PRELUDE:
                    piece(L, use)
                scores(L, 0, 0)
                scores(L, 0, 1)
                for h in range(M_HEADS):
                    for q in range(NT):
                        if q + 2 < NT:
                            scores(L, h, q + 2)
                        elif h + 1 < M_HEADS:
                            scores(L, h + 1, q + 2 - NT)
                        for use in pieces(B2_SLOTS, M_HEADS, h, q, 0):
                            piece(L, use)
                        if q == 4:
                            values(L, h, 0)
                        if q == 0 and h:
                            values(L, h - 1, 1)
                        if TP.before((h, q)):
                            pe.wait_ge(*TP.room(L, (h, q)))
                        pe.wait_ge(*mixed.upto(L, h * NT + q + 1))
                        turn(psTP, PR[q % 2], q + 1).then_inc(TP.filled_sem, 1)
                        for use in pieces(B2_SLOTS, M_HEADS, h, q, 1):
                            piece(L, use)
                values(L, M_HEADS - 1, 1)

            with pe.Fori(0, DEPTH) as L:
                pe.wait_ge(*sq_added.upto(L, KT))
                full(psT[:, 0], ones[:], SQSUM).then_inc(summed.sem, 1)

                def h_split(k):
                    pe.wait_ge(*h_hi.upto(L, k + 1))
                    pe.wait_ge(*h_lo.upto(L, k + 1))

                def y_split(k):
                    pe.wait_ge(*y_hi.upto(L, Y_ORDER.index(k) + 1))
                    pe.wait_ge(*y_lo.upto(L, Y_ORDER.index(k) + 1))

                for name, nk, M in P2[:PAN2[("cq", 0)]]:
                    panel(L, name, arrived=h_split if name == ("g", 0) else None)
                pe.wait_ge(*conv_done.upto(L, 2))
                pair_sum(L, "cmean", [YC[:, 0], YC[:, 1]])
                pe.wait_ge(*A.drained(L, ("v", 1)))
                pair_sum(L, "smean", [VG[:, 0], VG[:, 1]])
                panel(L, ("cq", 0))
                pe.wait_ge(*sq2.upto(L, 1))
                pair_sum(L, "cvar", SQ_C)
                pe.wait_ge(*sq2.upto(L, 2))
                pair_sum(L, "svar", SQ_S)
                panel(L, ("cq", 1))
                pe.wait_ge(*c_act.upto(L, 2))
                pe.wait_ge(*layer_in.upto(L, 64))
                for m in (0, 1):
                    pe.wait_ge(*A.room(L, ("pw", m)))
                    for k in (0, 1):
                        mm = full(psA[:, A.buf(("pw", m))], pww[:, k * 2 * P + m * P:k * 2 * P + (m + 1) * P],
                                  YC[:, k], k == 0, k == 1)
                    mm.then_inc(A.filled_sem, 1)
                panel(L, ("cq", 2))
                pe.wait_ge(*sq2.upto(L, 3))
                pair_sum(L, "cbn", SQ_C)
                for t in (0, 1):
                    pe.wait_ge(*s_act.upto(L, t + 1))
                    pe.wait_ge(*T.room(L, ("vst", t)))
                    turn(psT[:, T.buf(("vst", t))], VG[:, t], NT).then_inc(T.filled_sem, 1)
                pe.wait_ge(*T.room(L, "wgt"))
                for g in range(4):
                    mm = pe.transpose(psT[:, T.buf("wgt"), g * P:(g + 1) * P], sgw[:, g], ident[:])
                mm.then_inc(T.filled_sem, 1)
                panel(L, ("cq", 3))
                pe.wait_ge(*T.drained(L, "wgt"))
                for t in (0, 1):
                    pe.wait_ge(*T.drained(L, ("vst", t)))
                    pe.wait_ge(*A.room(L, ("sg", t)))
                    for n in range(NT):
                        for g in (0, 1):
                            mm = pe.matmul(psA[g * 64:(g + 1) * 64, A.buf(("sg", t)), n * P:(n + 1) * P],
                                           VG[:, t, n * P + g * 64:n * P + (g + 1) * 64],
                                           WG[:, (2 * t + g) * P:(2 * t + g + 1) * P], start=True, stop=True)
                    mm.then_inc(A.filled_sem, 1)
                panel(L, ("cq", 4))
                pe.wait_ge(*sq2.upto(L, 4))
                pair_sum(L, "sbn", SQ_S)
                panel(L, ("cq", 5))
                panel(L, ("ckv", 0))
                pe.wait_ge(*l_added.upto(L, Q_LORA_T - 1))
                total(L, "cqs", LSUM[0])
                panel(L, ("ckv", 1))
                pe.wait_ge(*T.room(L, "kr"))
                panel(L, ("kr", 0), KT // 2, M_QK, dst=psT[:, T.buf("kr")], last=False)
                panel(L, ("kr", 1), KT // 2, M_QK, tiles=range(KT // 2, KT), dst=psT[:, T.buf("kr")],
                      done=T.filled_sem, first=False)
                pe.wait_ge(*l_added.upto(L, KT - 2))
                total(L, "ckvs", LSUM[1])
                panel(L, ("zm", 0))
                pe.wait_ge(*kr_g.upto(L, 1))
                pe.wait_ge(*T.room(L, "krswap"))
                full(psT[ROPE, T.buf("krswap")], swapm[QK, :], KR[QK]).then_inc(T.filled_sem, 1)
                for t in (1, 2, 3):
                    panel(L, ("zm", t))
                pe.wait_ge(*T.room(L, "mbn"))
                attention(L)
                pe.wait_ge(*m_added.upto(L, 3))
                full(psT[:, T.buf("mbn")], ones[:], MSUM).then_inc(T.filled_sem, 1)
                with pe.Fori(0, KT // 2) as jj:
                    for b in (0, 1):
                        pe.wait_ge(*x_ready.upto(L + 1, jj * 2 + b - 1))
                        panel(L, ("out", b), j=jj, dst=psA[:, b], done=out_filled.sem, arrived=y_split,
                              order=Y_ORDER)

            pe.wait_ge(*x_ready.upto(DEPTH, KT))
            for t in range(NT):
                if t >= 2:
                    pe.wait_ge(copied, t - 1)
                for j in range(KT):
                    mm = pe.transpose(psA[:, t % 2, j * P:(j + 1) * P], X[:, j, t * P:(t + 1) * P], ident[:])
                mm.then_inc(turned, 1)

        @block.scalar
        def _(act):
            def root(L, use, dst, mean, done, rows=slice(0, P)):
                act.wait_ge(*T.filled(L, use))
                act.activation(dst[rows], psT[rows, T.buf(use)], ACT.Ln, bias=epsc[rows, 0:1], scale=mean)\
                    .then_inc(T.freed(use), 1)
                act.wait_ge(*T.drained(L, use))
                act.activation(dst[rows], dst[rows], ACT.Exp, scale=-0.5).then_inc(done, 1)

            def take(L, use, dst, func=ACT.Copy):
                act.wait_ge(*A.filled(L, use))
                act.activation(dst, psA[:, A.buf(use)], func).then_inc(A.freed(use), 1)

            def squares(dst, tiles):
                act.activation(dst[0], tiles[0], ACT.Square)
                act.activation(dst[1], tiles[1], ACT.Square).then_inc(sq2.sem, 1)

            def latent(L, j):
                name = ("cq", j) if j < Q_LORA_T else ("ckv", j - Q_LORA_T)
                take(L, name, X[:, j])
                act.wait_ge(*A.drained(L, name))
                first = j in (0, Q_LORA_T)
                if not first and j != 1:
                    act.wait_ge(*l_added.upto(L, j - 1 if j < Q_LORA_T else j - 2))
                act.activation(LSUM[j // Q_LORA_T] if first else LSQ, X[:, j], ACT.Square).then_inc(l_sq.sem, 1)

            def exps(L, h, q):
                use, n = ("s", h, q), (q + 1) * P
                act.wait_ge(*nmax.upto(L, h * NT + q + 1))
                act.activation(PR[q % 2][:, 0:n], psA[:, A.buf(use), 0:n], ACT.Exp, bias=negmax[:, q % 2:q % 2 + 1],
                               scale=q_root[:, h % 2, 1, q:q + 1], accum_out=rowsum[:, q % 2:q % 2 + 1]).then_inc(A.freed(use), 1)

            def piece(L, use):
                kind, h, half = use
                c = slice(half * HALF, (half + 1) * HALF)
                if kind == "q":
                    act.wait_ge(*F.filled(L, use))
                    act.activation(QSQ[QK, c], psF[QK], ACT.Square)
                    act.activation(Q[h % 2][QK, c], psF[QK], ACT.Copy, scale=cur[QK, C2.qg:C2.qg + 1])\
                        .then_inc(F.freed(use), 1)
                elif kind == "kv":
                    act.wait_ge(*F.filled(L, use))
                    act.activation(SQK[NOPE, c], psF[NOPE], ACT.Square)
                    act.activation(RAWKV[:, c], psF, ACT.Copy).then_inc(F.freed(use), 1)
                elif kind == "st":
                    qk_roots(L, h)

            def qk_roots(L, h):
                use, both = ("st", h, 0), qk_root[:].rearrange("p a t -> p (a t)")
                act.wait_ge(*F.filled(L, use))
                act.activation(both, psF[:, 0:2 * NT], ACT.Ln, bias=epsc[:, 0:1], scale=1.0 / M_QK)\
                    .then_inc(F.freed(use), 1)
                act.wait_ge(*F.drained(L, use))
                act.activation(both, both, ACT.Exp, scale=-0.5).then_inc(qk_rs.sem, 1)

            def square(L, t):
                if t >= 2:
                    act.wait_ge(*m_added.upto(L, t - 1))
                act.activation(MSQ if t else MSUM, ZM[:, t], ACT.Square).then_inc(m_sq.sem, 1)

            def attention(L):
                for use in B2_PRELUDE:
                    piece(L, use)
                exps(L, 0, 0)
                for h in range(M_HEADS):
                    for q in range(NT):
                        if q + 1 < NT:
                            exps(L, h, q + 1)
                        elif h + 1 < M_HEADS:
                            exps(L, h + 1, 0)
                        for use in pieces(B2_SLOTS, M_HEADS, h, q, 0):
                            piece(L, use)
                        act.wait_ge(*TP.filled(L, (h, q)))
                        act.activation(WT[:, 0:q + 1, (q % 4) * P:(q % 4 + 1) * P],
                                       psTP[:, 0:(q + 1) * P].rearrange("p (k c) -> p k c", c=P),
                                       ACT.Copy).then_inc(TP.freed((h, q)), 1)
                        for use in pieces(B2_SLOTS, M_HEADS, h, q, 1):
                            piece(L, use)
                        if h == M_HEADS - 1 and 1 <= q <= 3:
                            act.wait_ge(*AV.drained(L, (h - 1, 1)))
                            square(L, q - 1)
                        if h == M_HEADS - 1 and q >= 4:
                            j = Y_ORDER[q - 4]
                            act.activation(Hhi[:, j], X[:, j], ACT.Copy).then_inc(y_hi.sem, 1)

            for j in range(KT):
                act.wait_ge(x_ready.sem, KT)
                if j >= 2:
                    act.wait_ge(sq_added.sem, j - 1)
                act.activation(wk[:, j % 2], X[:, j], ACT.Square).then_inc(sq_done.sem, 1)
            with act.Fori(0, DEPTH) as L:
                act_step.layer(L)
                act.wait_ge(*x_ready.upto(L, KT))
                act.dma_start(xs_v, X[:]).then_inc(x_saved.sem, 16)
                act.dma_start(pww[:], env.pww[L]).then_inc(layer_in.sem, 16)
                act.dma_start(sgw[:], env.sgw[L]).then_inc(layer_in.sem, 16)
                for b in (0, 1):
                    src = env.sgb[L].rearrange("(two b) t -> b two t", b=2)[b]
                    act.dma_start(sgb[b * 64:(b + 1) * 64], src.partition_broadcast(64)).then_inc(layer_in.sem, 16)
                act.wait_ge(*summed.upto(L, 1))
                act_step.step(act, act.activation(wk[:, 2], psT[:, 0], ACT.Ln, bias=epsc[:, 0:1],
                                                  scale=1.0 / D_MODEL))
                act.activation(wk[:, 2], wk[:, 2], ACT.Exp, scale=-0.5).then_inc(rstd.sem, 1)
                for j in range(KT):
                    act.wait_ge(*h_scaled.upto(L, j + 1))
                    act.activation(Hhi[:, j], X[:, j], ACT.Copy).then_inc(h_hi.sem, 1)
                act.wait_ge(*h_lo.upto(L, KT))
                for t in (0, 1):
                    take(L, ("g", t), YC[:, t], ACT.Sigmoid)
                for t in (0, 1):
                    take(L, ("v", t), VG[:, t], ACT.Gelu_apprx_tanh)
                for t in (0, 1):
                    take(L, ("u", t), UZ[:, t], ACT.Gelu_apprx_tanh)
                for t in (0, 1):
                    take(L, ("zs", t), ZS[t], ACT.Silu)
                for t in (0, 1):
                    take(L, ("zc", t), ZC[:, t], ACT.Silu)
                act.wait_ge(*T.drained(L, "cmean"))
                squares(SQ_C, [YC[:, 0], YC[:, 1]])
                act.wait_ge(*T.drained(L, "smean"))
                squares(SQ_S, [VG[:, 0], VG[:, 1]])
                act.wait_ge(*uz_done.upto(L, 2))
                latent(L, 0)
                root(L, "cvar", ROOT, 1.0 / 256, roots.sem)
                for t in (0, 1):
                    act.wait_ge(*normed.upto(L, t + 1))
                    act.activation(YC[:, t], YC[:, t], ACT.Silu, bias=col(C2.cln_b + t)).then_inc(c_act.sem, 1)
                root(L, "svar", ROOT, 1.0 / 256, roots.sem)
                latent(L, 1)
                for t in (0, 1):
                    act.wait_ge(*normed.upto(L, t + 3))
                    act.activation(VG[:, t], VG[:, t], ACT.Identity, bias=col(C2.sln_b + t)).then_inc(s_act.sem, 1)
                act.wait_ge(*A.drained(L, ("pw", 0)))
                act.wait_ge(*A.drained(L, ("pw", 1)))
                squares(SQ_C, [ZC[:, 0], ZC[:, 1]])
                latent(L, 2)
                root(L, "cbn", ROOT_C, 1.0 / 256, roots.sem)
                for t in (0, 1):
                    act.wait_ge(*T.filled(L, ("vst", t)))
                    act.activation(VG[:, t], psT[:, T.buf(("vst", t))], ACT.Copy).then_inc(T.freed(("vst", t)), 1)
                latent(L, 3)
                act.wait_ge(*s_out.upto(L, 2))
                squares(SQ_S, [UZ[:, 0], UZ[:, 1]])
                latent(L, 4)
                root(L, "sbn", ROOT_S, 1.0 / 256, roots.sem)
                latent(L, 5)
                latent(L, 6)
                root(L, "cqs", LROOT[0], 1.0 / (Q_LORA_T * P), l_rs.sem)
                latent(L, 7)
                act.wait_ge(*T.filled(L, "kr"))
                act.activation(KR[ROPE], psT[ROPE, T.buf("kr")], ACT.Copy).then_inc(T.freed("kr"), 1)
                act.wait_ge(*l_added.upto(L, KT - 2))
                act.wait_ge(*T.drained(L, "kr"))
                act.activation(SQK[ROPE], KR[ROPE], ACT.Square).then_inc(kr_sq.sem, 1)
                root(L, "ckvs", LROOT[1], 1.0 / (KV_LORA_T * P), l_rs.sem)
                for t in range(4):
                    take(L, ("zm", t), ZM[:, t], ACT.Silu)
                for j in range(KT):
                    act.wait_ge(*l_scaled.upto(L, j + 1))
                    act.activation(Hhi[:, j], X[:, j], ACT.Copy).then_inc(l_hi.sem, 1)
                act.wait_ge(*s_fin.upto(L, 2))
                attention(L)
                act.wait_ge(*AV.drained(L, (M_HEADS - 1, 1)))
                square(L, 3)
                root(L, "mbn", MSUM, 1.0 / 512, m_rs.sem)
                for j in Y_ORDER[4:]:
                    act.wait_ge(*m_fin.upto(L, j - 1))
                    act.activation(Hhi[:, j], X[:, j], ACT.Copy).then_inc(y_hi.sem, 1)
                with act.Fori(0, KT // 2) as jj:
                    for b in (0, 1):
                        act.wait_ge(*x_ready.upto(L + 1, jj * 2 + b - 1))
                        act.dma_start(wk[:, 4 + b], tile_of(xs_v, jj * 2 + b)).then_inc(x_back[b].sem, 16)
                        act.wait_ge(*x_ready.upto(L + 1, jj * 2 + b + 1))
                        act.wait_ge(*sq_added.upto(L + 1, jj * 2 + b - 1))
                        act.activation(wk[:, b], tile_of(X, jj * 2 + b), ACT.Square).then_inc(sq_done.sem, 1)

            out_tiles = env.out.rearrange("(t p) d -> t p d", p=P)
            for t in range(NT):
                act.wait_ge(copied, t + 1)
                act.dma_start(out_tiles[t], OUT[t % 4]).then_inc(written[t % 4], 16)
            for b in range(4):
                act.wait_ge(written[b], 16 * NT // 4)

        @block.vector
        def _(dve):
            def step(ins):
                dve_step.step(dve, ins)

            def scale_by(dst, g, root_tile, rows=slice(0, P), src=None):
                return dve.scalar_tensor_tensor(out=dst[rows], in0=(dst if src is None else src)[rows],
                                                scalar=cur[rows, g:g + 1], in1=root_tile[rows], op0=ALU.mult,
                                                op1=ALU.mult)

            def split_low(dst, src, hi):
                return dve.tensor_tensor(dst, src, hi.bitcast(F32), ALU.subtract)

            def centre(L, use, tiles):
                dve.wait_ge(*T.filled(L, use))
                dve.scalar_tensor_tensor(out=tiles[:, 0], in0=psT[:, T.buf(use)], scalar=-1.0 / 256,
                                         in1=tiles[:, 0], op0=ALU.mult, op1=ALU.add)
                dve.scalar_tensor_tensor(out=tiles[:, 1], in0=psT[:, T.buf(use)], scalar=-1.0 / 256,
                                         in1=tiles[:, 1], op0=ALU.mult, op1=ALU.add).then_inc(T.freed(use), 1)

            def add_latent(L, j):
                total = LSUM[j // Q_LORA_T]
                if j not in (1, Q_LORA_T + 1):
                    dve.wait_ge(*l_added.upto(L, j - 1))
                dve.wait_ge(*l_sq.upto(L, j + 1))
                dve.tensor_tensor(total, total, LSQ, ALU.add).then_inc(l_added.sem, 1)

            def rotate_key(L):
                use = "krswap"
                dve.wait_ge(*T.filled(L, use))
                dve.tensor_tensor(KROT[ROPE], psT[ROPE, T.buf(use)], rope[ROPE, 1], ALU.mult)\
                    .then_inc(T.freed(use), 1)
                step(dve.tensor_tensor(KR[ROPE], KR[ROPE], rope[ROPE, 0], ALU.mult))
                dve.tensor_tensor(KR[ROPE], KR[ROPE], KROT[ROPE], ALU.add).then_inc(kr_rot.sem, 1)

            def piece(L, use):
                kind, h, half = use
                c = slice(half * HALF, (half + 1) * HALF)
                if kind == "st":
                    dve.wait_ge(*qk_rs.upto(L, h + 1))
                    dve.tensor_scalar(q_root[:, h % 2, 0], qk_root[:, 0], -SCALE, None, ALU.mult)
                    dve.tensor_scalar(q_root[:, h % 2, 1], qk_root[:, 0], SCALE, None, ALU.mult)
                    dve.tensor_tensor(by_chunk(QSQ), ident[:].unsqueeze(1).broadcast_to([P, NT, P]),
                                      qk_root[:, 1].unsqueeze(2).broadcast_to([P, NT, P]), ALU.mult)\
                        .then_inc(k_diag.sem, 1)
                elif kind == "kb":
                    k = KK[h % 2]
                    dve.wait_ge(*F.filled(L, use))
                    dve.tensor_tensor(k[ROPE, c], KR[ROPE, c], psF[ROPE], ALU.mult)
                    dve.scalar_tensor_tensor(out=k[NOPE, c], in0=RAWKV[NOPE, c], scalar=cur[NOPE, C2.kg:C2.kg + 1],
                                             in1=psF[NOPE], op0=ALU.mult, op1=ALU.mult).then_inc(F.freed(use), 1)
                elif kind == "vt":
                    dve.wait_ge(*F.filled(L, use))
                    dve.tensor_copy(V[h % 2], psF).then_inc(F.freed(use), 1)
                elif kind == "sq":
                    rot, q = ROT[ROPE, c], Q[h % 2][ROPE, c]
                    dve.wait_ge(*F.filled(L, use))
                    dve.tensor_tensor(rot, psF[ROPE], rope[ROPE, 1, c], ALU.mult).then_inc(F.freed(use), 1)
                    step(dve.tensor_tensor(q, q, rope[ROPE, 0, c], ALU.mult))
                    dve.tensor_tensor(q, q, rot, ALU.add).then_inc(q_rot.sem, 1)

            def add_square(L, t):
                if t > 1:
                    dve.wait_ge(*m_added.upto(L, t - 1))
                dve.wait_ge(*m_sq.upto(L, t + 1))
                dve.tensor_tensor(MSUM, MSUM, MSQ, ALU.add).then_inc(m_added.sem, 1)

            def values(L, h, g):
                rows = head_rows(h)
                y = ZM[rows, h // 2, g * HALF:(g + 1) * HALF]
                dve.wait_ge(*AV.filled(L, (h, g)))
                dve.tensor_tensor(y, y, psAV[rows], ALU.mult).then_inc(AV.freed((h, g)), 1)

            def attention(L):
                for use in B2_PRELUDE:
                    piece(L, use)
                maxima(L, 0, 0)
                for h in range(M_HEADS):
                    for q in range(NT):
                        if q + 1 < NT:
                            maxima(L, h, q + 1)
                        elif h + 1 < M_HEADS:
                            maxima(L, h + 1, 0)
                        b, n = q % 2, (q + 1) * P
                        dve.wait_ge(*A.drained(L, ("s", h, q)))
                        step(dve.reciprocal(inv[:, b:b + 1], rowsum[:, b:b + 1]))
                        dve.tensor_scalar(PR[b][:, 0:n], PR[b][:, 0:n], inv[:, b:b + 1], None, ALU.mult)\
                            .then_inc(mixed.sem, 1)
                        for use in pieces(B2_SLOTS, M_HEADS, h, q, 0):
                            piece(L, use)
                        if q == 4:
                            values(L, h, 0)
                        if q == 0 and h:
                            values(L, h - 1, 1)
                        for use in pieces(B2_SLOTS, M_HEADS, h, q, 1):
                            piece(L, use)
                        if h == M_HEADS - 1 and 2 <= q <= 3:
                            add_square(L, q - 1)
                values(L, M_HEADS - 1, 1)
                add_square(L, 3)

            def maxima(L, h, q):
                use, b = ("s", h, q), q % 2
                dve.wait_ge(*A.filled(L, use))
                step(dve.reduce_max(rowmax[:, b:b + 1], psA[:, A.buf(use), 0:(q + 1) * P], AX_X))
                dve.tensor_scalar(negmax[:, b:b + 1], rowmax[:, b:b + 1], q_root[:, h % 2, 0, q:q + 1], None, ALU.mult)\
                    .then_inc(nmax.sem, 1)

            dve.memset(ypad[:, :, 0:PAD], 0.0).then_inc(dve_step.sem, 1)
            dve.memset(KR[NOPE], 0.0).then_inc(dve_step.sem, 1)
            dve.memset(rowmax[:], 0.0).then_inc(x_ready.sem, KT)
            dve.memset(SQSUM, 0.0).then_inc(dve_step.sem, 1)
            dve.wait_ge(dve_step.sem, 3)
            for j in range(KT):
                if j:
                    dve.wait_ge(sq_added.sem, j)
                dve.wait_ge(sq_done.sem, j + 1)
                dve.tensor_tensor(SQSUM, SQSUM, wk[:, j % 2], ALU.add).then_inc(sq_added.sem, 1)
            dve.wait_ge(params_in, 64)
            with dve.Fori(0, DEPTH) as L:
                dve_step.layer(L)
                step(dve.tensor_copy(cur[:], par[:, bass.ds(L, 1), :].rearrange("p a c -> p (a c)")))
                dve.wait_ge(*rstd.upto(L, 1))
                dve.wait_ge(*x_saved.upto(L, 16))
                for j in range(KT + 1):
                    if j < KT:
                        scale_by(X[:, j], C2.norm + j, wk[:, 2]).then_inc(h_scaled.sem, 1)
                    if j:
                        dve.wait_ge(*h_hi.upto(L, j))
                        split_low(Hlo[:, j - 1], X[:, j - 1], Hhi[:, j - 1]).then_inc(h_lo.sem, 1)
                for t in (0, 1):
                    dve.wait_ge(*A.filled(L, ("a", t)))
                    dve.wait_ge(*A.drained(L, ("g", t)))
                    dve.tensor_tensor(ypad[:, t, PAD:], psA[:, A.buf(("a", t))], YC[:, t], ALU.mult)\
                        .then_inc(A.freed(("a", t)), 1)
                for t in (0, 1):
                    dve.wait_ge(*A.drained(L, ("a", t)))
                    step(dve.tensor_scalar(YC[:, t], ypad[:, t, 0:SEQ], col(C2.conv_w + t), col(C2.conv_b + t),
                                           ALU.mult, ALU.add))
                    for k in range(1, CONV_K):
                        ins = dve.scalar_tensor_tensor(out=YC[:, t], in0=ypad[:, t, k:k + SEQ],
                                                       scalar=col(C2.conv_w + 2 * k + t), in1=YC[:, t],
                                                       op0=ALU.mult, op1=ALU.add)
                        if k < CONV_K - 1:
                            step(ins)
                        else:
                            ins.then_inc(conv_done.sem, 1)
                for t in (0, 1):
                    dve.wait_ge(*A.drained(L, ("zs", t)))
                    dve.tensor_tensor(UZ[:, t], UZ[:, t], ZS[t], ALU.mult).then_inc(uz_done.sem, 1)
                centre(L, "cmean", YC)
                centre(L, "smean", VG)
                dve.wait_ge(*roots.upto(L, 1))
                for t in (0, 1):
                    scale_by(YC[:, t], C2.cln_g + t, ROOT).then_inc(normed.sem, 1)
                dve.wait_ge(*roots.upto(L, 2))
                for t in (0, 1):
                    scale_by(VG[:, t], C2.sln_g + t, ROOT).then_inc(normed.sem, 1)
                add_latent(L, 1)
                for m in (0, 1):
                    dve.wait_ge(*A.filled(L, ("pw", m)))
                    dve.scalar_tensor_tensor(out=ZC[:, m], in0=psA[:, A.buf(("pw", m))], scalar=col(C2.pwb + m),
                                             in1=ZC[:, m], op0=ALU.add, op1=ALU.mult).then_inc(A.freed(("pw", m)), 1)
                add_latent(L, 2)
                dve.wait_ge(*T.filled(L, "wgt"))
                dve.tensor_tensor(WG.rearrange("p (g t) -> p g t", g=4),
                                  psT[:, T.buf("wgt"), 0:4 * P].rearrange("p (g t) -> p g t", g=4),
                                  causal[:].unsqueeze(1).broadcast_to([P, 4, P]), ALU.mult)\
                    .then_inc(T.freed("wgt"), 1)
                add_latent(L, 3)
                for t in (0, 1):
                    dve.wait_ge(*A.filled(L, ("sg", t)))
                    dve.tensor_tensor(by_chunk(X[:, 6 + t]), by_chunk(psA[:, A.buf(("sg", t))]),
                                      every_chunk(sgb[:, t]), ALU.add).then_inc(A.freed(("sg", t)), 1)
                    dve.wait_ge(*A.drained(L, ("sg", t)))
                    dve.tensor_tensor(UZ[:, t], X[:, 6 + t], UZ[:, t], ALU.mult).then_inc(s_out.sem, 1)
                add_latent(L, 4)
                add_latent(L, 5)
                dve.wait_ge(*l_rs.upto(L, 1))
                for j in range(Q_LORA_T):
                    scale_by(X[:, j], C2.qn + j, LROOT[0]).then_inc(l_scaled.sem, 1)
                add_latent(L, 7)
                dve.wait_ge(*kr_sq.upto(L, 1))
                dve.tensor_scalar(KR[ROPE], KR[ROPE], cur[ROPE, C2.kg:C2.kg + 1], None, ALU.mult)\
                    .then_inc(kr_g.sem, 1)
                dve.wait_ge(*l_rs.upto(L, 2))
                for j in range(Q_LORA_T, KT):
                    scale_by(X[:, j], C2.kvn - Q_LORA_T + j, LROOT[1]).then_inc(l_scaled.sem, 1)
                rotate_key(L)
                for j in range(KT):
                    dve.wait_ge(*l_hi.upto(L, j + 1))
                    split_low(Hlo[:, j], X[:, j], Hhi[:, j]).then_inc(l_lo.sem, 1)
                dve.wait_ge(*l_lo.upto(L, KT))
                dve.wait_ge(*roots.upto(L, 4))
                dve.wait_ge(*kr_rot.upto(L, 1))
                for m in (0, 1):
                    scale_by(X[:, m], C2.bn + m, ROOT_C, src=ZC[:, m]).then_inc(c_fin.sem, 1)
                for t in (0, 1):
                    scale_by(X[:, 6 + t], C2.bn + 6 + t, ROOT_S, src=UZ[:, t]).then_inc(s_fin.sem, 1)
                attention(L)
                for i, j in enumerate(Y_ORDER[:4]):
                    dve.wait_ge(*y_hi.upto(L, i + 1))
                    split_low(Hlo[:, j], X[:, j], Hhi[:, j]).then_inc(y_lo.sem, 1)
                dve.wait_ge(*m_rs.upto(L, 1))
                for t in range(4):
                    scale_by(X[:, 2 + t], C2.bn + 2 + t, MSUM, src=ZM[:, t]).then_inc(m_fin.sem, 1)
                dve.wait_ge(*m_fin.upto(L, 4))
                for j in Y_ORDER[4:]:
                    dve.wait_ge(*y_hi.upto(L, j + 3))
                    split_low(Hlo[:, j], X[:, j], Hhi[:, j]).then_inc(y_lo.sem, 1)
                dve.memset(SQSUM, 0.0)
                with dve.Fori(0, KT // 2) as jj:
                    for b in (0, 1):
                        dve.wait_ge(*out_filled.upto(L, jj * 2 + b + 1))
                        dve.wait_ge(*x_back[b].upto(L, jj * 16 + 16))
                        dve.tensor_tensor(tile_of(X, jj * 2 + b), psA[:, b], wk[:, 4 + b], ALU.add)\
                            .then_inc(x_ready.sem, 1)
                        dve.wait_ge(*sq_done.upto(L + 1, jj * 2 + b + 1))
                        dve.tensor_tensor(SQSUM, SQSUM, wk[:, b], ALU.add).then_inc(sq_added.sem, 1)
            counts["d2"] = dve_step.k
            for t in range(NT):
                dve.wait_ge(turned, t + 1)
                if t >= 4:
                    dve.wait_ge(written[t % 4], 16 * (t // 4))
                dve.tensor_copy(OUT[t % 4], psA[:, t % 2]).then_inc(copied, 1)


def _tiles(v, n):
    return np.ascontiguousarray(v.reshape(n, P).T)


def _panel(w, nk):
    m = w.shape[1]
    return w.reshape(nk, P, m).transpose(1, 0, 2).reshape(P, nk * m)


def _pack1(w_in, w_branch, w_out):
    starts = dict(zip(("aq", "ak", "av", "az", "cx", "cb", "cc", "cz", "rq", "rk", "rv", "rz", "gate"),
                      np.cumsum([0, 512, 512, 512, 512, 512, 512, 512, 512, 256, 256, 512, 512]).tolist()))
    out = []
    for name, nk, m in P1:
        if name[0] == "branch":
            w = w_branch[name[1]][:, name[2] * P:(name[2] + 1) * P]
        elif name[0] == "out":
            w = w_out[:, name[1] * P:(name[1] + 1) * P]
        else:
            c = starts[name[0]] + (name[1] * D_MODEL + name[2] * P if name[0] == "gate" else name[1] * P)
            w = w_in[:, c:c + P]
        out.append(_panel(w, nk))
    return np.concatenate(out, axis=1)


def _pack2(w_in, w_uq, w_ukv, w_out):
    starts = dict(zip(("a", "g", "zc", "cq", "ckv", "kr", "zm", "u", "v", "zs"),
                      np.cumsum([0, 256, 256, 256, 768, 256, 32, 512, 256, 256]).tolist()))
    out = []
    for name, nk, m in P2:
        i = name[1]
        if name[0] == "q":
            w = w_uq[:, i * M_QK:(i + 1) * M_QK]
        elif name[0] == "kv":
            w = w_ukv[:, i * P:(i + 1) * P]
        elif name[0] == "out":
            w = w_out[:, i * P:(i + 1) * P]
        elif name[0] == "kr":
            c = starts["kr"]
            w = w_in[i * 512:(i + 1) * 512, c - M_NOPE:c + M_ROPE]
        else:
            c = starts[name[0]] + i * P
            w = w_in[:, c:c + P]
        out.append(_panel(w, nk))
    return np.concatenate(out, axis=1)


def _tables():
    f = np.float32
    t = np.zeros((P, K.n), f)
    idx = np.arange(P)
    t[:, K.ident:K.ident + P] = np.eye(P)
    t[:, K.ones:K.ones + P] = 1
    t[:, K.mask:K.mask + P] = np.where(idx[None, :] <= idx[:, None], 0.0, NEG)
    for col, size, half in ((K.swapa, 64, 8), (K.swapr, 64, 32)):
        for m in range(P):
            r = m % size
            if r < 2 * half:
                t[m - r + (r + half) % (2 * half), col + m] = 1
    for r in range(M_ROPE):
        t[M_NOPE + (r + 16) % 32, K.swapm + r] = 1
    t[:, K.causal:K.causal + P] = idx[:, None] <= idx[None, :]
    log_g = np.log(f(1.0) - f(2.0) ** (f(-5.0) - np.arange(HEADS, dtype=f))).astype(f)
    diff = (idx[None, :] - idx[:, None]).astype(f)
    scale = f(A_QK ** -0.5)
    pos = idx.astype(f)
    for h in range(HEADS):
        t[:, K.dmask + h * P:K.dmask + (h + 1) * P] = np.where(diff >= 0, np.exp(np.maximum(diff, 0) * log_g[h]), 0) * scale
        rows, pr = slice((h % 2) * 64, (h % 2 + 1) * 64), h // 2
        t[rows, K.xi + pr * P:K.xi + (pr + 1) * P] = np.exp((pos + 1) * log_g[h])[None]
        t[rows, K.zeta + pr * P:K.zeta + (pr + 1) * P] = (np.exp((R_CHUNK - 1 - pos) * log_g[h]) * scale)[None]
        t[rows, K.decay + pr] = np.exp(f(R_CHUNK) * log_g[h])
    pos = np.arange(SEQ, dtype=f)
    ropes = np.zeros((3, P, 2, SEQ), f)
    ropes[:, :, 0] = 1
    inv_a = f(500000.0) ** (-np.arange(0, 16, 2, dtype=f) / f(16))
    inv_r = f(1.0) / (f(10000.0) ** np.linspace(0.0, 1.0, 32, dtype=f))
    inv_m = f(10000.0) ** (-np.arange(16, dtype=f) / f(16))
    for n, inv, half, size, base in ((0, inv_a, 8, 64, 0), (1, inv_r, 32, 64, 0), (2, inv_m, 16, 128, 64)):
        ang = (pos[None, :] * inv[:, None].astype(f)).astype(f)
        for m in range(P):
            r = (m - base) % size
            if m >= base and r < 2 * half:
                ropes[n, m, 0] = np.cos(ang[r % half])
                ropes[n, m, 1] = np.sin(ang[r % half]) * (-1 if r < half else 1)
    return t, ropes


def _params1(norm_g, attn_subln_g, conv_w):
    out = np.zeros((DEPTH, P, C1.n), np.float32)
    for l in range(DEPTH):
        out[l, :, C1.norm:C1.norm + KT] = _tiles(norm_g[l], KT)
        out[l, :, C1.subln] = attn_subln_g[l]
        for k in range(3):
            out[l, :, C1.conv + 4 * k:C1.conv + 4 * k + 4] = _tiles(conv_w[l, k], 4)
        lam_init = 0.8 - 0.6 * np.exp(-0.3 * l)
        out[l, :, C1.lam_init] = lam_init
        out[l, :, C1.lam_rest] = 1.0 - lam_init
    return out


def _params2(norm_g, conv_w, conv_b, cln_g, cln_b, pwb, qn, kvn, qg, kg, sln_g, sln_b, bn):
    out = np.zeros((DEPTH, P, C2.n), np.float32)
    for l in range(DEPTH):
        o = out[l]
        o[:, C2.norm:C2.norm + 8] = _tiles(norm_g[l], 8)
        for k in range(CONV_K):
            o[:, C2.conv_w + 2 * k:C2.conv_w + 2 * k + 2] = _tiles(conv_w[l, k], 2)
        for col, v in ((C2.conv_b, conv_b), (C2.cln_g, cln_g), (C2.cln_b, cln_b), (C2.pwb, pwb),
                       (C2.sln_g, sln_g), (C2.sln_b, sln_b)):
            o[:, col:col + 2] = _tiles(v[l], 2)
        o[:, C2.qn:C2.qn + 6] = _tiles(qn[l], 6)
        o[:, C2.kvn:C2.kvn + 2] = _tiles(kvn[l], 2)
        o[:M_QK, C2.qg] = qg[l]
        o[:M_QK, C2.kg] = kg[l]
        o[:, C2.bn:C2.bn + 8] = _tiles(bn[l], 8)
    return out


def kernel(x, norm_g, w_in, attn_lambda, attn_subln_g, conv_w, w_branch, w_out, final_norm_g, norm_g_2,
           w_in_2, conv_w_2, conv_b_2, conv_ln_g_2, conv_ln_b_2, conv_pw_w_2, conv_pw_b_2, q_norm_g_2,
           w_uq_2, kv_norm_g_2, w_ukv_2, qk_q_g_2, qk_k_g_2, sg_ln_g_2, sg_ln_b_2, sg_w_2, sg_b_2,
           branch_norm_g_2, w_out_2):
    import concourse.bacc as bacc
    from concourse.bass_utils import run_bass_kernel_spmd

    def n(a):
        return np.asarray(a)

    consts, ropes = _tables()
    arrays = {
        "x": n(x)[0],
        "w1": np.stack([_pack1(n(w_in)[l], n(w_branch)[l], n(w_out)[l]) for l in range(DEPTH)]),
        "par1": _params1(n(norm_g), n(attn_subln_g), n(conv_w)),
        "lamv": n(attn_lambda).reshape(DEPTH, 4 * A_QK),
        "finalg": _tiles(n(final_norm_g), KT),
        "w2": np.stack([_pack2(n(w_in_2)[l], n(w_uq_2)[l], n(w_ukv_2)[l], n(w_out_2)[l]) for l in range(DEPTH)]),
        "par2": _params2(n(norm_g_2), n(conv_w_2), n(conv_b_2), n(conv_ln_g_2), n(conv_ln_b_2), n(conv_pw_b_2),
                         n(q_norm_g_2), n(kv_norm_g_2), n(qk_q_g_2), n(qk_k_g_2), n(sg_ln_g_2), n(sg_ln_b_2),
                         n(branch_norm_g_2)),
        "pww": np.stack([_panel(n(conv_pw_w_2)[l], 2) for l in range(DEPTH)]),
        "sgw": np.ascontiguousarray(n(sg_w_2).transpose(0, 2, 1, 3)),
        "sgb": n(sg_b_2),
        "consts": consts,
        "ropes": ropes,
    }
    arrays = {f"in_{k}": np.ascontiguousarray(v) for k, v in arrays.items()}

    def program(per1, per2):
        nc = bacc.Bacc("TRN2", target_bir_lowering=False, num_devices=1)
        args = {k[3:]: nc.dram_tensor(k, v.shape, F32, kind="ExternalInput").ap() for k, v in arrays.items()}
        out = nc.dram_tensor("out", (SEQ, D_MODEL), F32, kind="ExternalOutput").ap()
        xs = nc.dram_tensor("xs", (KT, P, SEQ), F32, kind="Internal").ap()
        return nc, build(nc, per1, per2, out=out, xs=xs, **args)

    _, counted = program({}, {})
    nc, _ = program(counted, counted)
    r = run_bass_kernel_spmd(nc, [arrays], core_ids=[0])
    return r.results[0]["out"].reshape(1, SEQ, D_MODEL)
```
